# Optimizing a Trainium2 kernel written in Bass

```python
import jax, jax.numpy as jnp
from jax import lax
import numpy as np

D_MODEL = 1024
BATCH = 1
SEQ = 256
DEPTH = 1

CHUNK = 64
P_DIM = 256
SB_HEAD_DIM = 64
SB_WIDTH = 3 * D_MODEL // 8
SB_HEADS = SB_WIDTH // SB_HEAD_DIM
SB_QBLOCK = 128
ML_HEADS = 4
ML_WIDTH = 3 * D_MODEL // 8
ML_HEAD_DIM = ML_WIDTH // ML_HEADS
CONV_K = 4
SGU_WIDTH = D_MODEL - SB_WIDTH - ML_WIDTH
SGU_GROUPS = 4
SGU_GROUP_DIM = SGU_WIDTH // SGU_GROUPS
SGU_BLOCK = 128
IN_SPLITS = (SB_WIDTH, SB_WIDTH, SB_WIDTH, ML_WIDTH, ML_WIDTH, ML_WIDTH, ML_WIDTH, ML_HEADS, ML_HEADS, SGU_WIDTH, SGU_WIDTH)
N_IN = 3 * SB_WIDTH + 4 * ML_WIDTH + 2 * ML_HEADS + 2 * SGU_WIDTH
N_GROUPS = 4
EXPERTS_PER_GROUP = 8
N_EXPERTS = N_GROUPS * EXPERTS_PER_GROUP
TOP_K = 2
D_EXPERT = D_MODEL // 4
MOE_BLOCK = 512
EPS = 1e-6


F32 = jnp.float32

def rms_norm(x, g):
    x32 = x.astype(F32)
    return x32 * lax.rsqrt(jnp.mean(x32 * x32, axis=-1, keepdims=True) + EPS) * g.astype(F32)

def split_cols(z, sizes):
    idx = np.cumsum(sizes)[:-1].tolist()
    return jnp.split(z, idx, axis=-1)

def causal_depthwise_conv(x, w, b):
    y = lax.conv_general_dilated(x.astype(F32), w.astype(F32)[:, None, :], window_strides=(1,),
                                 padding=[(CONV_K - 1, 0)], dimension_numbers=('NWC', 'WIO', 'NWC'),
                                 feature_group_count=x.shape[-1])
    return y + b.astype(F32)

def stick_breaking_attention(q, k, v):
    S = q.shape[1]
    scale = q.shape[-1] ** -0.5
    outs = []
    for n in range(S // SB_QBLOCK):
        t0 = n * SB_QBLOCK
        kend = t0 + SB_QBLOCK
        z = jnp.einsum('bthd,bshd->bhts', q[:, t0:kend], k[:, :kend]) * scale
        tpos = t0 + jnp.arange(SB_QBLOCK)
        spos = jnp.arange(kend)
        mask = spos[None, :] < tpos[:, None]
        log_1m = jnp.where(mask, -jax.nn.softplus(z), 0.0)
        after = lax.cumsum(log_1m, axis=3, reverse=True) - log_1m
        a = jnp.where(mask, jnp.exp(jax.nn.log_sigmoid(z) + after), 0.0)
        outs.append(jnp.einsum('bhts,bshd->bthd', a, v[:, :kend]))
    return jnp.concatenate(outs, axis=1)

def mlstm_chunkwise(q, k, v, i_pre, f_pre):
    Bn, S, H, d = q.shape
    N, L = S // CHUNK, CHUNK
    q = q.reshape(Bn, N, L, H, d)
    k = k.reshape(Bn, N, L, H, d) * (d ** -0.5)
    v = v.reshape(Bn, N, L, H, d)
    ig = i_pre.reshape(Bn, N, L, H)
    bcum = jnp.cumsum(jax.nn.log_sigmoid(f_pre.reshape(Bn, N, L, H)), axis=2)
    btot = bcum[:, :, -1]
    a = btot[:, :, None] - bcum + ig

    def step(carry, xs):
        c, nvec, m = carry
        k_c, v_c, a_c, bt_c = xs
        m_new = jnp.maximum(bt_c + m, a_c.max(axis=1))
        decay = jnp.exp(bt_c + m - m_new)
        w = jnp.exp(a_c - m_new[:, None])
        c_new = decay[..., None, None] * c + jnp.einsum('blh,blhd,blhe->bhde', w, k_c, v_c)
        n_new = decay[..., None] * nvec + jnp.einsum('blh,blhd->bhd', w, k_c)
        return (c_new, n_new, m_new), (c, nvec, m)

    init = (jnp.zeros((Bn, H, d, d), F32), jnp.zeros((Bn, H, d), F32), jnp.zeros((Bn, H), F32))
    xs = (jnp.moveaxis(k, 1, 0), jnp.moveaxis(v, 1, 0), jnp.moveaxis(a, 1, 0), jnp.moveaxis(btot, 1, 0))
    _, (c_in, n_in, m_in) = lax.scan(step, init, xs)
    c_in = jnp.moveaxis(c_in, 0, 1)
    n_in = jnp.moveaxis(n_in, 0, 1)
    m_in = jnp.moveaxis(m_in, 0, 1)

    bT = jnp.moveaxis(bcum, 2, -1)
    igT = jnp.moveaxis(ig, 2, -1)
    causal = jnp.tril(jnp.ones((L, L), dtype=bool))
    dmat = jnp.where(causal, bT[..., :, None] - bT[..., None, :] + igT[..., None, :], -jnp.inf)
    m_inter = bT + m_in[..., None]
    m_t = jnp.maximum(m_inter, dmat.max(axis=-1))
    wd = jnp.where(causal, jnp.exp(dmat - m_t[..., None]), 0.0)
    s = jnp.einsum('bnthd,bnshd->bnhts', q, k) * wd
    inter = jnp.exp(m_inter - m_t)
    num = jnp.einsum('bnhts,bnshd->bnthd', s, v) + jnp.einsum('bnhl,bnlhd,bnhde->bnlhe', inter, q, c_in)
    den = s.sum(axis=-1) + inter * jnp.einsum('bnlhd,bnhd->bnhl', q, n_in)
    den = jnp.maximum(jnp.abs(den), jnp.exp(-m_t))
    h = num / jnp.moveaxis(den, 2, -1)[..., None]
    return h.reshape(Bn, S, H, d)

def spatial_gating(u, v, ln_g, ln_b, w_s, b_s):
    Bn, S, _ = u.shape
    v = v.reshape(Bn, S, SGU_GROUPS, SGU_GROUP_DIM)
    mu = v.mean(axis=-1, keepdims=True)
    var = jnp.mean(jnp.square(v - mu), axis=-1, keepdims=True)
    v = (v - mu) * lax.rsqrt(var + EPS) * ln_g.reshape(SGU_GROUPS, SGU_GROUP_DIM) + ln_b.reshape(SGU_GROUPS, SGU_GROUP_DIM)
    v = v.reshape(Bn, S // SGU_BLOCK, SGU_BLOCK, SGU_GROUPS, SGU_GROUP_DIM)
    cpos = jnp.arange(SGU_BLOCK) // CHUNK
    mask = cpos[None, :] <= cpos[:, None]
    w = jnp.where(mask[None], w_s.astype(F32), 0.0)
    mixed = jnp.einsum('gts,bnsgc->bntgc', w, v) + b_s.astype(F32).T[:, :, None]
    return u * mixed.reshape(Bn, S, SGU_WIDTH)

def routed_experts(xt, e_idx, e_w, w_gate, w_up, w_down):
    T, D = xt.shape
    M = T * TOP_K
    flat_e = e_idx.reshape(M)
    order = jnp.argsort(flat_e)
    sorted_e = flat_e[order]
    sorted_tok = order // TOP_K
    sorted_w = e_w.reshape(M)[order]
    sizes = jnp.bincount(flat_e, length=N_EXPERTS)
    padded = (sizes + MOE_BLOCK - 1) // MOE_BLOCK * MOE_BLOCK
    start = jnp.cumsum(sizes) - sizes
    pend = jnp.cumsum(padded)
    pstart = pend - padded
    dest = pstart[sorted_e] + jnp.arange(M) - start[sorted_e]
    n_blocks = -(-(M + N_EXPERTS * (MOE_BLOCK - 1)) // MOE_BLOCK)
    rows = n_blocks * MOE_BLOCK
    row_tok = jnp.zeros((rows,), jnp.int32).at[dest].set(sorted_tok.astype(jnp.int32))
    row_w = jnp.zeros((rows,), F32).at[dest].set(sorted_w)
    block_e = jnp.minimum(jnp.searchsorted(pend, jnp.arange(n_blocks) * MOE_BLOCK, side='right'), N_EXPERTS - 1)

    def block_ffn(args):
        tok, wt, e = args
        xb = xt[tok]
        hb = jax.nn.silu(xb @ w_gate[e]) * (xb @ w_up[e])
        return (hb @ w_down[e]).astype(F32) * wt[:, None]

    yb = lax.map(block_ffn, (row_tok.reshape(n_blocks, MOE_BLOCK), row_w.reshape(n_blocks, MOE_BLOCK), block_e))
    return jnp.zeros((T, D), F32).at[row_tok].add(yb.reshape(rows, D))

def hierarchical_moe(h, rg_w, rg_b, re_w, re_b, w_gate, w_up, w_down):
    Bn, S, D = h.shape
    xt = h.reshape(Bn * S, D)
    g_logits = (xt @ rg_w + rg_b).astype(F32)
    g_prob = jax.nn.softmax(g_logits, axis=-1)
    g_top = jnp.argmax(g_logits, axis=-1)
    g_w = jnp.take_along_axis(g_prob, g_top[:, None], axis=-1)[:, 0]
    e_logits = (xt @ re_w + re_b).astype(F32).reshape(-1, N_GROUPS, EXPERTS_PER_GROUP)
    e_in = jnp.take_along_axis(e_logits, g_top[:, None, None], axis=1)[:, 0]
    e_val, e_loc = lax.top_k(e_in, TOP_K)
    e_w = jax.nn.softmax(e_val, axis=-1) * g_w[:, None]
    e_idx = g_top[:, None].astype(jnp.int32) * EXPERTS_PER_GROUP + e_loc.astype(jnp.int32)
    y = routed_experts(xt, e_idx, e_w, w_gate, w_up, w_down)
    return y.reshape(Bn, S, D)

def first_inputs(seed: int = 0) -> dict:
    key = jax.random.key(seed)
    ks = jax.random.split(key, 32)

    def nrm(k, shape, scale):
        return jax.random.normal(k, shape, F32) * scale

    def gain(k, shape):
        return 1.0 + 0.05 * jax.random.normal(k, shape, F32)

    D = D_MODEL
    return {
        "x": nrm(ks[0], (BATCH, SEQ, D), 1.0),
        "p": nrm(ks[1], (DEPTH, BATCH, SEQ, P_DIM), 1.0),
        "norm1_g": gain(ks[2], (DEPTH, D)),
        "w_in": nrm(ks[3], (DEPTH, D, N_IN), D ** -0.5),
        "conv_w": nrm(ks[4], (DEPTH, CONV_K, 2 * ML_WIDTH), CONV_K ** -0.5),
        "conv_b": nrm(ks[5], (DEPTH, 2 * ML_WIDTH), 0.01),
        "igate_b": nrm(ks[6], (DEPTH, ML_HEADS), 0.1),
        "fgate_b": jnp.linspace(3.0, 6.0, ML_HEADS, dtype=F32)[None, :] + nrm(ks[7], (DEPTH, ML_HEADS), 0.1),
        "mnorm_g": gain(ks[8], (DEPTH, ML_WIDTH)),
        "sb_out_g": gain(ks[9], (DEPTH, SB_WIDTH)),
        "sgu_ln_g": gain(ks[10], (DEPTH, SGU_WIDTH)),
        "sgu_ln_b": nrm(ks[11], (DEPTH, SGU_WIDTH), 0.01),
        "sgu_w": nrm(ks[12], (DEPTH, SGU_GROUPS, SGU_BLOCK, SGU_BLOCK), SGU_BLOCK ** -0.5),
        "sgu_b": gain(ks[13], (DEPTH, SGU_GROUPS, SGU_BLOCK)),
        "sgu_out_g": gain(ks[14], (DEPTH, SGU_WIDTH)),
        "w_out": nrm(ks[15], (DEPTH, D, D), D ** -0.5),
        "norm2_g": gain(ks[16], (DEPTH, D)),
        "router_gw": nrm(ks[17], (DEPTH, D, N_GROUPS), D ** -0.5),
        "router_gb": nrm(ks[18], (DEPTH, N_GROUPS), 0.01),
        "router_ew": nrm(ks[19], (DEPTH, D, N_EXPERTS), D ** -0.5),
        "router_eb": nrm(ks[20], (DEPTH, N_EXPERTS), 0.01),
        "w_gate": nrm(ks[21], (DEPTH, N_EXPERTS, D, D_EXPERT), D ** -0.5),
        "w_up": nrm(ks[22], (DEPTH, N_EXPERTS, D, D_EXPERT), D ** -0.5),
        "w_down": nrm(ks[23], (DEPTH, N_EXPERTS, D_EXPERT, D), D_EXPERT ** -0.5),
        "ple_norm_g": gain(ks[24], (DEPTH, D)),
        "ple_gate_w": nrm(ks[25], (DEPTH, D, D), D ** -0.5),
        "ple_proj_w": nrm(ks[26], (DEPTH, P_DIM, D), P_DIM ** -0.5),
        "final_g": gain(ks[27], (D,)),
    }

def first_block(x, p, norm1_g, w_in, conv_w, conv_b, igate_b, fgate_b, mnorm_g, sb_out_g,
              sgu_ln_g, sgu_ln_b, sgu_w, sgu_b, sgu_out_g, w_out, norm2_g,
              router_gw, router_gb, router_ew, router_eb, w_gate, w_up, w_down,
              ple_norm_g, ple_gate_w, ple_proj_w, final_g):
    Bn, S, D = x.shape
    h = x.astype(F32)
    for i in range(DEPTH):
        hn = rms_norm(h, norm1_g[i])
        z = hn @ w_in[i]
        qa, ka, va, qb, kb, vb, ob, ib, fb, uc, vc = split_cols(z, IN_SPLITS)
        ya = stick_breaking_attention(qa.reshape(Bn, S, SB_HEADS, SB_HEAD_DIM),
                                      ka.reshape(Bn, S, SB_HEADS, SB_HEAD_DIM),
                                      va.reshape(Bn, S, SB_HEADS, SB_HEAD_DIM)).reshape(Bn, S, SB_WIDTH)
        ya = rms_norm(ya, sb_out_g[i])
        qk = jax.nn.silu(causal_depthwise_conv(jnp.concatenate([qb, kb], axis=-1), conv_w[i], conv_b[i]))
        qb, kb = jnp.split(qk, 2, axis=-1)
        hb = mlstm_chunkwise(qb.reshape(Bn, S, ML_HEADS, ML_HEAD_DIM),
                             kb.reshape(Bn, S, ML_HEADS, ML_HEAD_DIM),
                             vb.astype(F32).reshape(Bn, S, ML_HEADS, ML_HEAD_DIM),
                             ib + igate_b[i], fb + fgate_b[i])
        hb = rms_norm(hb, mnorm_g[i].reshape(ML_HEADS, ML_HEAD_DIM)).reshape(Bn, S, ML_WIDTH)
        yb = hb * jax.nn.sigmoid(ob)
        yc = spatial_gating(jax.nn.gelu(uc), jax.nn.gelu(vc), sgu_ln_g[i], sgu_ln_b[i], sgu_w[i], sgu_b[i])
        yc = rms_norm(yc, sgu_out_g[i])
        h = h + jnp.concatenate([ya, yb, yc], axis=-1) @ w_out[i]
        h = h + hierarchical_moe(rms_norm(h, norm2_g[i]), router_gw[i], router_gb[i], router_ew[i], router_eb[i],
                                 w_gate[i], w_up[i], w_down[i])
        gate = jax.nn.sigmoid(rms_norm(h, ple_norm_g[i]) @ ple_gate_w[i])
        h = h + gate * (p[i] @ ple_proj_w[i]).astype(F32)
    return rms_norm(h, final_g).astype(x.dtype)


DEPTH_2 = 2

N_MIXERS = 2
N_HEADS = 16
HEAD_DIM = D_MODEL // N_HEADS
MOBA_BLOCK = 256
MOBA_TOPK = 3
Q_CHUNK = 32
ROPE_THETA = 10000.0
CONV_WIDTH = 3
D_FF = 2816
RMS_EPS = 1e-6
NEG_INF = -1e30
N_CONV_LAYERS = (DEPTH_2 + 1) // 2
N_ATTN_LAYERS = DEPTH_2 // 2


def rmsnorm(x, g):
    xf = x.astype(jnp.float32)
    var = jnp.mean(xf * xf, axis=-1, keepdims=True)
    return (xf * lax.rsqrt(var + RMS_EPS)).astype(x.dtype) * g

def causal_dwconv(x, w):
    S = x.shape[1]
    xp = jnp.pad(x, ((0, 0), (CONV_WIDTH - 1, 0), (0, 0)))
    y = xp[:, 0:S] * w[0]
    for j in range(1, CONV_WIDTH):
        y = y + xp[:, j:j + S] * w[j]
    return y

def short_conv_mixer(h, w_in, w_conv, w_out):
    bcv = h @ w_in
    b, c, v = jnp.split(bcv, 3, axis=-1)
    return (b * causal_dwconv(c * v, w_conv)) @ w_out

def rope(x, pos):
    half = HEAD_DIM // 2
    inv = ROPE_THETA ** (-jnp.arange(half, dtype=jnp.float32) / half)
    ang = pos.astype(jnp.float32)[:, None] * inv[None, :]
    cos = jnp.cos(ang).astype(x.dtype)
    sin = jnp.sin(ang).astype(x.dtype)
    x1, x2 = x[..., :half], x[..., half:]
    return jnp.concatenate([x1 * cos - x2 * sin, x2 * cos + x1 * sin], axis=-1)

def moba_attention(h, w_qkv, w_o):
    Bsz, S, _ = h.shape
    qkv = (h @ w_qkv).reshape(Bsz, S, 3, N_HEADS, HEAD_DIM)
    q = jnp.transpose(qkv[:, :, 0], (0, 2, 1, 3))
    k = jnp.transpose(qkv[:, :, 1], (0, 2, 1, 3))
    v = jnp.transpose(qkv[:, :, 2], (0, 2, 1, 3))
    pos = jnp.arange(S, dtype=jnp.int32)
    q = rope(q, pos) * (HEAD_DIM ** -0.5)
    k = rope(k, pos)

    n_blocks = -(-S // MOBA_BLOCK)
    pad = n_blocks * MOBA_BLOCK - S
    k = jnp.pad(k, ((0, 0), (0, 0), (0, pad), (0, 0)))
    v = jnp.pad(v, ((0, 0), (0, 0), (0, pad), (0, 0)))
    k_blocks = k.reshape(Bsz, N_HEADS, n_blocks, MOBA_BLOCK, HEAD_DIM)
    v_blocks = v.reshape(Bsz, N_HEADS, n_blocks, MOBA_BLOCK, HEAD_DIM)
    k_mean = jnp.mean(k_blocks.astype(jnp.float32), axis=3).astype(k.dtype)

    topk = min(MOBA_TOPK, n_blocks)
    b_idx = jnp.arange(Bsz)[:, None, None, None]
    h_idx = jnp.arange(N_HEADS)[None, :, None, None]
    block_ids = jnp.arange(n_blocks)
    key_off = jnp.arange(MOBA_BLOCK)
    q_off = jnp.arange(Q_CHUNK)

    def chunk(c):
        q0 = c * Q_CHUNK
        qc = lax.dynamic_slice_in_dim(q, q0, Q_CHUNK, axis=2)
        qpos = q0 + q_off
        own = q0 // MOBA_BLOCK
        gate = jnp.einsum('bhqd,bhnd->bhqn', qc, k_mean).astype(jnp.float32)
        gate = jnp.where((block_ids < own)[None, None, None, :], gate, NEG_INF)
        _, top_i = lax.top_k(gate, topk)
        rank_valid = jnp.arange(topk) < jnp.minimum(own, MOBA_TOPK)
        kg = k_blocks[b_idx, h_idx, top_i]
        vg = v_blocks[b_idx, h_idx, top_i]
        s_sel = jnp.einsum('bhqd,bhqnjd->bhqnj', qc, kg).astype(jnp.float32)
        s_sel = jnp.where(rank_valid[:, None], s_sel, NEG_INF)
        s_sel = s_sel.reshape(Bsz, N_HEADS, Q_CHUNK, topk * MOBA_BLOCK)
        ko = lax.dynamic_slice_in_dim(k, own * MOBA_BLOCK, MOBA_BLOCK, axis=2)
        vo = lax.dynamic_slice_in_dim(v, own * MOBA_BLOCK, MOBA_BLOCK, axis=2)
        s_own = jnp.einsum('bhqd,bhjd->bhqj', qc, ko).astype(jnp.float32)
        kpos = own * MOBA_BLOCK + key_off
        s_own = jnp.where(kpos[None, :] <= qpos[:, None], s_own, NEG_INF)
        p = jax.nn.softmax(jnp.concatenate([s_sel, s_own], axis=-1), axis=-1).astype(v.dtype)
        p_sel = p[..., :topk * MOBA_BLOCK].reshape(Bsz, N_HEADS, Q_CHUNK, topk, MOBA_BLOCK)
        p_own = p[..., topk * MOBA_BLOCK:]
        return (jnp.einsum('bhqnj,bhqnjd->bhqd', p_sel, vg)
                + jnp.einsum('bhqj,bhjd->bhqd', p_own, vo))

    o = lax.map(chunk, jnp.arange(S // Q_CHUNK))
    o = jnp.transpose(o, (1, 0, 3, 2, 4)).reshape(Bsz, S, N_HEADS * HEAD_DIM)
    return o @ w_o

def conv_ffn(h, w_up, w_conv, w_down):
    gu = causal_dwconv(h @ w_up, w_conv)
    g, u = jnp.split(gu, 2, axis=-1)
    return (jax.nn.silu(g) * u) @ w_down

def second_inputs(seed: int = 0) -> dict:
    key = jax.random.key(seed)
    ks = jax.random.split(key, 16)
    D = D_MODEL
    f32 = jnp.float32

    def nrm(k, shape, scale):
        return jax.random.normal(k, shape, dtype=f32) * scale

    return {
        "x": nrm(ks[0], (BATCH, SEQ, D), 1.0),
        "mix_norm": 1.0 + nrm(ks[1], (DEPTH_2, D), 0.02),
        "sc_w_in": nrm(ks[2], (N_CONV_LAYERS, D, 3 * D), D ** -0.5),
        "sc_w_conv": nrm(ks[3], (N_CONV_LAYERS, CONV_WIDTH, D), CONV_WIDTH ** -0.5),
        "sc_w_out": nrm(ks[4], (N_CONV_LAYERS, D, D), D ** -0.5),
        "moba_w_qkv": nrm(ks[5], (N_ATTN_LAYERS, D, 3 * D), D ** -0.5),
        "moba_w_o": nrm(ks[6], (N_ATTN_LAYERS, D, D), D ** -0.5),
        "ffn_norm": 1.0 + nrm(ks[7], (DEPTH_2, D), 0.02),
        "ffn_w_up": nrm(ks[8], (DEPTH_2, D, 2 * D_FF), D ** -0.5),
        "ffn_w_conv": nrm(ks[9], (DEPTH_2, CONV_WIDTH, 2 * D_FF), CONV_WIDTH ** -0.5),
        "ffn_w_down": nrm(ks[10], (DEPTH_2, D_FF, D), D_FF ** -0.5),
        "final_norm": 1.0 + nrm(ks[11], (D,), 0.02),
    }

def second_block(x, mix_norm, sc_w_in, sc_w_conv, sc_w_out, moba_w_qkv, moba_w_o,
              ffn_norm, ffn_w_up, ffn_w_conv, ffn_w_down, final_norm):
    for i in range(DEPTH_2):
        h = rmsnorm(x, mix_norm[i])
        j = i // N_MIXERS
        if i % N_MIXERS == 0:
            x = x + short_conv_mixer(h, sc_w_in[j], sc_w_conv[j], sc_w_out[j])
        else:
            x = x + moba_attention(h, moba_w_qkv[j], moba_w_o[j])
        x = x + conv_ffn(rmsnorm(x, ffn_norm[i]), ffn_w_up[i], ffn_w_conv[i], ffn_w_down[i])
    return rmsnorm(x, final_norm)


def setup_inputs(seed=0):
    out = dict(first_inputs(seed))
    for name, value in second_inputs(seed + 1).items():
        if name != "x":
            out[name + "_2"] = value
    return out


def reference(
    x, p, norm1_g, w_in, conv_w, conv_b, igate_b, fgate_b, mnorm_g, sb_out_g, sgu_ln_g,
    sgu_ln_b, sgu_w, sgu_b, sgu_out_g, w_out, norm2_g, router_gw, router_gb, router_ew,
    router_eb, w_gate, w_up, w_down, ple_norm_g, ple_gate_w, ple_proj_w, final_g, mix_norm_2,
    sc_w_in_2, sc_w_conv_2, sc_w_out_2, moba_w_qkv_2, moba_w_o_2, ffn_norm_2, ffn_w_up_2,
    ffn_w_conv_2, ffn_w_down_2, final_norm_2,
):
    x = first_block(
        x, p, norm1_g, w_in, conv_w, conv_b, igate_b, fgate_b, mnorm_g, sb_out_g, sgu_ln_g,
        sgu_ln_b, sgu_w, sgu_b, sgu_out_g, w_out, norm2_g, router_gw, router_gb, router_ew,
        router_eb, w_gate, w_up, w_down, ple_norm_g, ple_gate_w, ple_proj_w, final_g,
    )
    return second_block(
        x, mix_norm_2, sc_w_in_2, sc_w_conv_2, sc_w_out_2, moba_w_qkv_2, moba_w_o_2, ffn_norm_2,
        ffn_w_up_2, ffn_w_conv_2, ffn_w_down_2, final_norm_2,
    )


_drawn_inputs = setup_inputs


def setup_inputs(seed=0):
    import zlib

    import numpy as np

    out = dict(_drawn_inputs(seed))
    spreads = {}
    factors = {'conv_b': 4.012,
     'igate_b': 44.603,
     'sgu_ln_b': 3.427,
     'router_gb': 3.015,
     'router_eb': 2.725,
     'ple_norm_g': 4.694,
     'ffn_norm_2': 3.533,
     'final_norm_2': 2.672}
    for name, (base, spread) in spreads.items():
        noise = np.random.default_rng([zlib.crc32(name.encode()), seed]).standard_normal(out[name].shape)
        drawn = base * np.exp(spread * noise) if base else spread * noise
        out[name] = __import__('jax').numpy.asarray(drawn.astype(out[name].dtype))
    for name, factor in factors.items():
        out[name] = (out[name] * factor).astype(out[name].dtype)
    return out
```

```python
from contextlib import ExitStack

import numpy as np

import concourse.bass as bass
from concourse import mybir

F32 = mybir.dt.float32
F32R = mybir.dt.float32r
ALU = mybir.AluOpType
ACT = mybir.ActivationFunctionType
AX = mybir.AxisListType

P = 128
D = 1024
T = 256
TT = T // P
KD = D // P
EPS = 1e-6
BIG = 1.0e30

SBW, SBH, SBD = 384, 6, 64
MLW, MLH, MLD = 384, 4, 96
SGW, SGG, SGD = 256, 4, 64
CONV_K = 4
NG, EPG, NE = 4, 8, 32
GATES = 8
N_IN = 3 * SBW + 4 * MLW + 2 * SGW + GATES
TAIL = N_IN - 6 * 512
Z_QB = 3 * SBW
Z_VB = Z_QB + 2 * MLW
Z_OB = Z_VB + MLW
Z_UC = Z_OB + MLW
Z_VC = Z_UC + SGW
Z_GATES = Z_VC + SGW
NH, HD = 16, 64
HALF = HD // 2
FF = 2816
FE = FF // 256
SCB = D // P

UNIT = 2048
U_WIN = 0
U_WOUT = U_WIN + 13
U_MOE = U_WOUT + 4
U_PLEG = U_MOE + 3 * NE
U_PLEP = U_PLEG + 4
U_SCIN = U_PLEP + 1
U_SCOUT = U_SCIN + 12
U_FFN0 = U_SCOUT + 4
U_QKV = U_FFN0 + 3 * FE
U_WO = U_QKV + 12
U_FFN1 = U_WO + 4
UNITS = U_FFN1 + 3 * FE
RING = 3

C_WIN, C_WOUT, C_PLEG, C_PLEP, C_SCOUT, C_QKV, C_WO, CHUNKS = 0, 7, 9, 11, 13, 15, 21, 23
BY_ACT = [1] * 7 + [0] * 2 + [1] * 2 + [0] * 2 + [0] * 2 + [0] * 4 + [1] * 2 + [0] * 2
BY_DVE = [1] * 7 + [1, 0] + [0] * 2 + [1] * 2 + [1, 0] + [1] * 4 + [0] * 2 + [1, 0]
CHUNK_END = [2, 4, 6, 8, 10, 12, 13] + [u + 2 * c + 2 for u, n in ((U_WOUT, 2), (U_PLEG, 2)) for c in range(n)] \
    + [U_PLEP + 1] * 2 + [u + 2 * c + 2 for u, n in ((U_SCOUT, 2), (U_QKV, 6), (U_WO, 2)) for c in range(n)]
G_MOE, G_SC, G_FFN0, G_FFN1 = 0, NE, NE + 6, NE + 6 + FE
D_MOE, D_FFN0, D_FFN1 = 0, NE, NE + FE


def layout(parts):
    at, out = 0, {}
    for name, width in parts:
        out[name] = (at, at + width)
        at += width
    return out, at


CONST, CONST_W = layout([("ident", P), ("later", P), ("ones", P), ("upto", P), ("strict", P), ("bigpast", P),
                         ("causal", P), ("cos", TT * HALF), ("sin", TT * HALF), ("iota4", NG), ("iota32", NE),
                         ("neghalf", 8)])
PARAM, PARAM_W = layout([("g0", KD), ("g1", KD), ("g2", KD), ("g3", KD), ("g4", KD), ("g5", KD), ("g6", KD),
                         ("g7", KD), ("gates_b", GATES), ("conv_w", 8 * CONV_K), ("conv_b", 8), ("ln_g", SGW),
                         ("ln_b", SGW), ("sgu_b", SGG), ("sgu_w", SGG * P), ("router_b", NG + NE),
                         ("router_w", KD * (NG + NE)), ("sc_conv", 3 * SCB), ("ffn_conv", 2 * FE * 12),
                         ("p_t", 2 * T)])

A_S = TT * N_IN
A_T1 = A_S + SBH * 384
A_QKA = A_T1 + SBH * 384
A_CV = A_QKA + 6 * T
A_QKB = A_CV + 8 * (T + 3)
ARENA = A_QKB + 8 * T


def program(nc, stream, table, params, finals, x_in, out):
    ctx = ExitStack()
    with ctx:
        def sb(name, shape, dt=F32):
            return ctx.enter_context(nc.sbuf_tensor(name, shape, dt))

        sems = {}

        def S(name):
            if name not in sems:
                sems[name] = ctx.enter_context(nc.semaphore(name))
            return sems[name]

        raw = sb("raw", [P, RING, UNIT])
        whi = sb("whi", [P, RING, UNIT], F32R)
        wlo = sb("wlo", [P, RING, UNIT], F32R)
        cst = sb("cst", [P, CONST_W])
        par = sb("par", [P, PARAM_W])
        xres = sb("xres", [P, TT, D])
        xn = sb("xn", [P, TT, D])
        xhi = sb("xhi", [P, KD, T], F32R)
        xlo = sb("xlo", [P, KD, T], F32R)
        hhi = sb("hhi", [P, 2, 2, T], F32R)
        hlo = sb("hlo", [P, 2, 2, T], F32R)
        rhi = sb("rhi", [P, KD, NG + NE], F32R)
        rlo = sb("rlo", [P, KD, NG + NE], F32R)
        phi = sb("phi", [P, 2, T], F32R)
        plo = sb("plo", [P, 2, T], F32R)
        identr = sb("identr", [NE, P], F32R)
        wthi = sb("wthi", [NE, T], F32R)
        wtlo = sb("wtlo", [NE, T], F32R)
        arena = sb("arena", [P, ARENA])
        sumsq = sb("sumsq", [P, TT])
        rstd = sb("rstd", [P, TT])
        mean = sb("mean", [P, TT])
        sm = sb("sm", [P, 640])
        final_g = sb("final_g", [P, D])
        cwn = sb("cwn", [P, 2, 12])
        bank = [ctx.enter_context(nc.psum_tensor(f"bank{i}", [P, 512], F32)) for i in range(8)]

        def C(name):
            a, b = CONST[name]
            return cst[:, a:b]

        def Q(name):
            a, b = PARAM[name]
            return par[:, a:b]

        ident = C("ident")
        sgu_w = Q("sgu_w").rearrange("p (g t) -> p g t", g=SGG)
        router_w = Q("router_w").rearrange("p (k n) -> p k n", k=KD)
        conv_w = Q("conv_w").rearrange("p (j t) -> p j t", j=8)
        sc_conv = Q("sc_conv").rearrange("p (t j) -> p t j", t=3)
        ffn_conv = Q("ffn_conv").rearrange("p (l n) -> p l n", l=2)
        gate_b = Q("gates_b")
        p_t = Q("p_t").rearrange("p (k t) -> p k t", k=2)
        small = {}
        at = 0
        for name, width in [("gt", 16), ("lf", 8), ("la", 8), ("ccol", 16), ("den", 8), ("ssb", 8), ("msb", 8),
                            ("rsb", 8), ("ssac", 4), ("msac", 4), ("rsac", 4), ("mu", 8), ("ssc", 8), ("msc", 8),
                            ("rsc", 8), ("lg", 72), ("gmax", 2), ("eqg", 8), ("ohg", 8), ("idx", 2), ("pen", 8),
                            ("eg", 8), ("gw", 2), ("em", 64), ("v1", 2), ("v2", 2), ("oh1", 64), ("oh2", 64),
                            ("cand", 64), ("dv", 2), ("p1", 2), ("p2", 2), ("m", 4), ("nm", 4), ("l", 4), ("rl", 4)]:
            small[name] = (at, at + width)
            at += width
        assert at <= 640

        def V(name):
            a, b = small[name]
            return sm[:, a:b]

        z = arena[:, 0:TT * N_IN].rearrange("p (a n) -> p a n", a=TT)
        sa = arena[:, A_S:A_T1].rearrange("p (h b t) -> p h b t", h=SBH, b=3)
        t1 = arena[:, A_T1:A_QKA].rearrange("p (h b t) -> p h b t", h=SBH, b=3)
        sa_flat = arena[:, A_S:A_T1]
        t1_flat = arena[:, A_T1:A_QKA]
        qka = arena[:, A_QKA:A_CV].rearrange("p (j t) -> p j t", j=6)
        qka_flat = arena[:, A_QKA:A_CV]
        cvb = arena[0:MLD, A_CV:A_QKB].rearrange("p (j t) -> p j t", j=8)
        qkb = arena[0:MLD, A_QKB:ARENA].rearrange("p (j t) -> p j t", j=8)
        mw = arena[:, A_CV:A_CV + MLH * 384].rearrange("p (h b t) -> p h b t", h=MLH, b=3)
        tmp = arena[:, 0:2 * SBW]
        rows = arena[0:MLH, A_QKA:A_QKA + 5 * T].rearrange("p (r t) -> p r t", r=5)
        wbc = arena[:, 0:NE * T].rearrange("p (e t) -> p e t", e=NE)
        A_H = NE * T
        sgl = arena[:, A_H:A_H + 1024].rearrange("p (b n) -> p b n", b=2)
        hv = arena[:, A_H + 1024:A_H + 2048].rearrange("p (b n) -> p b n", b=2)
        gsb = arena[:, 0:TT * D].rearrange("p (a n) -> p a n", a=TT)
        gpr = arena[:, TT * D:TT * D + 1024].rearrange("p (a n) -> p a n", a=TT)
        csb = arena[:, 0:1024].rearrange("p (b n) -> p b n", b=2)
        cvp = arena[:, 1024:1024 + SCB * (T + 2)].rearrange("p (j t) -> p j t", j=SCB)
        A_Y = 1024 + SCB * (T + 2)
        scy = arena[:, A_Y:A_Y + SCB * T].rearrange("p (j t) -> p j t", j=SCB)
        facc = arena[:, 0:2048].rearrange("p (b f t) -> p b f t", b=2, f=4)
        qkv = arena[:, 0:TT * 3 * D].rearrange("p (a n) -> p a n", a=TT)
        A_QT = TT * 3 * D
        qkt = arena[:, A_QT:A_QT + 16 * T].rearrange("p (j t) -> p j t", j=16)
        qkt_flat = arena[:, A_QT:A_QT + 16 * T]
        A_RP = A_QT + 16 * T
        rp = arena[:, A_RP:A_RP + 1024].rearrange("p (k n) -> p k n", k=4)
        ap_ = arena[:, A_RP + 1024:A_RP + 1024 + 768].rearrange("p (b n) -> p b n", b=2)
        apt = arena[:, A_RP + 1792:A_RP + 2560].rearrange("p (b n) -> p b n", b=2)

        block = ctx.enter_context(nc.Block())

        R_WOUT, R_MOE, R_PLE, R_FINAL1, R_SC, R_FFN0, R_ATT, R_FFN1 = range(1, 9)
        NORM_READS = [0, R_WOUT, R_MOE, R_PLE, R_FINAL1, R_SC, R_FFN0, R_ATT, R_FFN1]

        def group_end(u0, e, e0):
            return u0 + 2 if e0 == 0 else e * 3 + (u0 + 1)

        def down_end(u0, count, e, e0):
            return e * 3 + (u0 + 5)

        class Chain:

            def __init__(self, eng, sem):
                self.eng, self.sem, self.n, self.off = eng, sem, 0, 0

            def link(self, ins):
                self.n += 1
                ins.then_inc(self.sem, 1)
                self.eng.wait_ge(self.sem, self.off + self.n)

            def enter(self, j, per):
                self.off, self.start = j * per, self.n

            def leave(self, per, times):
                assert self.n - self.start == per
                self.off, self.n = 0, self.start + per * times

        @block.sync
        def _(sp):
            sp.dma_start(xres[:], x_in).then_inc(S("x_loaded"), 16)
            sp.dma_start(cst[:], table).then_inc(S("table_loaded"), 16)
            sp.dma_start(raw[:, 0, :], stream[0]).then_inc(S("landed0"), 16)
            sp.dma_start(par[:], params).then_inc(S("params_loaded"), 16)
            sp.dma_start(final_g[:], finals[0]).then_inc(S("final1_loaded"), 16)
            for n in range(1, RING):
                sp.dma_start(raw[:, n, :], stream[n]).then_inc(S(f"landed{n}"), 16)
            with sp.Fori(0, UNITS // RING - 1) as j:
                for s in range(RING):
                    sp.wait_ge(S("low_done"), RING * j + s + 1)
                    sp.dma_start(raw[:, s, :], stream[RING * j + (s + RING)]).then_inc(S(f"landed{s}"), 16)
            sp.wait_ge(S("y_ready"), 1)
            sp.dma_start(out, xn[:]).then_inc(S("stored"), 16)
            sp.wait_ge(S("stored"), 16)

        @block.scalar
        def _(act):
            chain = Chain(act, S("act_chain"))
            done = [0]

            def split(n):
                unit0, off = n if isinstance(n, tuple) else (n, 0)
                s = unit0 % RING
                act.wait_ge(S(f"landed{s}"), off * 16 // RING + 16 * (unit0 // RING + 1) if isinstance(off, int)
                            else off * (16 // 1) + 16 * (unit0 // RING + 1))
                if unit0 >= RING:
                    act.wait_ge(S("unit_used"), (off if isinstance(off, int) else off * RING) + unit0 - RING + 1)
                act.activation(whi[:, s, :], raw[:, s, :], ACT.Copy).then_inc(S("high_done"), 1)

            def split_to(n):
                while done[0] <= min(n, UNITS - 1):
                    split(done[0])
                    done[0] += 1

            def norm_act(i, turn=True):
                if i == 0:
                    act.wait_ge(S("x_loaded"), 16)
                else:
                    act.wait_ge(S("residual_ready"), NORM_READS[i])
                for t in range(TT):
                    ins = act.activation(xn[:, t, :], xres[:, t, :], ACT.Square, accum_out=sumsq[:, t:t + 1])
                ins.then_inc(S("sumsq_ready"), 1)
                if turn:
                    act.wait_ge(S("rstd_ready"), i + 1)
                    act.activation(xn[:, 1, :], xres[:, 1, :], ACT.Copy, scale=rstd[:, 1:2]).then_inc(S("xn1_ready"), 1)

            def turn_act(q):
                for k in range(KD):
                    if k % 2 == 0:
                        act.wait_ge(S("turned"), 4 * q + k // 2 + 1)
                    ins = act.activation(xhi[:, k, :], bank[k // 2][:, (k % 2) * T:(k % 2 + 1) * T], ACT.Copy,
                                         scale=Q(f"g{q}")[:, k:k + 1])
                    if k % 2:
                        ins.then_inc(S("xhi_ready"), 1)

            split_to(0)
            act.wait_ge(S("table_loaded"), 16)
            act.wait_ge(S("params_loaded"), 16)
            norm_act(0)
            split_to(1)
            act.activation(rhi[:], router_w, ACT.Copy).then_inc(S("setup_high"), 1)
            act.activation(phi[:], p_t, ACT.Copy).then_inc(S("setup_high"), 1)
            act.activation(identr[:], ident[0:NE, :], ACT.Copy).then_inc(S("setup_high"), 1)
            turn_act(0)
            for c in range(7):
                split_to(min(U_WIN + 2 * c + 1, 12) + 2)
                act.wait_ge(S("unit_used"), CHUNK_END[C_WIN + c])
                w = min(512, N_IN - 512 * c)
                act.activation(z[:, 0, 512 * c:512 * c + w], bank[2 * (c % 2)][:, 0:w], ACT.Copy)\
                   .then_inc(S("act_freed"), 1)
            split_to(15)
            for b in (0, 2):
                act.wait_ge(S("turned_a"), b + 1)
                act.activation(qka_flat[:, 512 * b:512 * b + 512], bank[4 + b][:], ACT.Copy).then_inc(S("qka_act"), 1)
            for b in range(2):
                act.wait_ge(S("turned_b"), b + 1)
                act.activation(cvb[:, 2 * b:2 * b + 2, 3:3 + T],
                               bank[(7, 0, 1, 2)[b]][0:MLD, :].rearrange("p (j t) -> p j t", j=2), ACT.Copy)\
                   .then_inc(S("cvb_act"), 1)
            act.wait_ge(S("dve_freed"), sum(BY_DVE[:7]))
            chain.link(act.activation(z[:, :, Z_UC:Z_GATES], z[:, :, Z_UC:Z_GATES], ACT.Gelu_apprx_tanh))
            act.activation(z[:, :, Z_OB:Z_UC], z[:, :, Z_OB:Z_UC], ACT.Sigmoid).then_inc(S("gelu_ready"), 1)
            act.wait_ge(S("cvb_dve"), 2)
            act.wait_ge(S("cvb_pad"), 1)
            act.wait_ge(S("cvb_act"), 2)
            for j in range(8):
                act.activation(qkb[:, j, :], cvb[:, j, 3:3 + T], ACT.Identity, scale=conv_w[0:MLD, j, 3:4],
                               bias=Q("conv_b")[0:MLD, j:j + 1]).then_inc(S("conv_begun"), 1)
            for h in range(SBH):
                act.wait_ge(S("scores_a"), h + 1)
                b = bank[(3, 4, 5, 6, 7, 0)[h]]
                act.activation(sa_flat[:, 384 * h:384 * h + 384], b[:, 0:384], ACT.Copy, scale=SBD ** -0.5)
                ins = act.activation(t1_flat[:, 384 * h:384 * h + 384], b[:, 0:384], ACT.Abs, scale=SBD ** -0.5)
            chain.link(ins)
            chain.link(act.activation(t1_flat, t1_flat, ACT.Exp, scale=-1.0))
            act.wait_ge(S("gates_ready"), 1)
            gt = V("gt").rearrange("p (a n) -> p a n", a=TT)
            la = V("la").rearrange("p (a n) -> p a n", a=TT)
            chain.link(act.activation(la, gt[:, :, 4:8], ACT.Abs))
            chain.link(act.activation(la, la, ACT.Exp, scale=-1.0))
            act.activation(la, la, ACT.Ln, bias=1.0).then_inc(S("gate_log"), 1)
            act.activation(t1_flat, t1_flat, ACT.Ln, bias=1.0).then_inc(S("softplus_log"), 1)
            act.wait_ge(S("conv_done"), 1)
            act.activation(qkb[:], qkb[:], ACT.Silu).then_inc(S("qkb_ready"), 1)
            act.wait_ge(S("mrow_ready"), 1)
            act.activation(rows[:, 4, :], rows[:, 3, :], ACT.Exp, scale=-1.0).then_inc(S("enrow_ready"), 1)
            act.wait_ge(S("ccol_ready"), 1)
            act.wait_ge(S("mw_ready"), 1)
            ccol = V("ccol")
            for h in range(MLH):
                act.activation(mw[:, h, 0:2, :], mw[:, h, 0:2, :], ACT.Exp, scale=-1.0, bias=ccol[:, h:h + 1])
                act.activation(mw[:, h, 2, :], mw[:, h, 2, :], ACT.Exp, scale=-1.0, bias=ccol[:, 4 + h:5 + h])\
                   .then_inc(S("decay_ready"), 1)
            act.wait_ge(S("expo_ready"), 1)
            act.activation(sa_flat, sa_flat, ACT.Exp).then_inc(S("weights_a"), 1)
            act.wait_ge(S("out_a"), 1)
            ssac = V("ssac")
            for t in range(TT):
                chain.link(act.activation(xn[:, t, 0:SBW], bank[1 + t][:, 0:SBW], ACT.Copy))
            for t in range(TT):
                ins = act.activation(tmp[:, 0:SBW], xn[:, t, 0:SBW], ACT.Square, accum_out=ssac[:, t:t + 1])
                chain.link(ins)
            act.wait_ge(S("yc_ready"), 1)
            for t in range(TT):
                ins = act.activation(tmp[:, 0:SGW], xn[:, t, SBW + MLW:D], ACT.Square, accum_out=ssac[:, 2 + t:3 + t])
                if t == 0:
                    chain.link(ins)
            ins.then_inc(S("sumsq_ac"), 1)
            act.wait_ge(S("sumsq_ac"), 1)
            act.wait_ge(S("hb_ready"), 1)
            act.activation(tmp.rearrange("p (a n) -> p a n", a=TT), xn[:, :, SBW:SBW + MLW], ACT.Square)\
               .then_inc(S("hb_squares"), 1)
            act.wait_ge(S("rstd_ac"), 1)
            for t in range(TT):
                act.activation(xn[:, t, 0:SBW], xn[:, t, 0:SBW], ACT.Copy, scale=V("rsac")[:, t:t + 1])
                ins = act.activation(xn[:, t, SBW + MLW:D], xn[:, t, SBW + MLW:D], ACT.Copy,
                                     scale=V("rsac")[:, 2 + t:3 + t])
            ins.then_inc(S("xn1_ready"), 1)
            turn_act(1)
            for c in range(2):
                split_to(U_WOUT + 2 * c + 3)
            norm_act(1)
            turn_act(2)
            act.wait_ge(S("gdiff_ready"), 1)
            act.activation(V("eg"), V("eg"), ACT.Exp).then_inc(S("gexp_ready"), 1)
            act.wait_ge(S("vdiff_ready"), 1)
            act.activation(V("dv"), V("dv"), ACT.Exp).then_inc(S("vexp_ready"), 1)
            act.wait_ge(S("wt_turned"), 1)
            act.activation(wthi[:], bank[0][0:NE, 256:512], ACT.Copy).then_inc(S("wthi_ready"), 1)
            for b in range(0, NE // 2, 2):
                act.wait_ge(S("wbc_done"), b + 1)
                act.activation(wbc[:, 2 * b:2 * b + 2, :],
                               bank[4 + b % 4][:].rearrange("p (e t) -> p e t", e=2), ACT.Copy)\
                   .then_inc(S("wbc_act"), 1)

            def moe_act(e, off, e0, last=False):
                b = e0 % 2
                n = U_MOE + 3 * e0 - 1
                at = lambda k: (n + k, off)
                if off is None:
                    split_to(n + 3)
                else:
                    split(at(3))
                act.wait_ge(S("unit_used"), group_end(U_MOE, e, e0))
                if e0 >= 2:
                    act.wait_ge(S("g_free"), G_MOE - 1 + e)
                act.activation(sgl[:, b, :], bank[2 * b][:], ACT.Silu).then_inc(S("silu_ready"), 1)
                if off is None:
                    split_to(n + 5)
                else:
                    split(at(4))
                    split(at(5))
                act.wait_ge(S("g_free"), G_MOE + 1 + e)
                if e0 >= 2:
                    act.wait_ge(S("unit_used"), down_end(U_MOE, NE, e - 2, e0 - 2))
                act.activation(hhi[:, b, :, :], hv[:, b, :].rearrange("p (f t) -> p f t", f=2), ACT.Copy)\
                   .then_inc(S("hhi_ready"), 1)

            def ffn_act(layer, e, off, e0):
                g0, d0, u0 = (G_FFN0, D_FFN0, U_FFN0) if layer == 0 else (G_FFN1, D_FFN1, U_FFN1)
                b, gb = e0 % 2, (g0 + e0) % 2
                n = u0 + 3 * e0 - 1

                def ahead(k):
                    if off is None:
                        split_to(n + k)
                    elif n + k < UNITS:
                        split((n + k, off))
                ahead(3)
                act.wait_ge(S("unit_used"), group_end(u0, e, e0))
                act.wait_ge(S("taps_ready"), layer * FE + 1 + e)
                if e0 >= 2:
                    act.wait_ge(S("hhi_ready"), d0 - 1 + e)
                    act.wait_ge(S("h_ready"), d0 - 1 + e)
                for f in range(4):
                    ins = act.activation(facc[:, b, f, :], bank[2 * gb + f // 2][:, (f % 2) * T:(f % 2 + 1) * T],
                                         ACT.Copy, scale=cwn[:, b, 8 + f:9 + f])
                ins.then_inc(S("ffn_begun"), 1)
                ahead(4)
                act.wait_ge(S("g_free"), g0 + 1 + e)
                act.activation(facc[:, b, 0:2, :], facc[:, b, 0:2, :], ACT.Silu).then_inc(S("silu_ready"), 1)
                ahead(5)
                act.wait_ge(S("hv_ready"), layer * FE + 1 + e)
                if e0 >= 2:
                    act.wait_ge(S("unit_used"), down_end(u0, FE, e - 2, e0 - 2))
                act.activation(hhi[:, b, :, :], facc[:, b, 2:4, :], ACT.Copy).then_inc(S("hhi_ready"), 1)

            moe_act(0, None, 0)
            moe_act(1, None, 1)
            with act.Fori(0, (NE - 2) // 2) as j:
                for b in range(2):
                    moe_act(2 * j + (2 + b), 2 * j, 2 + b)
            done[0] = U_MOE + 3 * NE + 2
            norm_act(2)
            turn_act(3)
            for c in range(2):
                split_to(U_PLEG + 2 * c + 3)
                act.wait_ge(S("unit_used"), CHUNK_END[C_PLEG + c])
                for t in range(TT):
                    ins = act.activation(gsb[:, t, 512 * c:512 * c + 512], bank[2 * ((C_PLEG + c) % 2) + t][:],
                                         ACT.Sigmoid)
                ins.then_inc(S("act_freed"), 1)
            split_to(U_PLEP + 2)
            norm_act(3, turn=False)
            split_to(U_SCIN + 1)
            norm_act(4)
            act.wait_ge(S("residual_ready"), R_FINAL1)
            act.dma_start(final_g[:], finals[1]).then_inc(S("final2_loaded"), 16)
            turn_act(4)
            for i in range(6):
                split_to(U_SCIN + 2 * i + 3)
                if i < 4:
                    g = G_SC + i
                    act.wait_ge(S("unit_used"), U_SCIN + 2 * i + 2)
                    act.activation(csb[:, i % 2, :], bank[2 * (g % 2)][:], ACT.Copy).then_inc(S("c_ready"), 1)
                    act.wait_ge(S("g_free"), g + 1)
                    for f in range(2 * i, 2 * i + 2):
                        ins = act.activation(scy[:, f, :], cvp[:, f, 2:2 + T], ACT.Copy, scale=sc_conv[:, 2, f:f + 1])
                    ins.then_inc(S("sc_begun"), 1)
            for f in range(4):
                act.wait_ge(*((S("g_free"), G_SC + 5 + f // 2) if f % 2 else (S("sc_product"), f // 2 + 1)))
                act.activation(xhi[:, 2 * f:2 * f + 2, :], scy[:, 2 * f:2 * f + 2, :], ACT.Copy)\
                   .then_inc(S("sc_high"), 1)
            for c in range(2):
                split_to(U_SCOUT + 2 * c + 3)

            def ffn(layer):
                ffn_act(layer, 0, None, 0)
                ffn_act(layer, 1, None, 1)
                u0 = U_FFN0 if layer == 0 else U_FFN1
                assert done[0] == min(u0 + 8, UNITS)
                with act.Fori(0, (FE - 3) // 2) as j:
                    for b in range(2):
                        ffn_act(layer, 2 * j + (2 + b), 2 * j, 2 + b)
                done[0] = u0 + 3 * (FE - 1) + 2
                ffn_act(layer, FE - 1, None, FE - 1)

            norm_act(5)
            turn_act(5)
            ffn(0)
            norm_act(6)
            turn_act(6)
            for c in range(6):
                split_to(U_QKV + 2 * c + 3)
                if c >= 4:
                    act.wait_ge(S("unit_used"), CHUNK_END[C_QKV + c])
                    for t in range(TT):
                        ins = act.activation(qkv[:, t, 512 * c:512 * c + 512], bank[2 * ((C_QKV + c) % 2) + t][:],
                                             ACT.Copy)
                    ins.then_inc(S("act_freed"), 1)
            split_to(U_WO + 2)
            for b in range(0, 8, 2):
                act.wait_ge(S("qk_turned"), b + 1)
                act.activation(qkt_flat[:, 512 * b:512 * b + 512], bank[b][:], ACT.Copy).then_inc(S("qkt_act"), 1)

            def pt_copy(h):
                act.wait_ge(S("p_turned"), h + 1)
                if h >= 2:
                    act.wait_ge(S("pv_done"), h - 1)
                act.activation(apt[:, h % 2, :], bank[2 + h % 2][:, 0:384], ACT.Copy).then_inc(S("pt_ready"), 1)

            for h in range(NH):
                act.wait_ge(S("negmax_ready"), h + 1)
                if h >= 2:
                    act.wait_ge(S("p_turned"), h - 1)
                b = h % 2
                nm, l = V("nm"), V("l")
                act.activation(ap_[:, b, 0:128], bank[b][:, 0:128], ACT.Exp, scale=HD ** -0.5,
                               bias=nm[:, 2 * b:2 * b + 1], accum_out=l[:, 2 * b:2 * b + 1])
                act.activation(ap_[:, b, 128:384], bank[b][:, 128:384], ACT.Exp, scale=HD ** -0.5,
                               bias=nm[:, 2 * b + 1:2 * b + 2], accum_out=l[:, 2 * b + 1:2 * b + 2])\
                   .then_inc(S("exp_done"), 1)
                if h >= 1:
                    pt_copy(h - 1)
            pt_copy(NH - 1)
            for b in range(4):
                act.wait_ge(S("pv_done"), 4 * b + 4)
                act.activation(xhi[:, 2 * b:2 * b + 2, :], bank[4 + b][:].rearrange("p (j t) -> p j t", j=2),
                               ACT.Copy).then_inc(S("o_high"), 1)
            for c in range(2):
                split_to(U_WO + 2 * c + 3)
            norm_act(7)
            turn_act(7)
            ffn(1)
            norm_act(8, turn=False)

        @block.gpsimd
        def _(pool):
            chain = Chain(pool, S("pool_chain"))
            nh = C("neghalf")

            def rsqrt(dst, mid, src, count, width):
                chain.link(pool.tensor_scalar(mid, src, 1.0 / count, EPS, ALU.mult, ALU.add))
                return pool.tensor_tensor(dst, mid, nh[:, 0:width], ALU.pow)

            def norm_pool(i):
                pool.wait_ge(S("sumsq_ready"), i + 1)
                rsqrt(rstd[:], mean[:], sumsq[:], D, TT).then_inc(S("rstd_ready"), 1)
                pool.wait_ge(S("rstd_ready"), i + 1)

            pool.memset(cvb[:, :, 0:3], 0.0).then_inc(S("cvb_pad"), 1)
            pool.wait_ge(S("cvb_pad"), 1)
            pool.wait_ge(S("table_loaded"), 16)
            norm_pool(0)
            pool.wait_ge(S("params_loaded"), 16)
            pool.memset(sgu_w[64:128, :, 0:64], 0.0).then_inc(S("sgu_masked"), 1)
            pool.wait_ge(S("sgu_masked"), 1)
            pool.wait_ge(S("ln_squares"), 1)
            rsqrt(V("rsc"), V("msc"), V("ssc"), SGD, 8).then_inc(S("ln_rstd"), 1)
            pool.wait_ge(S("sumsq_ac"), 1)
            chain.link(pool.tensor_scalar(V("msac")[:, 0:2], V("ssac")[:, 0:2], 1.0 / SBW, EPS, ALU.mult, ALU.add))
            chain.link(pool.tensor_scalar(V("msac")[:, 2:4], V("ssac")[:, 2:4], 1.0 / SGW, EPS, ALU.mult, ALU.add))
            pool.tensor_tensor(V("rsac"), V("msac"), nh[:, 0:4], ALU.pow).then_inc(S("rstd_ac"), 1)
            pool.wait_ge(S("hb_sums"), 1)
            rsqrt(V("rsb"), V("msb"), V("ssb"), MLD, 8).then_inc(S("hb_rstd"), 1)
            norm_pool(1)

            def moe_pool(e):
                b = e % 2 if isinstance(e, int) else e[1] % 2
                ev = e if isinstance(e, int) else e[0]
                pool.wait_ge(S("silu_ready"), ev + 1)
                half = sgl[:, b, :].rearrange("p (f t) -> p f t", f=2)
                w = wbc[:, ev:ev + 1, :] if isinstance(e, int) else arena[:, bass.ds(ev * T, T)].unsqueeze(1)
                pool.tensor_tensor(half, half, w.broadcast_to([P, 2, T]), ALU.mult).then_inc(S("weighted"), 1)

            pool.wait_ge(S("wbc_act"), NE // 4)
            pool.wait_ge(S("wbc_dve"), NE // 4)
            moe_pool(0)
            moe_pool(1)
            with pool.Fori(0, (NE - 2) // 2) as j:
                for b in range(2):
                    moe_pool((2 * j + (2 + b), 2 + b))
            norm_pool(2)
            norm_pool(3)
            norm_pool(4)

            def taps(layer, e, e0):
                g0 = G_FFN0 if layer == 0 else G_FFN1
                b = e0 % 2
                if e0 >= 2 or layer == 1:
                    pool.wait_ge(S("g_free"), g0 - 1 + e)
                src = ffn_conv[:, layer, 12 * e0:12 * e0 + 12] if isinstance(e, int) else \
                    par[:, bass.ds(e * 12 + (PARAM["ffn_conv"][0] + layer * FE * 12), 12)]
                pool.tensor_copy(cwn[:, b, :], src).then_inc(S("taps_ready"), 1)

            def ffn(layer):
                taps(layer, 0, 0)
                taps(layer, 1, 1)
                with pool.Fori(0, (FE - 3) // 2) as j:
                    for b in range(2):
                        taps(layer, 2 * j + (2 + b), 2 + b)
                taps(layer, FE - 1, FE - 1)

            norm_pool(5)
            ffn(0)
            norm_pool(6)
            norm_pool(7)
            ffn(1)
            norm_pool(8)

        @block.vector
        def _(dve):
            chain = Chain(dve, S("dve_chain"))
            link = chain.link
            done = [0]

            def split(n):
                unit0, off = n if isinstance(n, tuple) else (n, 0)
                s = unit0 % RING
                dve.wait_ge(S("high_done"), (off if isinstance(off, int) else off * RING) + unit0 + 1)
                dve.tensor_tensor(wlo[:, s, :], raw[:, s, :], whi[:, s, :].bitcast(F32), ALU.subtract)\
                   .then_inc(S("low_done"), 1)

            def split_to(n):
                while done[0] <= min(n, UNITS - 1):
                    split(done[0])
                    done[0] += 1

            def norm_dve(i):
                dve.wait_ge(S("rstd_ready"), i + 1)
                dve.tensor_scalar(xn[:, 0, :], xres[:, 0, :], rstd[:, 0:1], None, ALU.mult)\
                   .then_inc(S("xn0_ready"), 1)

            def turn_dve(q):
                for k in range(KD):
                    if k % 2 == 0:
                        dve.wait_ge(S("xhi_ready"), 4 * q + k // 2 + 1)
                    ins = dve.scalar_tensor_tensor(xlo[:, k, :], bank[k // 2][:, (k % 2) * T:(k % 2 + 1) * T],
                                                   Q(f"g{q}")[:, k:k + 1], xhi[:, k, :].bitcast(F32), ALU.mult,
                                                   ALU.subtract)
                    if k % 2:
                        ins.then_inc(S("xt_ready"), 1)

            def add_chunks(u0, c0):
                for c in range(2):
                    split_to(u0 + 2 * c + 3)
                    dve.wait_ge(S("unit_used"), CHUNK_END[c0 + c])
                    for t in range(TT):
                        r = xres[:, t, 512 * c:512 * c + 512]
                        ins = dve.tensor_tensor(r, bank[2 * ((c0 + c) % 2) + t][:], r, ALU.add)
                    ins.then_inc(S("dve_freed") if c == 0 else S("residual_ready"), 1)

            def add_down(units):
                dve.wait_ge(S("unit_used"), units)
                for t in range(TT):
                    for c in range(2):
                        r = xres[:, t, 512 * c:512 * c + 512]
                        ins = dve.tensor_tensor(r, bank[4 + 2 * t + c][:], r, ALU.add)
                ins.then_inc(S("residual_ready"), 1)

            split_to(0)
            dve.wait_ge(S("table_loaded"), 16)
            dve.wait_ge(S("params_loaded"), 16)
            dve.wait_ge(S("x_loaded"), 16)
            norm_dve(0)
            split_to(1)
            dve.wait_ge(S("setup_high"), 3)
            dve.tensor_tensor(rlo[:], router_w, rhi[:].bitcast(F32), ALU.subtract)
            dve.tensor_tensor(plo[:], p_t, phi[:].bitcast(F32), ALU.subtract).then_inc(S("setup_low"), 1)
            turn_dve(0)
            for c in range(7):
                split_to(min(U_WIN + 2 * c + 1, 12) + 2)
                dve.wait_ge(S("unit_used"), CHUNK_END[C_WIN + c])
                w = min(512, N_IN - 512 * c)
                dve.tensor_copy(z[:, 1, 512 * c:512 * c + w], bank[2 * (c % 2) + 1][:, 0:w]).then_inc(S("dve_freed"), 1)
            split_to(15)
            dve.wait_ge(S("act_freed"), 7)
            dve.wait_ge(S("dve_freed"), 7)
            gt = V("gt").rearrange("p (a n) -> p a n", a=TT)
            dve.tensor_tensor(gt, z[:, :, Z_GATES:N_IN], gate_b.unsqueeze(1).broadcast_to([P, TT, GATES]), ALU.add)\
               .then_inc(S("gates_ready"), 1)
            dve.wait_ge(S("turned_a"), 2)
            dve.tensor_copy(qka_flat[:, 512:1024], bank[5][:]).then_inc(S("qka_dve"), 1)
            for b in range(2, 4):
                dve.wait_ge(S("turned_b"), b + 1)
                dve.tensor_copy(cvb[:, 2 * b:2 * b + 2, 3:3 + T],
                                bank[(7, 0, 1, 2)[b]][0:MLD, :].rearrange("p (j t) -> p j t", j=2))\
                   .then_inc(S("cvb_dve"), 1)
            dve.wait_ge(S("cvb_act"), 2)
            dve.wait_ge(S("cvb_pad"), 1)
            dve.wait_ge(S("conv_begun"), 8)
            for k in range(3):
                for j in range(8):
                    ins = dve.scalar_tensor_tensor(qkb[:, j, :], cvb[:, j, k:k + T], conv_w[0:MLD, j, k:k + 1],
                                                   qkb[:, j, :], ALU.mult, ALU.add)
                if k < 2:
                    link(ins)
            ins.then_inc(S("conv_done"), 1)
            dve.wait_ge(S("gates_ready"), 1)
            dve.wait_ge(S("gate_log"), 1)
            lf = V("lf").rearrange("p (a n) -> p a n", a=TT)
            dve.scalar_tensor_tensor(lf, gt[:, :, 4:8], 0.0, V("la").rearrange("p (a n) -> p a n", a=TT),
                                     ALU.min, ALU.subtract).then_inc(S("logf_ready"), 1)
            dve.wait_ge(S("softplus_log"), 1)
            link(dve.scalar_tensor_tensor(t1_flat, sa_flat, 0.0, t1_flat, ALU.max, ALU.add))
            link(dve.tensor_tensor(sa_flat, sa_flat, t1_flat, ALU.subtract))
            strict = C("strict").unsqueeze(1).broadcast_to([P, SBH, P])
            link(dve.tensor_tensor(t1[:, :, 2, :], t1[:, :, 2, :], strict, ALU.mult))
            dve.tensor_tensor(t1[:, :, 0, :], t1[:, :, 0, :], strict, ALU.mult).then_inc(S("l_ready"), 1)
            dve.wait_ge(S("brow_done"), 1)
            link(dve.tensor_copy(rows[:, 0, :], bank[1][0:MLH, 0:T]))
            link(dve.tensor_tensor(rows[:, 1, :], bank[1][0:MLH, T:2 * T], rows[:, 0, :], ALU.subtract))
            link(dve.tensor_tensor_scan(rows[:, 2, :], rows[:, 1, :], rows[:, 1, :], 0.0, ALU.max, ALU.max))
            dve.tensor_tensor(rows[:, 3, :], rows[:, 0, :], rows[:, 2, :], ALU.add).then_inc(S("mrow_ready"), 1)
            dve.wait_ge(S("gelu_ready"), 1)
            vg = [z[:, t, Z_VC:Z_GATES].rearrange("p (g d) -> p g d", g=SGG) for t in range(TT)]
            mu = V("mu").rearrange("p (a g) -> p a g", a=TT)
            ssc = V("ssc").rearrange("p (a g) -> p a g", a=TT)
            rsc = V("rsc").rearrange("p (a g) -> p a g", a=TT)
            sq = [tmp[:, 256 * t:256 * t + 256].rearrange("p (g d) -> p g d", g=SGG) for t in range(TT)]
            wide = lambda v, t: v[:, t, :].unsqueeze(2).broadcast_to([P, SGG, SGD])
            for t in range(TT):
                ins = dve.tensor_reduce(mu[:, t, :], vg[t], AX.X, ALU.add)
            link(ins)
            link(dve.tensor_scalar(V("mu"), V("mu"), 1.0 / SGD, None, ALU.mult))
            for t in range(TT):
                ins = dve.tensor_tensor(vg[t], vg[t], wide(mu, t), ALU.subtract)
            link(ins)
            for t in range(TT):
                ins = dve.tensor_tensor(sq[t], vg[t], vg[t], ALU.mult)
            link(ins)
            for t in range(TT):
                ins = dve.tensor_reduce(ssc[:, t, :], sq[t], AX.X, ALU.add)
            ins.then_inc(S("ln_squares"), 1)
            for h in range(SBH):
                dve.wait_ge(S("after_a"), h + 1)
                s = sa_flat[:, 384 * h:384 * h + 384]
                ins = dve.tensor_tensor(s, s, bank[(3, 4, 5, 6, 7, 0)[h]][:, 0:384], ALU.subtract)
            ins.then_inc(S("expo_ready"), 1)
            dve.wait_ge(S("mbc_done"), 1)
            big = C("bigpast").unsqueeze(1).broadcast_to([P, 2, P])
            for k in range(2):
                mb = bank[3 + 4 * k][:].rearrange("p (h b t) -> p h b t", h=2, b=2)
                dve.tensor_tensor(mw[:, 2 * k:2 * k + 2, 0, :], mb[:, :, 0, :], big, ALU.add)
                dve.tensor_copy(mw[:, 2 * k:2 * k + 2, 1, :], mb[:, :, 1, :])
                ins = dve.tensor_tensor(mw[:, 2 * k:2 * k + 2, 2, :], mb[:, :, 1, :], big, ALU.add)
            ins.then_inc(S("mw_ready"), 1)
            dve.wait_ge(S("cols_done"), 1)
            dve.tensor_copy(V("ccol"), bank[2][:, 0:16]).then_inc(S("ccol_ready"), 1)
            dve.wait_ge(S("ln_rstd"), 1)
            for t in range(TT):
                ins = dve.tensor_tensor(vg[t], vg[t], wide(rsc, t), ALU.mult)
            link(ins)
            for t in range(TT):
                ins = dve.tensor_tensor(z[:, t, Z_VC:Z_GATES], z[:, t, Z_VC:Z_GATES], Q("ln_g"), ALU.mult)
            link(ins)
            for t in range(TT):
                ins = dve.tensor_tensor(z[:, t, Z_VC:Z_GATES], z[:, t, Z_VC:Z_GATES], Q("ln_b"), ALU.add)
            ins.then_inc(S("ln_ready"), 1)
            for h in range(MLH):
                dve.wait_ge(S("scores_b"), h + 1)
                dve.wait_ge(S("decay_ready"), h + 1)
                m = mw[:, h, :, :]
                dve.scalar_tensor_tensor(m, bank[(4, 5, 6, 7)[h]][:, 0:384].rearrange("p (b t) -> p b t", b=3),
                                         MLD ** -0.5, m, ALU.mult, ALU.mult).then_inc(S("s_ready"), 1)
            dve.wait_ge(S("weights_a"), 1)
            dve.tensor_tensor(sa[:, :, 0, :], sa[:, :, 0, :], strict, ALU.mult)
            dve.tensor_tensor(sa[:, :, 2, :], sa[:, :, 2, :], strict, ALU.mult).then_inc(S("a_ready"), 1)
            dve.wait_ge(S("mixed_done"), 1)
            mx = [bank[3][:, 256 * t:256 * t + 256].rearrange("p (g d) -> p g d", g=SGG) for t in range(TT)]
            yc = [xn[:, t, SBW + MLW:D] for t in range(TT)]
            for t in range(TT):
                ins = dve.tensor_tensor(yc[t].rearrange("p (g d) -> p g d", g=SGG), mx[t],
                                        Q("sgu_b").unsqueeze(2).broadcast_to([P, SGG, SGD]), ALU.add)
            link(ins)
            for t in range(TT):
                ins = dve.tensor_tensor(yc[t], yc[t], z[:, t, Z_UC:Z_VC], ALU.mult)
            ins.then_inc(S("yc_ready"), 1)
            dve.wait_ge(S("out_b"), 1)
            dve.wait_ge(S("ccol_ready"), 1)
            den = V("den")
            for t in range(TT):
                ins = dve.scalar_tensor_tensor(den[:, 4 * t:4 * t + 4], bank[4 + t][:, MLW:MLW + MLH], -1.0,
                                               V("ccol")[:, 8 + 4 * t:12 + 4 * t], ALU.mult, ALU.max)
            link(ins)
            for t in range(TT):
                d = den[:, 4 * t:4 * t + 4]
                ins = dve.tensor_tensor(d, bank[4 + t][:, MLW:MLW + MLH], d, ALU.max)
            link(ins)
            link(dve.reciprocal(den, den))
            hb = [xn[:, t, SBW:SBW + MLW].rearrange("p (h d) -> p h d", h=MLH) for t in range(TT)]
            for t in range(TT):
                ins = dve.tensor_tensor(hb[t], bank[4 + t][:, 0:MLW].rearrange("p (h d) -> p h d", h=MLH),
                                        den[:, 4 * t:4 * t + 4].unsqueeze(2).broadcast_to([P, MLH, MLD]), ALU.mult)
            ins.then_inc(S("hb_ready"), 1)
            dve.wait_ge(S("hb_squares"), 1)
            dve.tensor_reduce(V("ssb"), tmp.rearrange("p (g d) -> p g d", d=MLD), AX.X, ALU.add)\
               .then_inc(S("hb_sums"), 1)
            dve.wait_ge(S("hb_ready"), 1)
            for t in range(TT):
                ins = dve.tensor_tensor(xn[:, t, SBW:SBW + MLW], xn[:, t, SBW:SBW + MLW], z[:, t, Z_OB:Z_UC], ALU.mult)
            link(ins)
            dve.wait_ge(S("hb_rstd"), 1)
            for t in range(TT):
                ins = dve.tensor_tensor(hb[t], hb[t],
                                        V("rsb")[:, 4 * t:4 * t + 4].unsqueeze(2).broadcast_to([P, MLH, MLD]), ALU.mult)
            ins.then_inc(S("xn0_ready"), 1)
            turn_dve(1)
            add_chunks(U_WOUT, C_WOUT)
            norm_dve(1)
            turn_dve(2)
            dve.wait_ge(S("router_done"), 1)
            lg = V("lg").rearrange("p (a n) -> p a n", a=TT)
            two = lambda v: v.rearrange("p (a n) -> p a n", a=TT)
            over = lambda v, n: v.unsqueeze(2).broadcast_to([P, TT, n])
            same = lambda v, n: v.unsqueeze(1).broadcast_to([P, TT, n])
            NR = NG + NE
            link(dve.tensor_tensor(lg, bank[0][:, 0:2 * NR].rearrange("p (a n) -> p a n", a=TT),
                                   same(Q("router_b"), NR), ALU.add))
            gmax, eqg, ohg, idx = V("gmax"), two(V("eqg")), two(V("ohg")), V("idx")

            def one_hot(oh, scores, top, iota, n, cand):
                link(dve.tensor_reduce(top, scores, AX.X, ALU.max))
                link(dve.tensor_tensor(cand, scores, over(top, n), ALU.is_ge))
                link(dve.scalar_tensor_tensor(cand, cand, -64.0, same(iota, n), ALU.mult, ALU.add))
                link(dve.tensor_reduce(idx, cand, AX.X, ALU.min))
                link(dve.tensor_tensor(oh, cand, over(idx, n), ALU.is_equal))

            one_hot(ohg, lg[:, :, 0:NG], gmax, C("iota4"), NG, eqg)
            eg = two(V("eg"))
            dve.tensor_tensor(eg, lg[:, :, 0:NG], over(gmax, NG), ALU.subtract).then_inc(S("gdiff_ready"), 1)
            link(dve.tensor_scalar(V("pen"), V("ohg"), BIG, -BIG, ALU.mult, ALU.add))
            em, em4 = two(V("em")), V("em").rearrange("p (a g e) -> p a g e", a=TT, g=NG)
            pen = V("pen").rearrange("p (a g) -> p a g", a=TT)
            for t in range(TT):
                ins = dve.tensor_tensor(em4[:, t], lg[:, t, NG:NR].rearrange("p (g e) -> p g e", g=NG),
                                        ohg[:, t, :].unsqueeze(2).broadcast_to([P, NG, EPG]), ALU.mult)
            link(ins)
            for t in range(TT):
                ins = dve.tensor_tensor(em4[:, t], em4[:, t],
                                        pen[:, t, :].unsqueeze(2).broadcast_to([P, NG, EPG]), ALU.add)
            link(ins)
            oh1, oh2, cand = two(V("oh1")), two(V("oh2")), two(V("cand"))
            v1, v2, dv = V("v1"), V("v2"), V("dv")
            one_hot(oh1, em, v1, C("iota32"), NE, cand)
            link(dve.scalar_tensor_tensor(V("em"), V("oh1"), -2.0 * BIG, V("em"), ALU.mult, ALU.add))
            one_hot(oh2, em, v2, C("iota32"), NE, cand)
            dve.tensor_tensor(dv, v2, v1, ALU.subtract).then_inc(S("vdiff_ready"), 1)
            dve.wait_ge(S("gexp_ready"), 1)
            gw, p1, p2 = V("gw"), V("p1"), V("p2")
            link(dve.tensor_reduce(gw, eg, AX.X, ALU.add))
            dve.wait_ge(S("vexp_ready"), 1)
            link(dve.scalar_tensor_tensor(p1, dv, 1.0, gw, ALU.add, ALU.mult))
            link(dve.reciprocal(p1, p1))
            link(dve.tensor_tensor(p2, p1, dv, ALU.mult))
            dve.tensor_tensor(oh1, oh1, over(p1, NE), ALU.mult)
            link(dve.tensor_tensor(oh2, oh2, over(p2, NE), ALU.mult))
            dve.tensor_tensor(oh1, oh1, oh2, ALU.add).then_inc(S("wt_ready"), 1)
            dve.wait_ge(S("wthi_ready"), 1)
            dve.tensor_tensor(wtlo[:], bank[0][0:NE, 256:512], wthi[:].bitcast(F32), ALU.subtract)\
               .then_inc(S("wtlo_ready"), 1)
            for b in range(1, NE // 2, 2):
                dve.wait_ge(S("wbc_done"), b + 1)
                dve.tensor_copy(wbc[:, 2 * b:2 * b + 2, :], bank[4 + b % 4][:].rearrange("p (e t) -> p e t", e=2))\
                   .then_inc(S("wbc_dve"), 1)

            def moe_dve(e, off, e0):
                b = e0 % 2
                n = U_MOE + 3 * e0 - 1
                if off is None:
                    split_to(n + 4)
                else:
                    split((n + 3, off))
                    split((n + 4, off))
                dve.wait_ge(S("weighted"), 1 + e)
                if e0 >= 2:
                    dve.wait_ge(S("h_ready"), D_MOE - 1 + e)
                dve.tensor_tensor(hv[:, b, :], sgl[:, b, :], bank[2 * b + 1][:], ALU.mult).then_inc(S("g_free"), 1)
                if off is None:
                    split_to(n + 5)
                else:
                    split((n + 5, off))
                dve.wait_ge(S("hhi_ready"), D_MOE + 1 + e)
                dve.tensor_tensor(hlo[:, b, :, :], hv[:, b, :].rearrange("p (f t) -> p f t", f=2),
                                  hhi[:, b, :, :].bitcast(F32), ALU.subtract).then_inc(S("h_ready"), 1)

            moe_dve(0, None, 0)
            moe_dve(1, None, 1)
            with dve.Fori(0, (NE - 2) // 2) as j:
                for b in range(2):
                    moe_dve(2 * j + (2 + b), 2 * j, 2 + b)
            done[0] = U_MOE + 3 * NE + 2
            add_down(U_MOE + 3 * NE)
            norm_dve(2)
            turn_dve(3)
            split_to(U_PLEP + 2)
            for c in range(2):
                dve.wait_ge(*((S("proj_half"), 1) if c == 0 else (S("unit_used"), U_PLEP + 1)))
                dve.wait_ge(S("act_freed"), sum(BY_ACT[:C_PLEG + c + 1]))
                for t in range(TT):
                    ins = dve.tensor_tensor(gpr[:, t, :], gsb[:, t, 512 * c:512 * c + 512],
                                            bank[2 * ((C_PLEP + c) % 2) + t][:], ALU.mult)
                ins.then_inc(S("dve_freed"), 1)
                dve.wait_ge(S("dve_freed"), sum(BY_DVE[:C_PLEP + c + 1]))
                for t in range(TT):
                    r = xres[:, t, 512 * c:512 * c + 512]
                    ins = dve.tensor_tensor(r, gpr[:, t, :], r, ALU.add)
                if c == 0:
                    link(ins)
            ins.then_inc(S("residual_ready"), 1)
            dve.wait_ge(S("residual_ready"), R_PLE)
            split_to(U_SCIN + 1)
            dve.wait_ge(S("rstd_ready"), 4)
            dve.wait_ge(S("final1_loaded"), 16)
            for t in range(TT):
                ins = dve.scalar_tensor_tensor(xres[:, t, :], xres[:, t, :], rstd[:, t:t + 1], final_g[:],
                                               ALU.mult, ALU.mult)
            ins.then_inc(S("residual_ready"), 1)
            dve.wait_ge(S("residual_ready"), R_FINAL1)
            norm_dve(4)
            link(dve.memset(cvp[:, :, 0:2], 0.0))
            turn_dve(4)
            for i in range(6):
                split_to(U_SCIN + 2 * i + 3)
                g = G_SC + i
                dve.wait_ge(S("unit_used"), U_SCIN + 2 * i + 2)
                if i < 4:
                    dve.wait_ge(S("c_ready"), i + 1)
                    dve.tensor_tensor(cvp[:, 2 * i:2 * i + 2, 2:2 + T],
                                      csb[:, i % 2, :].rearrange("p (j t) -> p j t", j=2),
                                      bank[2 * (g % 2) + 1][:].rearrange("p (j t) -> p j t", j=2), ALU.mult)\
                       .then_inc(S("g_free"), 1)
                    dve.wait_ge(S("g_free"), g + 1)
                    dve.wait_ge(S("sc_begun"), i + 1)
                    for k in range(1, -1, -1):
                        for f in range(2 * i, 2 * i + 2):
                            ins = dve.scalar_tensor_tensor(scy[:, f, :], cvp[:, f, k:k + T], sc_conv[:, k, f:f + 1],
                                                           scy[:, f, :], ALU.mult, ALU.add)
                        link(ins)
                else:
                    f = 4 * (i - 4)
                    for k in range(2):
                        y = scy[:, f + 2 * k:f + 2 * k + 2, :]
                        dve.tensor_tensor(y, y, bank[2 * (g % 2) + k][:].rearrange("p (j t) -> p j t", j=2), ALU.mult)\
                           .then_inc(S("sc_product") if k == 0 else S("g_free"), 1)
            for f in range(4):
                dve.wait_ge(S("sc_high"), f + 1)
                dve.tensor_tensor(xlo[:, 2 * f:2 * f + 2, :], scy[:, 2 * f:2 * f + 2, :],
                                  xhi[:, 2 * f:2 * f + 2, :].bitcast(F32), ALU.subtract).then_inc(S("sc_ready"), 1)
            add_chunks(U_SCOUT, C_SCOUT)

            def ffn_dve(layer, e, off, e0):
                g0, d0, u0 = (G_FFN0, D_FFN0, U_FFN0) if layer == 0 else (G_FFN1, D_FFN1, U_FFN1)
                b, gb = e0 % 2, (g0 + e0) % 2
                n = u0 + 3 * e0 - 1

                def ahead(k):
                    if off is None:
                        split_to(n + k)
                    elif n + k < UNITS:
                        split((n + k, off))
                ahead(3)
                dve.wait_ge(S("ffn_begun"), layer * FE + 1 + e)
                for k in range(1, -1, -1):
                    for f in range(4):
                        src = bank[2 * gb + f // 2][:, (f % 2) * T:(f % 2 + 1) * T]
                        a = facc[:, b, f, 2 - k:T]
                        ins = dve.scalar_tensor_tensor(a, src[:, 0:T - 2 + k], cwn[:, b, 4 * k + f:4 * k + f + 1], a,
                                                       ALU.mult, ALU.add)
                    if k == 1:
                        link(ins)
                ins.then_inc(S("g_free"), 1)
                ahead(4)
                dve.wait_ge(S("g_free"), g0 + 1 + e)
                dve.wait_ge(S("silu_ready"), NE + layer * FE + 1 + e)
                dve.tensor_tensor(facc[:, b, 2:4, :], facc[:, b, 0:2, :], facc[:, b, 2:4, :], ALU.mult)\
                   .then_inc(S("hv_ready"), 1)
                ahead(5)
                dve.wait_ge(S("hhi_ready"), d0 + 1 + e)
                dve.tensor_tensor(hlo[:, b, :, :], facc[:, b, 2:4, :], hhi[:, b, :, :].bitcast(F32), ALU.subtract)\
                   .then_inc(S("h_ready"), 1)

            def ffn(layer):
                ffn_dve(layer, 0, None, 0)
                ffn_dve(layer, 1, None, 1)
                u0 = U_FFN0 if layer == 0 else U_FFN1
                with dve.Fori(0, (FE - 3) // 2) as j:
                    chain.enter(j, 2)
                    for b in range(2):
                        ffn_dve(layer, 2 * j + (2 + b), 2 * j, 2 + b)
                    chain.leave(2, (FE - 3) // 2)
                done[0] = u0 + 3 * (FE - 1) + 2
                ffn_dve(layer, FE - 1, None, FE - 1)

            norm_dve(5)
            turn_dve(5)
            ffn(0)
            add_down(U_FFN0 + 3 * FE)
            norm_dve(6)
            turn_dve(6)
            cos = C("cos").rearrange("p (a n) -> p a n", a=TT)
            sin = C("sin").rearrange("p (a n) -> p a n", a=TT)
            rot = rp.rearrange("p k (h n) -> p k h n", h=8)
            for c in range(4):
                split_to(U_QKV + 2 * c + 3)
                dve.wait_ge(S("unit_used"), CHUNK_END[C_QKV + c])
                for t in range(TT):
                    src = bank[2 * ((C_QKV + c) % 2) + t][:].rearrange("p (h n) -> p h n", h=8)
                    dst = qkv[:, t, 512 * c:512 * c + 512].rearrange("p (h n) -> p h n", h=8)
                    cb = cos[:, t, :].unsqueeze(1).broadcast_to([P, 8, HALF])
                    sb_ = sin[:, t, :].unsqueeze(1).broadcast_to([P, 8, HALF])
                    x1, x2 = src[:, :, 0:HALF], src[:, :, HALF:HD]
                    dve.tensor_tensor(rot[:, 0], x1, cb, ALU.mult)
                    dve.tensor_tensor(rot[:, 1], x2, sb_, ALU.mult)
                    dve.tensor_tensor(rot[:, 2], x2, cb, ALU.mult)
                    link(dve.tensor_tensor(rot[:, 3], x1, sb_, ALU.mult))
                    dve.tensor_tensor(dst[:, :, 0:HALF], rot[:, 0], rot[:, 1], ALU.subtract)
                    ins = dve.tensor_tensor(dst[:, :, HALF:HD], rot[:, 2], rot[:, 3], ALU.add)
                    if t == 0:
                        link(ins)
                ins.then_inc(S("dve_freed"), 1)
                dve.wait_ge(S("dve_freed"), sum(BY_DVE[:C_QKV + c + 1]))
            split_to(U_WO + 2)
            for b in range(1, 8, 2):
                dve.wait_ge(S("qk_turned"), b + 1)
                dve.tensor_copy(qkt_flat[:, 512 * b:512 * b + 512], bank[b][:]).then_inc(S("qkt_dve"), 1)

            def attend_norm(h):
                b = h % 2
                dve.wait_ge(S("exp_done"), h + 1)
                link(dve.reciprocal(V("rl")[:, 2 * b:2 * b + 2], V("l")[:, 2 * b:2 * b + 2]))
                dve.tensor_scalar(ap_[:, b, 0:128], ap_[:, b, 0:128], V("rl")[:, 2 * b:2 * b + 1], None, ALU.mult)
                dve.tensor_scalar(ap_[:, b, 128:384], ap_[:, b, 128:384], V("rl")[:, 2 * b + 1:2 * b + 2], None,
                                  ALU.mult).then_inc(S("p_ready"), 1)

            for h in range(NH):
                b = h % 2
                dve.wait_ge(S("scores_done"), h + 1)
                dve.tensor_tensor(bank[b][:, 0:128], bank[b][:, 0:128], C("causal"), ALU.add)
                link(dve.tensor_tensor(bank[b][:, 256:384], bank[b][:, 256:384], C("causal"), ALU.add))
                dve.tensor_reduce(V("m")[:, 2 * b:2 * b + 1], bank[b][:, 0:128], AX.X, ALU.max)
                link(dve.tensor_reduce(V("m")[:, 2 * b + 1:2 * b + 2], bank[b][:, 128:384], AX.X, ALU.max))
                dve.tensor_scalar(V("nm")[:, 2 * b:2 * b + 2], V("m")[:, 2 * b:2 * b + 2], -(HD ** -0.5), None,
                                  ALU.mult).then_inc(S("negmax_ready"), 1)
                if h >= 1:
                    attend_norm(h - 1)
            attend_norm(NH - 1)
            for b in range(4):
                dve.wait_ge(S("o_high"), b + 1)
                dve.tensor_tensor(xlo[:, 2 * b:2 * b + 2, :], bank[4 + b][:].rearrange("p (j t) -> p j t", j=2),
                                  xhi[:, 2 * b:2 * b + 2, :].bitcast(F32), ALU.subtract).then_inc(S("o_ready"), 1)
            add_chunks(U_WO, C_WO)
            norm_dve(7)
            turn_dve(7)
            ffn(1)
            add_down(UNITS)
            dve.wait_ge(S("residual_ready"), R_FFN1)
            dve.wait_ge(S("rstd_ready"), 9)
            dve.wait_ge(S("final2_loaded"), 16)
            for t in range(TT):
                ins = dve.scalar_tensor_tensor(xn[:, t, :], xres[:, t, :], rstd[:, t:t + 1], final_g[:],
                                               ALU.mult, ALU.mult)
            ins.then_inc(S("y_ready"), 1)

        @block.tensor
        def _(pe):
            def wait_unit(n):
                unit0, off = n if isinstance(n, tuple) else (n, 0)
                pe.wait_ge(S("low_done"), (off if isinstance(off, int) else off * RING) + unit0 + 1)
                return unit0 % RING

            def mm3(o, ah, al, bh, bl, start, stop=False):
                pe.matmul(o, ah, bh, start=start, stop=False, skip_group_check=True)
                pe.matmul(o, ah, bl, start=False, stop=False, skip_group_check=True)
                return pe.matmul(o, al, bh, start=False, stop=stop, skip_group_check=True)

            def turn(q):
                pe.wait_ge(S("xn0_ready"), q + 1)
                pe.wait_ge(S("xn1_ready"), q + 1)
                for k in range(KD):
                    for t in range(TT):
                        ins = pe.transpose(bank[k // 2][:, (k % 2) * T + t * P:(k % 2) * T + t * P + P],
                                           xn[:, t, P * k:P * k + P], ident)
                    if k % 2:
                        ins.then_inc(S("turned"), 1)
                pe.wait_ge(S("xt_ready"), 4 * (q + 1))

            def dense(g, u0, width=512):
                if g >= 2:
                    if sum(BY_ACT[:g - 1]):
                        pe.wait_ge(S("act_freed"), sum(BY_ACT[:g - 1]))
                    pe.wait_ge(S("dve_freed"), sum(BY_DVE[:g - 1]))
                for u in range(2):
                    s = wait_unit(u0 + u)
                    for k in range(4):
                        kk = 4 * u + k
                        for t in range(TT):
                            w = slice(512 * k, 512 * k + 512)
                            ins = mm3(bank[2 * (g % 2) + t][:], xhi[:, kk, P * t:P * t + P], xlo[:, kk, P * t:P * t + P],
                                      whi[:, s, w], wlo[:, s, w], start=kk == 0, stop=kk == 7)
                    ins.then_inc(S("unit_used"), 1)

            pe.wait_ge(S("table_loaded"), 16)
            pe.wait_ge(S("params_loaded"), 16)
            turn(0)
            for c in range(6):
                dense(C_WIN + c, U_WIN + 2 * c)
            pe.wait_ge(S("act_freed"), 5)
            pe.wait_ge(S("dve_freed"), 5)
            s = wait_unit(12)
            for k in range(KD):
                for t in range(TT):
                    w = slice(TAIL * k, TAIL * k + TAIL)
                    ins = mm3(bank[t][:, 0:TAIL], xhi[:, k, P * t:P * t + P], xlo[:, k, P * t:P * t + P],
                              whi[:, s, w], wlo[:, s, w], start=k == 0, stop=k == 7)
            ins.then_inc(S("unit_used"), 1)
            pe.wait_ge(S("act_freed"), 7)
            pe.wait_ge(S("dve_freed"), 7)
            for j in range(6):
                for t in range(TT):
                    at = j * T + t * P
                    ins = pe.transpose(bank[4 + at // 512][:, at % 512:at % 512 + P], z[:, t, P * j:P * j + P], ident)
                if j % 2:
                    ins.then_inc(S("turned_a"), 1)
            for j in range(8):
                for t in range(TT):
                    ins = pe.transpose(bank[(7, 0, 1, 2)[j // 2]][0:MLD, (j % 2) * T + t * P:(j % 2) * T + t * P + P],
                                       z[:, t, Z_QB + MLD * j:Z_QB + MLD * j + MLD], ident)
                if j % 2:
                    ins.then_inc(S("turned_b"), 1)
            pe.wait_ge(S("qka_act"), 2)
            pe.wait_ge(S("qka_dve"), 1)
            for h in range(SBH):
                p0 = 64 * (h % 2)
                q_, k_ = qka[p0:p0 + 64, h // 2, :], qka[p0:p0 + 64, 3 + h // 2, :]
                if h == 4:
                    pe.wait_ge(S("cvb_act"), 2)
                b = bank[(3, 4, 5, 6, 7, 0)[h]]
                pe.matmul(b[:, 0:256], k_[:, 0:P], q_, start=True, stop=True, skip_group_check=True)
                pe.matmul(b[:, 256:384], k_[:, P:T], q_[:, P:T], start=True, stop=True, skip_group_check=True)\
                  .then_inc(S("scores_a"), 1)
            pe.wait_ge(S("logf_ready"), 1)
            pe.wait_ge(S("cvb_dve"), 2)
            lf = V("lf").rearrange("p (a n) -> p a n", a=TT)
            gt = V("gt").rearrange("p (a n) -> p a n", a=TT)
            upto, ones, later = C("upto"), C("ones"), C("later")
            r = bank[1][0:MLH, :]
            pe.matmul(r[:, 0:P], lf[:, 0, :], upto, start=True, stop=True, skip_group_check=True)
            pe.matmul(r[:, P:T], lf[:, 0, :], ones, start=True, stop=False, skip_group_check=True)
            pe.matmul(r[:, P:T], lf[:, 1, :], upto, start=False, stop=True, skip_group_check=True)
            pe.transpose(r[:, T:T + P], gt[:, 0, 0:4], ident)
            pe.transpose(r[:, T + P:2 * T], gt[:, 1, 0:4], ident).then_inc(S("brow_done"), 1)
            pe.wait_ge(S("l_ready"), 1)
            for h in range(SBH):
                b = bank[(3, 4, 5, 6, 7, 0)[h]]
                l = t1_flat[:, 384 * h:384 * h + 384]
                pe.matmul(b[:, 0:384], later, l, start=True, stop=False, skip_group_check=True)
                pe.matmul(b[:, 128:256], ones, l[:, 256:384], start=False, stop=True, skip_group_check=True)\
                  .then_inc(S("after_a"), 1)
            pe.wait_ge(S("mrow_ready"), 1)
            pe.wait_ge(S("enrow_ready"), 1)
            for t in range(TT):
                pe.transpose(bank[2][:, 4 * t:4 * t + 4], rows[:, 1, P * t:P * t + P], ident[0:4, 0:4])
                ins = pe.transpose(bank[2][:, 8 + 4 * t:12 + 4 * t], rows[:, 4, P * t:P * t + P], ident[0:4, 0:4])
            ins.then_inc(S("cols_done"), 1)
            pe.wait_ge(S("expo_ready"), 1)
            for h in range(MLH):
                ins = pe.matmul(bank[3 + 4 * (h // 2)][:, (h % 2) * T:(h % 2 + 1) * T],
                                ident[0:4, h:h + 1].broadcast_to([4, P]), rows[:, 2, :], start=True, stop=True,
                                skip_group_check=True)
            ins.then_inc(S("mbc_done"), 1)
            pe.wait_ge(S("qkb_ready"), 1)
            pe.wait_ge(S("mw_ready"), 1)
            for h in range(MLH):
                b = bank[(4, 5, 6, 7)[h]]
                q_, k_ = qkb[:, h, :], qkb[:, 4 + h, :]
                pe.matmul(b[:, 0:256], k_[:, 0:P], q_, start=True, stop=True, skip_group_check=True)
                pe.matmul(b[:, 256:384], k_[:, P:T], q_[:, P:T], start=True, stop=True, skip_group_check=True)\
                  .then_inc(S("scores_b"), 1)
            pe.wait_ge(S("ln_ready"), 1)
            pe.wait_ge(S("sgu_masked"), 1)
            for t in range(TT):
                for g in range(SGG):
                    ins = pe.matmul(bank[3][:, 256 * t + 64 * g:256 * t + 64 * g + 64], sgu_w[:, g, :],
                                    z[:, t, Z_VC + 64 * g:Z_VC + 64 * g + 64], start=True, stop=True,
                                    skip_group_check=True)
            ins.then_inc(S("mixed_done"), 1)
            pe.wait_ge(S("a_ready"), 1)
            pe.wait_ge(S("ccol_ready"), 1)
            for h in range(SBH):
                v = [z[:, t, 2 * SBW + 64 * h:2 * SBW + 64 * h + 64] for t in range(TT)]
                o = [bank[1 + t][:, 64 * h:64 * h + 64] for t in range(TT)]
                pe.matmul(o[0], sa[:, h, 0, :], v[0], start=True, stop=True, skip_group_check=True)
                pe.matmul(o[1], sa[:, h, 1, :], v[0], start=True, stop=False, skip_group_check=True)
                ins = pe.matmul(o[1], sa[:, h, 2, :], v[1], start=False, stop=True, skip_group_check=True)
            ins.then_inc(S("out_a"), 1)
            pe.wait_ge(S("s_ready"), 4)
            for h in range(MLH):
                v = [z[:, t, Z_VB + MLD * h:Z_VB + MLD * h + MLD] for t in range(TT)]
                for vv, a, w in ((v, MLD * h, MLD), ([ones[:, 0:1]] * 2, MLW + h, 1)):
                    pe.matmul(bank[4][:, a:a + w], mw[:, h, 0, :], vv[0], start=True, stop=True, skip_group_check=True)
                    pe.matmul(bank[5][:, a:a + w], mw[:, h, 1, :], vv[0], start=True, stop=False, skip_group_check=True)
                    ins = pe.matmul(bank[5][:, a:a + w], mw[:, h, 2, :], vv[1], start=False, stop=True,
                                    skip_group_check=True)
            ins.then_inc(S("out_b"), 1)
            turn(1)
            for c in range(2):
                dense(C_WOUT + c, U_WOUT + 2 * c)
            turn(2)
            pe.wait_ge(S("setup_low"), 1)
            NR = NG + NE
            for t in range(TT):
                for k in range(KD):
                    ins = mm3(bank[0][:, NR * t:NR * t + NR], xhi[:, k, P * t:P * t + P], xlo[:, k, P * t:P * t + P],
                              rhi[:, k, :], rlo[:, k, :], start=k == 0, stop=k == 7)
            ins.then_inc(S("router_done"), 1)
            pe.wait_ge(S("wt_ready"), 1)
            oh1 = V("oh1").rearrange("p (a n) -> p a n", a=TT)
            for t in range(TT):
                ins = pe.transpose(bank[0][0:NE, 256 + P * t:256 + P * t + P], oh1[:, t, :], ident)
            ins.then_inc(S("wt_turned"), 1)
            pe.wait_ge(S("wtlo_ready"), 1)
            for b in range(NE // 2):
                if b >= 4:
                    pe.wait_ge(S("wbc_act") if b % 2 == 0 else S("wbc_dve"), b // 2 - 1)
                for i in range(2):
                    o = bank[4 + b % 4][:, i * T:(i + 1) * T]
                    sel = identr[:, 2 * b + i:2 * b + i + 1].broadcast_to([NE, P])
                    pe.matmul(o, sel, wthi[:], start=True, stop=False, skip_group_check=True)
                    ins = pe.matmul(o, sel, wtlo[:], start=False, stop=True, skip_group_check=True)
                ins.then_inc(S("wbc_done"), 1)
            pe.wait_ge(S("wbc_act"), NE // 4)
            pe.wait_ge(S("wbc_dve"), NE // 4)

            def group(g0, u):
                unit0, off = u if isinstance(u, tuple) else (u, 0)
                for i in range(2):
                    s = wait_unit((unit0 + i, off))
                    for k in range(4):
                        kk = 4 * i + k
                        for f in range(4):
                            o = bank[2 * (g0 % 2) + f // 2][:, (f % 2) * T:(f % 2 + 1) * T]
                            w = slice(512 * k + P * f, 512 * k + P * f + P)
                            first = kk == 0 and f % 2 == 0
                            pe.matmul(o, whi[:, s, w], xhi[:, kk, :], start=first, stop=False, skip_group_check=True)
                            pe.matmul(o, whi[:, s, w], xlo[:, kk, :], start=False, stop=False, skip_group_check=True)
                            ins = pe.matmul(o, wlo[:, s, w], xhi[:, kk, :], start=False, stop=kk == 7,
                                            skip_group_check=True)
                    ins.then_inc(S("unit_used"), 1)

            def down(b, u, first):
                unit0, off = u if isinstance(u, tuple) else (u, 0)
                s = wait_unit(u)
                for t in range(TT):
                    for c in range(2):
                        for f in range(2):
                            w = slice(D * f + 512 * c, D * f + 512 * c + 512)
                            ins = mm3(bank[4 + 2 * t + c][:], hhi[:, b, f, P * t:P * t + P], hlo[:, b, f, P * t:P * t + P],
                                      whi[:, s, w], wlo[:, s, w], start=first and f == 0)
                ins.then_inc(S("unit_used"), 1)

            def expert_step(g0, d0, u0, e, e0, off):
                n = u0 + 2 + 3 * e0
                if not (g0 == 0 and e0 + 1 < 2):
                    pe.wait_ge(S("g_free"), g0 + e)
                group(g0 + e0 + 1, (n, off))
                pe.wait_ge(S("h_ready"), d0 + 1 + e)
                down(e0 % 2, (n + 2, off), first=e0 == 0)

            def experts(g0, d0, u0, count):
                if g0:
                    pe.wait_ge(S("g_free"), g0 - 1)
                group(g0, u0)
                expert_step(g0, d0, u0, 0, 0, 0)
                pairs = (count - 2) // 2
                with pe.Fori(0, pairs) as j:
                    for b in range(2):
                        expert_step(g0, d0, u0, 2 * j + (1 + b), 1 + b, 2 * j)
                for e in range(1 + 2 * pairs, count - 1):
                    expert_step(g0, d0, u0, e, e, 0)
                pe.wait_ge(S("h_ready"), d0 + count)
                down((count - 1) % 2, u0 + 3 * count - 1, first=False)

            experts(G_MOE, D_MOE, U_MOE, NE)
            turn(3)
            for c in range(2):
                dense(C_PLEG + c, U_PLEG + 2 * c)
            s = wait_unit(U_PLEP)
            for c in range(2):
                g = C_PLEP + c
                pe.wait_ge(S("act_freed"), sum(BY_ACT[:g - 1]))
                for t in range(TT):
                    for k in range(2):
                        w = slice(D * k + 512 * c, D * k + 512 * c + 512)
                        ins = mm3(bank[2 * (g % 2) + t][:], phi[:, k, P * t:P * t + P], plo[:, k, P * t:P * t + P],
                                  whi[:, s, w], wlo[:, s, w], start=k == 0, stop=k == 1)
                ins.then_inc(S("proj_half") if c == 0 else S("unit_used"), 1)
            turn(4)
            for i in range(6):
                pe.wait_ge(S("g_free"), G_SC + i - 1)
                group(G_SC + i, U_SCIN + 2 * i)
            pe.wait_ge(S("sc_ready"), 4)
            for c in range(2):
                dense(C_SCOUT + c, U_SCOUT + 2 * c)
            turn(5)
            experts(G_FFN0, D_FFN0, U_FFN0, FE)
            turn(6)
            for c in range(6):
                dense(C_QKV + c, U_QKV + 2 * c)
            pe.wait_ge(S("dve_freed"), sum(BY_DVE[:C_QKV + 6]))
            pe.wait_ge(S("act_freed"), sum(BY_ACT[:C_QKV + 6]))
            for j in range(16):
                for t in range(TT):
                    ins = pe.transpose(bank[j // 2][:, (j % 2) * T + t * P:(j % 2) * T + t * P + P],
                                       qkv[:, t, P * j:P * j + P], ident)
                if j % 2:
                    ins.then_inc(S("qk_turned"), 1)
            pe.wait_ge(S("qkt_act"), 4)
            pe.wait_ge(S("qkt_dve"), 4)

            def scores(h):
                b, p0 = h % 2, 64 * (h % 2)
                q_, k_ = qkt[p0:p0 + 64, h // 2, :], qkt[p0:p0 + 64, 8 + h // 2, :]
                if h >= 2:
                    pe.wait_ge(S("exp_done"), h - 1)
                pe.matmul(bank[b][:, 0:128], q_[:, 0:P], k_[:, 0:P], start=True, stop=True, skip_group_check=True)
                pe.matmul(bank[b][:, 128:384], q_[:, P:T], k_, start=True, stop=True, skip_group_check=True)\
                  .then_inc(S("scores_done"), 1)

            def turn_p(h):
                b = h % 2
                pe.wait_ge(S("p_ready"), h + 1)
                if h >= 2:
                    pe.wait_ge(S("pt_ready"), h - 1)
                for k in range(3):
                    ins = pe.transpose(bank[2 + b][:, P * k:P * k + P], ap_[:, b, P * k:P * k + P], ident)
                ins.then_inc(S("p_turned"), 1)

            def values(h):
                b, j = h % 2, h // 2
                pe.wait_ge(S("pt_ready"), h + 1)
                v = [qkv[:, t, 2 * D + HD * h:2 * D + HD * h + HD] for t in range(TT)]
                o = bank[4 + j // 2][64 * (h % 2):64 * (h % 2) + 64, (j % 2) * T:(j % 2 + 1) * T]
                pe.matmul(o, v[0], apt[:, b, 0:256], start=True, stop=False, skip_group_check=True)
                pe.matmul(o[:, P:T], v[1], apt[:, b, 256:384], start=False, stop=True, skip_group_check=True)\
                  .then_inc(S("pv_done"), 1)

            scores(0)
            scores(1)
            for h in range(NH):
                turn_p(h)
                if h + 2 < NH:
                    scores(h + 2)
                values(h)
            pe.wait_ge(S("o_ready"), 4)
            for c in range(2):
                dense(C_WO + c, U_WO + 2 * c)
            turn(7)
            experts(G_FFN1, D_FFN1, U_FFN1, FE)


def constants():
    t = np.zeros((P, CONST_W), np.float32)

    def put(name, v):
        a, b = CONST[name]
        t[:, a:b] = np.asarray(v, np.float32).reshape(-1, b - a)

    i, j = np.arange(P)[:, None], np.arange(P)[None, :]
    put("ident", i == j)
    put("later", i > j)
    put("ones", np.ones((P, P)))
    put("upto", i <= j)
    put("strict", i < j)
    put("bigpast", np.where(i > j, BIG, 0.0))
    put("causal", np.where(j > i, -BIG, 0.0))
    inv = np.float32(10000.0) ** (-np.arange(HALF, dtype=np.float32) / np.float32(HALF))
    ang = np.arange(T, dtype=np.float32)[:, None] * inv.astype(np.float32)[None, :]
    for name, f in (("cos", np.cos), ("sin", np.sin)):
        put(name, f(ang).reshape(TT, P, HALF).transpose(1, 0, 2).reshape(P, -1))
    put("iota4", np.broadcast_to(np.arange(NG), (P, NG)))
    put("iota32", np.broadcast_to(np.arange(NE), (P, NE)))
    put("neghalf", np.full((P, 8), -0.5))
    return t


def rows_units(w, cols=512):
    k, n = w.shape
    per = UNIT // cols
    v = w.reshape(k // P // per, per, P, n // cols, cols)
    return v.transpose(3, 0, 2, 1, 4).reshape(-1, P, UNIT)


def expert_units(pairs, downs):
    e = pairs.shape[0]
    g = pairs.reshape(e, 2, 4, P, 512).transpose(0, 1, 3, 2, 4).reshape(e, 2, P, UNIT)
    d = downs.reshape(e, 2, P, D).transpose(0, 2, 1, 3).reshape(e, 1, P, UNIT)
    parts = [g[0]]
    for n in range(e - 1):
        parts += [g[n + 1], d[n]]
    parts.append(d[e - 1])
    return np.concatenate(parts)


def kernel(x, p, norm1_g, w_in, conv_w, conv_b, igate_b, fgate_b, mnorm_g, sb_out_g, sgu_ln_g, sgu_ln_b, sgu_w,
           sgu_b, sgu_out_g, w_out, norm2_g, router_gw, router_gb, router_ew, router_eb, w_gate, w_up, w_down,
           ple_norm_g, ple_gate_w, ple_proj_w, final_g, mix_norm_2, sc_w_in_2, sc_w_conv_2, sc_w_out_2, moba_w_qkv_2,
           moba_w_o_2, ffn_norm_2, ffn_w_up_2, ffn_w_conv_2, ffn_w_down_2, final_norm_2):
    import concourse.bacc as _bacc
    from concourse.bass_utils import run_bass_kernel_spmd as _run

    w = w_in[0]
    g0 = 3 * SBW + 4 * MLW
    w = np.concatenate([w[:, :g0], w[:, g0 + GATES:], w[:, g0:g0 + GATES]], axis=1)
    tail = w[:, 6 * 512:].reshape(KD, P, TAIL).transpose(1, 0, 2).reshape(P, KD * TAIL)
    tail = np.concatenate([tail, np.zeros((P, UNIT - KD * TAIL), w.dtype)], axis=1)[None]

    sc = sc_w_in_2[0]
    b_, c_, v_ = sc[:, :D], sc[:, D:2 * D], sc[:, 2 * D:]
    sc_cols = [np.concatenate([c_[:, 256 * i:256 * i + 256], v_[:, 256 * i:256 * i + 256]], axis=1) for i in range(4)]
    sc_cols = np.concatenate(sc_cols + [b_], axis=1)

    def ffn_units(layer):
        up = ffn_w_up_2[layer]
        pairs = np.concatenate([up[:, :FF].reshape(D, FE, 256), up[:, FF:].reshape(D, FE, 256)], axis=2)
        return expert_units(pairs.transpose(1, 0, 2), ffn_w_down_2[layer].reshape(FE, 256, D))

    stream = np.concatenate([
        rows_units(w[:, :6 * 512]), tail, rows_units(w_out[0]),
        expert_units(np.concatenate([w_gate[0], w_up[0]], axis=2), w_down[0]),
        rows_units(ple_gate_w[0]), ple_proj_w[0].reshape(2, P, D).transpose(1, 0, 2).reshape(1, P, UNIT),
        rows_units(sc_cols), rows_units(sc_w_out_2[0]), ffn_units(0),
        rows_units(moba_w_qkv_2[0]), rows_units(moba_w_o_2[0]), ffn_units(1)])

    prm = np.zeros((P, PARAM_W), np.float32)

    def put(name, v, rows=P):
        a, b = PARAM[name]
        prm[:rows, a:b] = v.reshape(-1, b - a)

    def cols(v):
        return v.reshape(-1, P).T

    put("g0", cols(norm1_g[0]))
    put("g1", cols(np.concatenate([sb_out_g[0], mnorm_g[0], sgu_out_g[0]])))
    put("g2", cols(norm2_g[0]))
    put("g3", cols(ple_norm_g[0]))
    put("g4", cols(mix_norm_2[0]))
    put("g5", cols(ffn_norm_2[0]))
    put("g6", cols(mix_norm_2[1]))
    put("g7", cols(ffn_norm_2[1]))
    put("gates_b", np.concatenate([igate_b[0], fgate_b[0]]))
    put("conv_w", conv_w[0].reshape(CONV_K, 8, MLD).transpose(2, 1, 0).reshape(MLD, -1), MLD)
    put("conv_b", conv_b[0].reshape(8, MLD).T, MLD)
    put("ln_g", sgu_ln_g[0])
    put("ln_b", sgu_ln_b[0])
    put("sgu_b", sgu_b[0].T)
    put("sgu_w", sgu_w[0].transpose(2, 0, 1).reshape(P, -1))
    put("router_b", np.concatenate([router_gb[0], router_eb[0]]))
    put("router_w", np.concatenate([router_gw[0], router_ew[0]], axis=1).reshape(KD, P, NG + NE)
        .transpose(1, 0, 2).reshape(P, -1))
    put("sc_conv", sc_w_conv_2[0].reshape(3, SCB, P).transpose(2, 0, 1).reshape(P, -1))
    fc = ffn_w_conv_2.reshape(2, 3, 2, FE, 2, P)
    put("ffn_conv", fc.transpose(5, 0, 3, 1, 2, 4).reshape(P, -1))
    put("p_t", p[0, 0].T.reshape(2, P, T).transpose(1, 0, 2).reshape(P, -1))
    finals = np.stack([np.broadcast_to(final_g, (P, D)), np.broadcast_to(final_norm_2, (P, D))])
    x_in = x[0].reshape(TT, P, D).transpose(1, 0, 2)

    nc = _bacc.Bacc("TRN2", target_bir_lowering=False, num_devices=1)
    arrays = {"stream": stream, "table": constants(), "params": prm, "finals": finals, "x_in": x_in}
    aps = []
    for name in arrays:
        arrays[name] = np.ascontiguousarray(arrays[name])
        aps.append(nc.dram_tensor(name, arrays[name].shape, F32, kind="ExternalInput").ap())
    out = nc.dram_tensor("out", (P, TT, D), F32, kind="ExternalOutput").ap()
    program(nc, *aps, out)
    r = _run(nc, [arrays], core_ids=[0])
    return np.ascontiguousarray(r.results[0]["out"].transpose(1, 0, 2)).reshape(1, T, D)
```

```python
from contextlib import ExitStack

import numpy as np

import concourse.bass as bass
from concourse import mybir

F32 = mybir.dt.float32
F32R = mybir.dt.float32r
ALU = mybir.AluOpType
ACT = mybir.ActivationFunctionType
AX = mybir.AxisListType

P = 128
D = 1024
T = 256
TT = T // P
KD = D // P
EPS = 1e-6
BIG = 1.0e30

SBW, SBH, SBD = 384, 6, 64
MLW, MLH, MLD = 384, 4, 96
SGW, SGG, SGD = 256, 4, 64
CONV_K = 4
NG, EPG, NE = 4, 8, 32
GATES = 8
N_IN = 3 * SBW + 4 * MLW + 2 * SGW + GATES
TAIL = N_IN - 6 * 512
Z_QB = 3 * SBW
Z_VB = Z_QB + 2 * MLW
Z_OB = Z_VB + MLW
Z_UC = Z_OB + MLW
Z_VC = Z_UC + SGW
Z_GATES = Z_VC + SGW
NH, HD = 16, 64
HALF = HD // 2
FF = 2816
FE = FF // 256
SCB = D // P

UNIT = 2048
U_WIN = 0
U_WOUT = U_WIN + 13
U_MOE = U_WOUT + 4
U_PLEG = U_MOE + 3 * NE
U_PLEP = U_PLEG + 4
U_SCIN = U_PLEP + 1
U_SCOUT = U_SCIN + 12
U_FFN0 = U_SCOUT + 4
U_QKV = U_FFN0 + 3 * FE
U_WO = U_QKV + 12
U_FFN1 = U_WO + 4
UNITS = U_FFN1 + 3 * FE
RING = 3

C_WIN, C_WOUT, C_PLEG, C_PLEP, C_SCOUT, C_QKV, C_WO, CHUNKS = 0, 7, 9, 11, 13, 15, 21, 23
BY_ACT = [1] * 7 + [0] * 2 + [1] * 2 + [0] * 2 + [0] * 2 + [0] * 4 + [1] * 2 + [0] * 2
BY_DVE = [1] * 7 + [1, 0] + [0] * 2 + [1] * 2 + [1, 0] + [1] * 4 + [0] * 2 + [1, 0]
CHUNK_END = [2, 4, 6, 8, 10, 12, 13] + [u + 2 * c + 2 for u, n in ((U_WOUT, 2), (U_PLEG, 2)) for c in range(n)] \
    + [U_PLEP + 1] * 2 + [u + 2 * c + 2 for u, n in ((U_SCOUT, 2), (U_QKV, 6), (U_WO, 2)) for c in range(n)]
G_SC, G_FFN0, G_FFN1 = 0, 6, 6 + FE

SLOTS = 64
PAIRS = NE // 2


def layout(parts):
    at, out = 0, {}
    for name, width in parts:
        out[name] = (at, at + width)
        at += width
    return out, at


CONST, CONST_W = layout([("ident", P), ("later", P), ("ones", P), ("upto", P), ("strict", P), ("bigpast", P),
                         ("causal", P), ("cos", TT * HALF), ("sin", TT * HALF), ("iota4", NG), ("iota32", NE),
                         ("neghalf", 8),
                         ("iota64", SLOTS)])
PARAM, PARAM_W = layout([("g0", KD), ("g1", KD), ("g2", KD), ("g3", KD), ("g4", KD), ("g5", KD), ("g6", KD),
                         ("g7", KD), ("gates_b", GATES), ("conv_w", 8 * CONV_K), ("conv_b", 8), ("ln_g", SGW),
                         ("ln_b", SGW), ("sgu_b", SGG), ("sgu_w", SGG * P), ("router_b", NG + NE),
                         ("router_w", KD * (NG + NE)), ("sc_conv", 3 * SCB), ("ffn_conv", 2 * FE * 12)])

A_S = TT * N_IN
A_T1 = A_S + SBH * 384
A_QKA = A_T1 + SBH * 384
ARENA = A_QKA + 8 * T
A_FINAL = 3072
A_PT = A_FINAL + D


def program(nc, stream, table, params, finals, p_in, x_in, out):
    ctx = ExitStack()
    with ctx:
        def sb(name, shape, dt=F32):
            return ctx.enter_context(nc.sbuf_tensor(name, shape, dt))

        sems = {}

        def S(name):
            if name not in sems:
                sems[name] = ctx.enter_context(nc.semaphore(name))
            return sems[name]

        raw = sb("raw", [P, RING, UNIT])
        whi = sb("whi", [P, RING, UNIT], F32R)
        wlo = sb("wlo", [P, RING, UNIT], F32R)
        cst = sb("cst", [P, CONST_W])
        par = sb("par", [P, PARAM_W])
        xres = sb("xres", [P, TT, D])
        xn = sb("xn", [P, TT, D])
        xhi = sb("xhi", [P, KD, T], F32R)
        xlo = sb("xlo", [P, KD, T], F32R)
        rounded = sb("rounded", [P, 7424], F32R)
        rhi = sb("rhi", [P, KD, NG + NE], F32R)
        rlo = sb("rlo", [P, KD, NG + NE], F32R)
        arena = sb("arena", [P, ARENA])
        sumsq = sb("sumsq", [P, TT])
        rstd = sb("rstd", [P, TT])
        mean = sb("mean", [P, TT])
        sm = sb("sm", [P, 832])
        rows2 = sb("rows2", [MLH, 2, T])
        spill_count = sb("spill_count", [1, 1], mybir.dt.int32)
        cwn = sb("cwn", [P, 2, 12])
        bank = [ctx.enter_context(nc.psum_tensor(f"bank{i}", [P, 512], F32)) for i in range(8)]

        def C(name):
            a, b = CONST[name]
            return cst[:, a:b]

        def Q(name):
            a, b = PARAM[name]
            return par[:, a:b]

        ident = C("ident")
        sgu_w = Q("sgu_w").rearrange("p (g t) -> p g t", g=SGG)
        router_w = Q("router_w").rearrange("p (k n) -> p k n", k=KD)
        conv_w = Q("conv_w").rearrange("p (j t) -> p j t", j=8)
        sc_conv = Q("sc_conv").rearrange("p (t j) -> p t j", t=3)
        ffn_conv = Q("ffn_conv").rearrange("p (l n) -> p l n", l=2)
        gate_b = Q("gates_b")
        small = {}
        at = 0
        for name, width in [("gt", 16), ("lf", 8), ("la", 8), ("ccol", 16), ("den", 8), ("ssb", 8), ("msb", 8),
                            ("rsb", 8), ("ssac", 4), ("msac", 4), ("rsac", 4), ("mu", 8), ("ssc", 8), ("msc", 8),
                            ("rsc", 8), ("lg", 72), ("gmax", 2), ("eqg", 8), ("ohg", 8), ("idx", 2), ("pen", 8),
                            ("eg", 8), ("gw", 2), ("em", 64), ("v1", 2), ("v2", 2), ("oh1", 64), ("oh2", 64),
                            ("cand", 64), ("dv", 2), ("p1", 2), ("p2", 2), ("m", 4), ("nm", 4), ("l", 4), ("rl", 4),
                            ("sel", 64), ("key", 64), ("over", 64), ("spill", 1)]:
            small[name] = (at, at + width)
            at += width
        assert at <= 832

        def V(name):
            a, b = small[name]
            return sm[:, a:b]

        z = arena[:, 0:TT * N_IN].rearrange("p (a n) -> p a n", a=TT)
        sa = arena[:, A_S:A_T1].rearrange("p (h b t) -> p h b t", h=SBH, b=3)
        t1 = arena[:, A_T1:A_QKA].rearrange("p (h b t) -> p h b t", h=SBH, b=3)
        sa_flat = arena[:, A_S:A_T1]
        t1_flat = arena[:, A_T1:A_QKA]
        qka = arena[:, A_QKA:A_QKA + 6 * T].rearrange("p (j t) -> p j t", j=6)
        qka_flat = arena[:, A_QKA:A_QKA + 6 * T]
        cvb = xn[0:MLD].rearrange("p a n -> p (a n)").rearrange("p (j t) -> p j t", j=8)
        qkb = arena[0:MLD, A_QKA:ARENA].rearrange("p (j t) -> p j t", j=8)
        mw = [z[:, a, Z_QB:Z_VB].rearrange("p (h b t) -> p h b t", h=2, b=3) for a in range(TT)]
        mwh = [mw[h // 2][:, h % 2] for h in range(MLH)]
        tmp = arena[:, 0:2 * SBW]
        rows = [z[0:MLH, 1, T * r:T * r + T] for r in range(3)] + [rows2[:, r, :] for r in range(2)]
        hhi = rounded[:, 0:1024].rearrange("p (b f t) -> p b f t", b=2, f=2)
        hlo = rounded[:, 1024:2048].rearrange("p (b f t) -> p b f t", b=2, f=2)
        phi = rounded[:, 0:512].rearrange("p (k t) -> p k t", k=2)
        plo = rounded[:, 512:1024].rearrange("p (k t) -> p k t", k=2)
        xghi = rounded[:, 0:1536].rearrange("p (k n) -> p k n", k=KD)
        xglo = rounded[:, 1536:3072].rearrange("p (k n) -> p k n", k=KD)
        hthi = rounded[:, 3072:3456].rearrange("p (f n) -> p f n", f=2)
        htlo = rounded[:, 3456:3840].rearrange("p (f n) -> p f n", f=2)
        yhi, ylo = rounded[:, 3840:4864], rounded[:, 4864:5888]
        pick = rounded[:, 5888:6400].rearrange("p (b a e s) -> p b a e s", b=2, a=TT, e=2)
        shi = rounded[:, 6400:6912].rearrange("p (b t) -> p b t", b=2)
        slo = rounded[:, 6912:7424].rearrange("p (b t) -> p b t", b=2)
        xtok_hi = xhi[:].rearrange("p k t -> p (k t)").rearrange("p (a n) -> p a n", a=TT)
        xtok_lo = xlo[:].rearrange("p k t -> p (k t)").rearrange("p (a n) -> p a n", a=TT)
        pickw = arena[:, 0:512].rearrange("p (b a e s) -> p b a e s", b=2, a=TT, e=2)
        sgl = arena[:, 512:768]
        hv = arena[:, 768:1024]
        xf = arena[:, 1024:1024 + KD * T].rearrange("p (k t) -> p k t", k=KD)
        wexp = arena[:, 3072:3072 + 3 * UNIT].rearrange("p (u n) -> p u n", u=3)
        osg = arena[:, 9216:9728]
        ohv = arena[:, 9728:10240]
        owt = arena[0:NE, 10240:10496]
        ows = arena[0:NE, 10496:10752]
        final_g = arena[:, A_FINAL:A_FINAL + D]
        p_t = arena[:, A_PT:A_PT + 2 * T].rearrange("p (k t) -> p k t", k=2)
        gsb = arena[:, 0:TT * D].rearrange("p (a n) -> p a n", a=TT)
        gpr = arena[:, TT * D:TT * D + 1024].rearrange("p (a n) -> p a n", a=TT)
        csb = arena[:, 0:1024].rearrange("p (b n) -> p b n", b=2)
        cvp = arena[:, 1024:1024 + SCB * (T + 2)].rearrange("p (j t) -> p j t", j=SCB)
        A_Y = 1024 + SCB * (T + 2)
        scy = arena[:, A_Y:A_Y + SCB * T].rearrange("p (j t) -> p j t", j=SCB)
        facc = arena[:, 0:2048].rearrange("p (b f t) -> p b f t", b=2, f=4)
        qkv = arena[:, 0:TT * 3 * D].rearrange("p (a n) -> p a n", a=TT)
        A_QT = TT * 3 * D
        qkt = arena[:, A_QT:A_QT + 16 * T].rearrange("p (j t) -> p j t", j=16)
        qkt_flat = arena[:, A_QT:A_QT + 16 * T]
        A_RP = A_QT + 16 * T
        rp = arena[:, A_RP:A_RP + 1024].rearrange("p (k n) -> p k n", k=4)
        ap_ = arena[:, A_RP + 1024:A_RP + 1024 + 768].rearrange("p (b n) -> p b n", b=2)
        apt = arena[:, A_RP + 1792:A_RP + 2560].rearrange("p (b n) -> p b n", b=2)

        block = ctx.enter_context(nc.Block())

        R_WOUT, R_MOE, R_PLE, R_FINAL1, R_SC, R_FFN0, R_ATT, R_FFN1 = range(1, 9)
        NORM_READS = [0, R_WOUT, R_MOE, R_PLE, R_FINAL1, R_SC, R_FFN0, R_ATT, R_FFN1]

        def group_end(u0, e, e0):
            return u0 + 2 if e0 == 0 else e * 3 + (u0 + 1)

        def down_end(u0, count, e, e0):
            return e * 3 + (u0 + 5)

        class Chain:

            def __init__(self, eng, sem):
                self.eng, self.sem, self.n, self.off = eng, sem, 0, 0

            def link(self, ins):
                self.n += 1
                ins.then_inc(self.sem, 1)
                self.eng.wait_ge(self.sem, self.off + self.n)

            def enter(self, j, per):
                self.off, self.start = j * per, self.n

            def leave(self, per, times):
                assert self.n - self.start == per
                self.off, self.n = 0, self.start + per * times

        def spilled(eng):
            eng.wait_ge(S("spill_known"), 1)
            return eng.value_load(spill_count[0:1, 0:1], min_val=0, max_val=2 * T)

        def each_expert(eng, body):
            for r in range(2):
                body(r, U_MOE + 2 * r, U_MOE + 8 + r)
            with eng.Fori(1, PAIRS - 1) as q:
                for r in range(2):
                    body(q * 2 + r, q * 6 + (U_MOE - 2 + 2 * r), q * 6 + (U_MOE + 8 + r))
            for r in range(2):
                body(NE - 2 + r, U_MOE + 3 * NE - 8 + 2 * r, U_MOE + 3 * NE - 2 + r)

        def overflow_act(act):
            with act.If(spilled(act) > 0):
                for k in range(KD):
                    act.wait_ge(S("of_turned"), k // 2 + 1)
                    ins = act.activation(xf[:, k, :], bank[k // 2][:, (k % 2) * T:(k % 2 + 1) * T], ACT.Copy,
                                         scale=Q("g2")[:, k:k + 1])
                ins.then_inc(S("of_tokens"), 1)

                def expert(n, gate_up, down):
                    for u, unit in enumerate((gate_up, gate_up + 1, down)):
                        act.dma_start(wexp[:, u, :], stream[unit]).then_inc(S(f"of_landed{u}"), 16)
                    act.wait_ge(S("of_gate_up"), n + 1)
                    act.activation(osg, bank[0][:], ACT.Silu).then_inc(S("of_silu"), 1)
                    act.wait_ge(S("of_down"), n + 1)

                each_expert(act, expert)

        def overflow_dve(dve):
            with dve.If(spilled(dve) > 0):
                dve.wait_ge(S("of_weights_turned"), 1)
                dve.tensor_copy(owt, bank[1][0:NE, 0:T]).then_inc(S("of_weights"), 1)
                dve.wait_ge(S("of_weights"), 1)

                def expert(n, gate_up, down):
                    one = ident[0:NE, n:n + 1] if isinstance(n, int) else ident[0:NE, bass.ds(n, 1)]
                    dve.tensor_tensor(ows, owt, one.broadcast_to([NE, T]), ALU.mult).then_inc(S("of_row"), 1)
                    dve.wait_ge(S("of_silu"), n + 1)
                    dve.tensor_tensor(ohv, osg, bank[1][:], ALU.mult).then_inc(S("of_product"), 1)
                    dve.wait_ge(S("of_product"), n + 1)
                    half = ohv.rearrange("p (f t) -> p f t", f=2)
                    dve.tensor_tensor(half, bank[2][:, 0:T].unsqueeze(1).broadcast_to([P, 2, T]), half, ALU.mult)\
                       .then_inc(S("of_hidden"), 1)
                    dve.wait_ge(S("of_down"), n + 1)

                each_expert(dve, expert)

        def overflow_pe(pe):
            with pe.If(spilled(pe) > 0):
                for k in range(KD):
                    for t in range(TT):
                        ins = pe.transpose(bank[k // 2][:, (k % 2) * T + t * P:(k % 2) * T + t * P + P],
                                           xn[:, t, P * k:P * k + P], ident)
                    if k % 2:
                        ins.then_inc(S("of_turned"), 1)
                pe.wait_ge(S("of_tokens"), 1)
                pe.wait_ge(S("over_ready"), 1)
                over = V("over").rearrange("p (a n) -> p a n", a=TT)
                for t in range(TT):
                    ins = pe.transpose(bank[1][0:NE, P * t:P * t + P], over[:, t, :], ident)
                ins.then_inc(S("of_weights_turned"), 1)
                pe.wait_ge(S("of_weights"), 1)

                def expert(n, gate_up, down):
                    pe.wait_ge(S("of_row"), n + 1)
                    pe.matmul(bank[2][:, 0:T], C("ones")[0:NE, :], ows, start=True, stop=True, skip_group_check=True)
                    for kk in range(KD):
                        if kk % 4 == 0:
                            pe.wait_ge(S(f"of_landed{kk // 4}"), n * 16 + 16)
                        for f in range(4):
                            w = 512 * (kk % 4) + P * f
                            ins = pe.matmul(bank[f // 2][:, (f % 2) * T:(f % 2 + 1) * T],
                                            wexp[:, kk // 4, w:w + P], xf[:, kk, :],
                                            start=kk == 0 and f % 2 == 0, stop=kk == 7, skip_group_check=True)
                    ins.then_inc(S("of_gate_up"), 1)
                    pe.wait_ge(S("of_hidden"), n + 1)
                    pe.wait_ge(S("of_landed2"), n * 16 + 16)
                    for t in range(TT):
                        for c in range(2):
                            for f in range(2):
                                w = D * f + 512 * c
                                ins = pe.matmul(bank[4 + 2 * t + c][:], ohv[:, T * f + P * t:T * f + P * t + P],
                                                wexp[:, 2, w:w + 512], start=False, stop=False, skip_group_check=True)
                    ins.then_inc(S("of_down"), 1)

                each_expert(pe, expert)

        @block.sync
        def _(sp):
            sp.dma_start(xres[:], x_in).then_inc(S("x_loaded"), 16)
            sp.dma_start(cst[:], table).then_inc(S("table_loaded"), 16)
            sp.dma_start(raw[:, 0, :], stream[0]).then_inc(S("landed0"), 16)
            sp.dma_start(par[:], params).then_inc(S("params_loaded"), 16)
            for n in range(1, RING):
                sp.dma_start(raw[:, n, :], stream[n]).then_inc(S(f"landed{n}"), 16)
            with sp.Fori(0, UNITS // RING - 1) as j:
                for s in range(RING):
                    sp.wait_ge(S("low_done"), RING * j + s + 1)
                    sp.dma_start(raw[:, s, :], stream[RING * j + (s + RING)]).then_inc(S(f"landed{s}"), 16)
            sp.wait_ge(S("y_ready"), 1)
            sp.dma_start(out, xn[:]).then_inc(S("stored"), 16)
            sp.wait_ge(S("stored"), 16)

        @block.scalar
        def _(act):
            chain = Chain(act, S("act_chain"))
            done = [0]

            def split(n):
                unit0, off = n if isinstance(n, tuple) else (n, 0)
                s = unit0 % RING
                act.wait_ge(S(f"landed{s}"), off * 16 // RING + 16 * (unit0 // RING + 1) if isinstance(off, int)
                            else off * (16 // 1) + 16 * (unit0 // RING + 1))
                if unit0 >= RING:
                    act.wait_ge(S("unit_used"), (off if isinstance(off, int) else off * RING) + unit0 - RING + 1)
                act.activation(whi[:, s, :], raw[:, s, :], ACT.Copy).then_inc(S("high_done"), 1)

            def split_to(n):
                while done[0] <= min(n, UNITS - 1):
                    split(done[0])
                    done[0] += 1

            def norm_act(i, turn=True):
                if i == 0:
                    act.wait_ge(S("x_loaded"), 16)
                else:
                    act.wait_ge(S("residual_ready"), NORM_READS[i])
                for t in range(TT):
                    ins = act.activation(xn[:, t, :], xres[:, t, :], ACT.Square, accum_out=sumsq[:, t:t + 1])
                ins.then_inc(S("sumsq_ready"), 1)
                if turn:
                    act.wait_ge(S("rstd_ready"), i + 1)
                    act.activation(xn[:, 1, :], xres[:, 1, :], ACT.Copy, scale=rstd[:, 1:2]).then_inc(S("xn1_ready"), 1)

            def turn_act(q):
                for k in range(KD):
                    if k % 2 == 0:
                        act.wait_ge(S("turned"), 4 * q + k // 2 + 1)
                    ins = act.activation(xhi[:, k, :], bank[k // 2][:, (k % 2) * T:(k % 2 + 1) * T], ACT.Copy,
                                         scale=Q(f"g{q}")[:, k:k + 1])
                    if k % 2:
                        ins.then_inc(S("xhi_ready"), 1)

            split_to(0)
            act.wait_ge(S("table_loaded"), 16)
            act.wait_ge(S("params_loaded"), 16)
            norm_act(0)
            split_to(1)
            act.activation(rhi[:], router_w, ACT.Copy).then_inc(S("setup_high"), 1)
            turn_act(0)
            for c in range(7):
                split_to(min(U_WIN + 2 * c + 1, 12) + 2)
                act.wait_ge(S("unit_used"), CHUNK_END[C_WIN + c])
                w = min(512, N_IN - 512 * c)
                act.activation(z[:, 0, 512 * c:512 * c + w], bank[2 * (c % 2)][:, 0:w], ACT.Copy)\
                   .then_inc(S("act_freed"), 1)
            split_to(15)
            for b in (0, 2):
                act.wait_ge(S("turned_a"), b + 1)
                act.activation(qka_flat[:, 512 * b:512 * b + 512], bank[4 + b][:], ACT.Copy).then_inc(S("qka_act"), 1)
            for b in range(2):
                act.wait_ge(S("turned_b"), b + 1)
                act.activation(cvb[:, 2 * b:2 * b + 2, :],
                               bank[(7, 0, 1, 2)[b]][0:MLD, :].rearrange("p (j t) -> p j t", j=2), ACT.Copy)\
                   .then_inc(S("cvb_act"), 1)
            act.wait_ge(S("dve_freed"), sum(BY_DVE[:7]))
            chain.link(act.activation(z[:, :, Z_UC:Z_GATES], z[:, :, Z_UC:Z_GATES], ACT.Gelu_apprx_tanh))
            act.activation(z[:, :, Z_OB:Z_UC], z[:, :, Z_OB:Z_UC], ACT.Sigmoid).then_inc(S("gelu_ready"), 1)
            for h in range(SBH):
                act.wait_ge(S("scores_a"), h + 1)
                b = bank[(3, 4, 5, 6, 7, 0)[h]]
                act.activation(sa_flat[:, 384 * h:384 * h + 384], b[:, 0:384], ACT.Copy, scale=SBD ** -0.5)
                ins = act.activation(t1_flat[:, 384 * h:384 * h + 384], b[:, 0:384], ACT.Abs, scale=SBD ** -0.5)
            chain.link(ins)
            act.wait_ge(S("cvb_dve"), 2)
            act.wait_ge(S("cvb_act"), 2)
            for j in range(8):
                act.activation(qkb[:, j, :], cvb[:, j, :], ACT.Identity, scale=conv_w[0:MLD, j, 3:4],
                               bias=Q("conv_b")[0:MLD, j:j + 1]).then_inc(S("conv_begun"), 1)
            chain.link(act.activation(t1_flat, t1_flat, ACT.Exp, scale=-1.0))
            act.wait_ge(S("gates_ready"), 1)
            gt = V("gt").rearrange("p (a n) -> p a n", a=TT)
            la = V("la").rearrange("p (a n) -> p a n", a=TT)
            chain.link(act.activation(la, gt[:, :, 4:8], ACT.Abs))
            chain.link(act.activation(la, la, ACT.Exp, scale=-1.0))
            act.activation(la, la, ACT.Ln, bias=1.0).then_inc(S("gate_log"), 1)
            act.activation(t1_flat, t1_flat, ACT.Ln, bias=1.0).then_inc(S("softplus_log"), 1)
            act.wait_ge(S("conv_done"), 1)
            act.activation(qkb[:], qkb[:], ACT.Silu).then_inc(S("qkb_ready"), 1)
            act.wait_ge(S("mrow_ready"), 1)
            act.activation(rows[4], rows[3], ACT.Exp, scale=-1.0).then_inc(S("enrow_ready"), 1)
            act.wait_ge(S("ccol_ready"), 1)
            act.wait_ge(S("mw_ready"), 1)
            ccol = V("ccol")
            for h in range(MLH):
                act.activation(mwh[h][:, 0:2, :], mwh[h][:, 0:2, :], ACT.Exp, scale=-1.0, bias=ccol[:, h:h + 1])
                act.activation(mwh[h][:, 2, :], mwh[h][:, 2, :], ACT.Exp, scale=-1.0, bias=ccol[:, 4 + h:5 + h])\
                   .then_inc(S("decay_ready"), 1)
            act.wait_ge(S("expo_ready"), 1)
            act.activation(sa_flat, sa_flat, ACT.Exp).then_inc(S("weights_a"), 1)
            act.wait_ge(S("out_a"), 1)
            ssac = V("ssac")
            for t in range(TT):
                chain.link(act.activation(xn[:, t, 0:SBW], bank[1 + t][:, 0:SBW], ACT.Copy))
            for t in range(TT):
                ins = act.activation(tmp[:, 0:SBW], xn[:, t, 0:SBW], ACT.Square, accum_out=ssac[:, t:t + 1])
                chain.link(ins)
            act.wait_ge(S("yc_ready"), 1)
            for t in range(TT):
                ins = act.activation(tmp[:, 0:SGW], xn[:, t, SBW + MLW:D], ACT.Square, accum_out=ssac[:, 2 + t:3 + t])
                if t == 0:
                    chain.link(ins)
            ins.then_inc(S("sumsq_ac"), 1)
            act.wait_ge(S("sumsq_ac"), 1)
            act.wait_ge(S("hb_ready"), 1)
            act.activation(tmp.rearrange("p (a n) -> p a n", a=TT), xn[:, :, SBW:SBW + MLW], ACT.Square)\
               .then_inc(S("hb_squares"), 1)
            act.wait_ge(S("rstd_ac"), 1)
            for t in range(TT):
                act.activation(xn[:, t, 0:SBW], xn[:, t, 0:SBW], ACT.Copy, scale=V("rsac")[:, t:t + 1])
                ins = act.activation(xn[:, t, SBW + MLW:D], xn[:, t, SBW + MLW:D], ACT.Copy,
                                     scale=V("rsac")[:, 2 + t:3 + t])
            ins.then_inc(S("xn1_ready"), 1)
            turn_act(1)
            for c in range(2):
                split_to(U_WOUT + 2 * c + 3)
            norm_act(1)
            turn_act(2)
            act.wait_ge(S("gdiff_ready"), 1)
            act.activation(V("eg"), V("eg"), ACT.Exp).then_inc(S("gexp_ready"), 1)
            act.wait_ge(S("vdiff_ready"), 1)
            act.activation(V("dv"), V("dv"), ACT.Exp).then_inc(S("vexp_ready"), 1)

            def gather_high(k0, wait):
                act.wait_ge(S("gathered"), wait)
                for k in range(4):
                    ins = act.activation(xghi[:, k0 + k, :].rearrange("p (c s) -> p c s", s=SLOTS)[:, 0:3:2, :],
                                         bank[1][:, P * k:P * k + P].rearrange("p (c s) -> p c s", s=SLOTS), ACT.Copy,
                                         scale=Q("g2")[:, k0 + k:k0 + k + 1])
                ins.then_inc(S("gather_high"), 1)

            def turned_high(p, b):
                act.wait_ge(S("turned_pair"), p + 1)
                act.activation(shi[:, b, :], bank[1][:, 0:T], ACT.Copy)
                for f in range(2):
                    ins = act.activation(hthi[:, f, :].rearrange("p (c s) -> p c s", s=SLOTS)[:, 0:3:2, :],
                                         bank[1][:, T + P * f:T + P * f + P].rearrange("p (c s) -> p c s", s=SLOTS),
                                         ACT.Copy)
                ins.then_inc(S("turned_high"), 1)

            def y_high(wait):
                act.wait_ge(S("unit_used"), wait)
                for c in range(2):
                    ins = act.activation(yhi[:, 512 * c:512 * c + 512], bank[2 + c][:], ACT.Copy)
                ins.then_inc(S("y_high"), 1)

            def silu_pair(wait):
                act.wait_ge(S("unit_used"), wait)
                act.activation(sgl, bank[0][:, 0:256], ACT.Silu).then_inc(S("pair_silu"), 1)

            def pair_act(p, p0, off):
                n = U_MOE + 6 * p0 - 2
                ahead = (lambda k: split_to(n + k)) if off is None else (lambda k: split((n + k, off)))
                used = lambda k: (0 if off is None else off * RING) + (n + k)
                ahead(2)
                turned_high(p - 1, (p0 - 1) % 2)
                ahead(3)
                ahead(4)
                ahead(5)
                silu_pair(used(4))
                if p0 < PAIRS - 1:
                    gather_high(0, 2 * p + 3)
                ahead(6)
                if p0 < PAIRS - 1:
                    gather_high(4, 2 * p + 4)
                ahead(7)
                y_high(used(6))

            act.wait_ge(S("router_done"), 1)
            act.activation(xtok_hi, xn[:], ACT.Copy).then_inc(S("xtok_high"), 1)
            act.wait_ge(S("zeros_ready"), 1)
            gather_high(0, 1)
            gather_high(4, 2)
            split_to(U_MOE + 5)
            silu_pair(U_MOE + 4)
            gather_high(0, 3)
            gather_high(4, 4)
            pair_act(1, 1, None)
            assert done[0] == U_MOE + 12
            with act.Fori(0, (PAIRS - 4) // 2) as j:
                for b in range(2):
                    pair_act(2 * j + (2 + b), 2 + b, 4 * j)
            done[0] = U_MOE + 6 * (PAIRS - 2)
            pair_act(PAIRS - 2, PAIRS - 2, None)
            pair_act(PAIRS - 1, PAIRS - 1, None)
            turned_high(PAIRS - 1, (PAIRS - 1) % 2)
            y_high(U_MOE + 3 * NE)
            overflow_act(act)

            def ffn_act(layer, e, off, e0):
                g0, d0, u0 = (G_FFN0, 0, U_FFN0) if layer == 0 else (G_FFN1, FE, U_FFN1)
                b, gb = e0 % 2, (g0 + e0) % 2
                n = u0 + 3 * e0 - 1

                def ahead(k):
                    if off is None:
                        split_to(n + k)
                    elif n + k < UNITS:
                        split((n + k, off))
                ahead(3)
                act.wait_ge(S("unit_used"), group_end(u0, e, e0))
                act.wait_ge(S("taps_ready"), layer * FE + 1 + e)
                if e0 >= 2:
                    act.wait_ge(S("h_ready"), d0 - 1 + e)
                for f in range(4):
                    ins = act.activation(facc[:, b, f, :], bank[2 * gb + f // 2][:, (f % 2) * T:(f % 2 + 1) * T],
                                         ACT.Copy, scale=cwn[:, b, 8 + f:9 + f])
                ins.then_inc(S("ffn_begun"), 1)
                ahead(4)
                act.wait_ge(S("g_free"), g0 + 1 + e)
                act.activation(facc[:, b, 0:2, :], facc[:, b, 0:2, :], ACT.Silu).then_inc(S("silu_ready"), 1)
                ahead(5)
                act.wait_ge(S("hv_ready"), layer * FE + 1 + e)
                if e0 >= 2:
                    act.wait_ge(S("unit_used"), down_end(u0, FE, e - 2, e0 - 2))
                act.activation(hhi[:, b, :, :], facc[:, b, 2:4, :], ACT.Copy).then_inc(S("hhi_ready"), 1)

            norm_act(2)
            act.dma_start(p_t, p_in).then_inc(S("p_loaded"), 16)
            act.dma_start(final_g, finals[0]).then_inc(S("final1_loaded"), 16)
            turn_act(3)
            act.wait_ge(S("p_loaded"), 16)
            act.activation(phi, p_t, ACT.Copy).then_inc(S("p_high"), 1)
            for c in range(2):
                split_to(U_PLEG + 2 * c + 3)
                act.wait_ge(S("unit_used"), CHUNK_END[C_PLEG + c])
                for t in range(TT):
                    ins = act.activation(gsb[:, t, 512 * c:512 * c + 512], bank[2 * ((C_PLEG + c) % 2) + t][:],
                                         ACT.Sigmoid)
                ins.then_inc(S("act_freed"), 1)
            split_to(U_PLEP + 2)
            norm_act(3, turn=False)
            split_to(U_SCIN + 1)
            norm_act(4)
            turn_act(4)
            for i in range(6):
                split_to(U_SCIN + 2 * i + 3)
                if i < 4:
                    g = G_SC + i
                    act.wait_ge(S("unit_used"), U_SCIN + 2 * i + 2)
                    act.activation(csb[:, i % 2, :], bank[2 * (g % 2)][:], ACT.Copy).then_inc(S("c_ready"), 1)
                    act.wait_ge(S("g_free"), g + 1)
                    for f in range(2 * i, 2 * i + 2):
                        ins = act.activation(scy[:, f, :], cvp[:, f, 2:2 + T], ACT.Copy, scale=sc_conv[:, 2, f:f + 1])
                    ins.then_inc(S("sc_begun"), 1)
            for f in range(4):
                act.wait_ge(*((S("g_free"), G_SC + 5 + f // 2) if f % 2 else (S("sc_product"), f // 2 + 1)))
                act.activation(xhi[:, 2 * f:2 * f + 2, :], scy[:, 2 * f:2 * f + 2, :], ACT.Copy)\
                   .then_inc(S("sc_high"), 1)
            for c in range(2):
                split_to(U_SCOUT + 2 * c + 3)

            def ffn(layer):
                ffn_act(layer, 0, None, 0)
                ffn_act(layer, 1, None, 1)
                u0 = U_FFN0 if layer == 0 else U_FFN1
                assert done[0] == min(u0 + 8, UNITS)
                with act.Fori(0, (FE - 3) // 2) as j:
                    for b in range(2):
                        ffn_act(layer, 2 * j + (2 + b), 2 * j, 2 + b)
                done[0] = u0 + 3 * (FE - 1) + 2
                ffn_act(layer, FE - 1, None, FE - 1)

            norm_act(5)
            turn_act(5)
            ffn(0)
            norm_act(6)
            turn_act(6)
            for c in range(6):
                split_to(U_QKV + 2 * c + 3)
                if c >= 4:
                    act.wait_ge(S("unit_used"), CHUNK_END[C_QKV + c])
                    for t in range(TT):
                        ins = act.activation(qkv[:, t, 512 * c:512 * c + 512], bank[2 * ((C_QKV + c) % 2) + t][:],
                                             ACT.Copy)
                    ins.then_inc(S("act_freed"), 1)
            split_to(U_WO + 2)
            for b in range(0, 8, 2):
                act.wait_ge(S("qk_turned"), b + 1)
                act.activation(qkt_flat[:, 512 * b:512 * b + 512], bank[b][:], ACT.Copy).then_inc(S("qkt_act"), 1)

            def pt_copy(h):
                act.wait_ge(S("p_turned"), h + 1)
                if h >= 2:
                    act.wait_ge(S("pv_done"), h - 1)
                act.activation(apt[:, h % 2, :], bank[2 + h % 2][:, 0:384], ACT.Copy).then_inc(S("pt_ready"), 1)

            for h in range(NH):
                act.wait_ge(S("negmax_ready"), h + 1)
                if h >= 2:
                    act.wait_ge(S("p_turned"), h - 1)
                b = h % 2
                nm, l = V("nm"), V("l")
                act.activation(ap_[:, b, 0:128], bank[b][:, 0:128], ACT.Exp, scale=HD ** -0.5,
                               bias=nm[:, 2 * b:2 * b + 1], accum_out=l[:, 2 * b:2 * b + 1])
                act.activation(ap_[:, b, 128:384], bank[b][:, 128:384], ACT.Exp, scale=HD ** -0.5,
                               bias=nm[:, 2 * b + 1:2 * b + 2], accum_out=l[:, 2 * b + 1:2 * b + 2])\
                   .then_inc(S("exp_done"), 1)
                if h >= 1:
                    pt_copy(h - 1)
            pt_copy(NH - 1)
            for b in range(4):
                act.wait_ge(S("pv_done"), 4 * b + 4)
                act.activation(xhi[:, 2 * b:2 * b + 2, :], bank[4 + b][:].rearrange("p (j t) -> p j t", j=2),
                               ACT.Copy).then_inc(S("o_high"), 1)
            for c in range(2):
                split_to(U_WO + 2 * c + 3)
            norm_act(7)
            act.dma_start(final_g, finals[1]).then_inc(S("final2_loaded"), 16)
            turn_act(7)
            ffn(1)
            norm_act(8, turn=False)

        @block.gpsimd
        def _(pool):
            chain = Chain(pool, S("pool_chain"))
            nh = C("neghalf")

            def rsqrt(dst, mid, src, count, width):
                chain.link(pool.tensor_scalar(mid, src, 1.0 / count, EPS, ALU.mult, ALU.add))
                return pool.tensor_tensor(dst, mid, nh[:, 0:width], ALU.pow)

            def norm_pool(i):
                pool.wait_ge(S("sumsq_ready"), i + 1)
                rsqrt(rstd[:], mean[:], sumsq[:], D, TT).then_inc(S("rstd_ready"), 1)
                pool.wait_ge(S("rstd_ready"), i + 1)

            pool.wait_ge(S("table_loaded"), 16)
            norm_pool(0)
            pool.wait_ge(S("params_loaded"), 16)
            pool.memset(sgu_w[64:128, :, 0:64], 0.0).then_inc(S("sgu_masked"), 1)
            pool.wait_ge(S("sgu_masked"), 1)
            pool.wait_ge(S("ln_squares"), 1)
            rsqrt(V("rsc"), V("msc"), V("ssc"), SGD, 8).then_inc(S("ln_rstd"), 1)
            pool.wait_ge(S("sumsq_ac"), 1)
            chain.link(pool.tensor_scalar(V("msac")[:, 0:2], V("ssac")[:, 0:2], 1.0 / SBW, EPS, ALU.mult, ALU.add))
            chain.link(pool.tensor_scalar(V("msac")[:, 2:4], V("ssac")[:, 2:4], 1.0 / SGW, EPS, ALU.mult, ALU.add))
            pool.tensor_tensor(V("rsac"), V("msac"), nh[:, 0:4], ALU.pow).then_inc(S("rstd_ac"), 1)
            pool.wait_ge(S("hb_sums"), 1)
            rsqrt(V("rsb"), V("msb"), V("ssb"), MLD, 8).then_inc(S("hb_rstd"), 1)
            norm_pool(1)

            def weigh_pair(p, p0):
                b = p0 % 2
                if p0 >= 2:
                    pool.wait_ge(S("turned_pair"), p - 1)
                two = bass.ds(2 * p, 2) if p0 is not p else slice(2 * p, 2 * p + 2)
                wt = V("oh1").rearrange("p (a e) -> p a e", a=TT)[:, :, two].unsqueeze(3)
                pool.wait_ge(S("pick_ready"), p + 1)
                for t in range(TT):
                    ins = pool.tensor_tensor(pickw[:, b, t], pick[:, b, t].bitcast(F32),
                                             wt[:, t].broadcast_to([P, 2, SLOTS]), ALU.mult)
                ins.then_inc(S("pickw_ready"), 1)

            for zero in (xghi, xglo, hthi, htlo):
                ins = pool.memset(zero[:, :, SLOTS:2 * SLOTS].bitcast(F32), 0.0)
            ins.then_inc(S("zeros_ready"), 1)
            pool.wait_ge(S("zeros_ready"), 1)
            pool.wait_ge(S("wt_ready"), 1)
            weigh_pair(0, 0)
            weigh_pair(1, 1)
            with pool.Fori(0, (PAIRS - 2) // 2) as j:
                for b in range(2):
                    weigh_pair(2 * j + (2 + b), 2 + b)
            norm_pool(2)
            norm_pool(3)
            norm_pool(4)

            def taps(layer, e, e0):
                g0 = G_FFN0 if layer == 0 else G_FFN1
                b = e0 % 2
                if e0 >= 2 or layer == 1:
                    pool.wait_ge(S("g_free"), g0 - 1 + e)
                src = ffn_conv[:, layer, 12 * e0:12 * e0 + 12] if isinstance(e, int) else \
                    par[:, bass.ds(e * 12 + (PARAM["ffn_conv"][0] + layer * FE * 12), 12)]
                pool.tensor_copy(cwn[:, b, :], src).then_inc(S("taps_ready"), 1)

            def ffn(layer):
                taps(layer, 0, 0)
                taps(layer, 1, 1)
                with pool.Fori(0, (FE - 3) // 2) as j:
                    for b in range(2):
                        taps(layer, 2 * j + (2 + b), 2 + b)
                taps(layer, FE - 1, FE - 1)

            norm_pool(5)
            ffn(0)
            norm_pool(6)
            norm_pool(7)
            ffn(1)
            norm_pool(8)

        @block.vector
        def _(dve):
            chain = Chain(dve, S("dve_chain"))
            link = chain.link
            done = [0]

            def split(n):
                unit0, off = n if isinstance(n, tuple) else (n, 0)
                s = unit0 % RING
                dve.wait_ge(S("high_done"), (off if isinstance(off, int) else off * RING) + unit0 + 1)
                dve.tensor_tensor(wlo[:, s, :], raw[:, s, :], whi[:, s, :].bitcast(F32), ALU.subtract)\
                   .then_inc(S("low_done"), 1)

            def split_to(n):
                while done[0] <= min(n, UNITS - 1):
                    split(done[0])
                    done[0] += 1

            def norm_dve(i):
                dve.wait_ge(S("rstd_ready"), i + 1)
                dve.tensor_scalar(xn[:, 0, :], xres[:, 0, :], rstd[:, 0:1], None, ALU.mult)\
                   .then_inc(S("xn0_ready"), 1)

            def turn_dve(q):
                for k in range(KD):
                    if k % 2 == 0:
                        dve.wait_ge(S("xhi_ready"), 4 * q + k // 2 + 1)
                    ins = dve.scalar_tensor_tensor(xlo[:, k, :], bank[k // 2][:, (k % 2) * T:(k % 2 + 1) * T],
                                                   Q(f"g{q}")[:, k:k + 1], xhi[:, k, :].bitcast(F32), ALU.mult,
                                                   ALU.subtract)
                    if k % 2:
                        ins.then_inc(S("xt_ready"), 1)

            def add_chunks(u0, c0):
                for c in range(2):
                    split_to(u0 + 2 * c + 3)
                    dve.wait_ge(S("unit_used"), CHUNK_END[c0 + c])
                    for t in range(TT):
                        r = xres[:, t, 512 * c:512 * c + 512]
                        ins = dve.tensor_tensor(r, bank[2 * ((c0 + c) % 2) + t][:], r, ALU.add)
                    ins.then_inc(S("dve_freed") if c == 0 else S("residual_ready"), 1)

            def add_down(units):
                if units != U_MOE + 3 * NE:
                    dve.wait_ge(S("unit_used"), units)
                for t in range(TT):
                    for c in range(2):
                        r = xres[:, t, 512 * c:512 * c + 512]
                        ins = dve.tensor_tensor(r, bank[4 + 2 * t + c][:], r, ALU.add)
                ins.then_inc(S("residual_ready"), 1)

            split_to(0)
            dve.wait_ge(S("table_loaded"), 16)
            dve.wait_ge(S("params_loaded"), 16)
            dve.wait_ge(S("x_loaded"), 16)
            norm_dve(0)
            split_to(1)
            dve.wait_ge(S("setup_high"), 1)
            dve.tensor_tensor(rlo[:], router_w, rhi[:].bitcast(F32), ALU.subtract).then_inc(S("setup_low"), 1)
            turn_dve(0)
            for c in range(7):
                split_to(min(U_WIN + 2 * c + 1, 12) + 2)
                dve.wait_ge(S("unit_used"), CHUNK_END[C_WIN + c])
                w = min(512, N_IN - 512 * c)
                dve.tensor_copy(z[:, 1, 512 * c:512 * c + w], bank[2 * (c % 2) + 1][:, 0:w]).then_inc(S("dve_freed"), 1)
            split_to(15)
            dve.wait_ge(S("act_freed"), 7)
            dve.wait_ge(S("dve_freed"), 7)
            gt = V("gt").rearrange("p (a n) -> p a n", a=TT)
            dve.tensor_tensor(gt, z[:, :, Z_GATES:N_IN], gate_b.unsqueeze(1).broadcast_to([P, TT, GATES]), ALU.add)\
               .then_inc(S("gates_ready"), 1)
            dve.wait_ge(S("turned_a"), 2)
            dve.tensor_copy(qka_flat[:, 512:1024], bank[5][:]).then_inc(S("qka_dve"), 1)
            for b in range(2, 4):
                dve.wait_ge(S("turned_b"), b + 1)
                dve.tensor_copy(cvb[:, 2 * b:2 * b + 2, :],
                                bank[(7, 0, 1, 2)[b]][0:MLD, :].rearrange("p (j t) -> p j t", j=2))\
                   .then_inc(S("cvb_dve"), 1)
            dve.wait_ge(S("cvb_act"), 2)
            dve.wait_ge(S("conv_begun"), 8)
            for k in range(3):
                for j in range(8):
                    y = qkb[:, j, 3 - k:T]
                    ins = dve.scalar_tensor_tensor(y, cvb[:, j, 0:T - 3 + k], conv_w[0:MLD, j, k:k + 1], y,
                                                   ALU.mult, ALU.add)
                if k < 2:
                    link(ins)
            ins.then_inc(S("conv_done"), 1)
            dve.wait_ge(S("gates_ready"), 1)
            dve.wait_ge(S("gate_log"), 1)
            lf = V("lf").rearrange("p (a n) -> p a n", a=TT)
            dve.scalar_tensor_tensor(lf, gt[:, :, 4:8], 0.0, V("la").rearrange("p (a n) -> p a n", a=TT),
                                     ALU.min, ALU.subtract).then_inc(S("logf_ready"), 1)
            dve.wait_ge(S("softplus_log"), 1)
            link(dve.scalar_tensor_tensor(t1_flat, sa_flat, 0.0, t1_flat, ALU.max, ALU.add))
            link(dve.tensor_tensor(sa_flat, sa_flat, t1_flat, ALU.subtract))
            strict = C("strict").unsqueeze(1).broadcast_to([P, SBH, P])
            link(dve.tensor_tensor(t1[:, :, 2, :], t1[:, :, 2, :], strict, ALU.mult))
            dve.tensor_tensor(t1[:, :, 0, :], t1[:, :, 0, :], strict, ALU.mult).then_inc(S("l_ready"), 1)
            dve.wait_ge(S("brow_done"), 1)
            link(dve.tensor_copy(rows[0], bank[1][0:MLH, 0:T]))
            link(dve.tensor_tensor(rows[1], bank[1][0:MLH, T:2 * T], rows[0], ALU.subtract))
            link(dve.tensor_tensor_scan(rows[2], rows[1], rows[1], 0.0, ALU.max, ALU.max))
            dve.tensor_tensor(rows[3], rows[0], rows[2], ALU.add).then_inc(S("mrow_ready"), 1)
            dve.wait_ge(S("gelu_ready"), 1)
            vg = [z[:, t, Z_VC:Z_GATES].rearrange("p (g d) -> p g d", g=SGG) for t in range(TT)]
            mu = V("mu").rearrange("p (a g) -> p a g", a=TT)
            ssc = V("ssc").rearrange("p (a g) -> p a g", a=TT)
            rsc = V("rsc").rearrange("p (a g) -> p a g", a=TT)
            sq = [tmp[:, 256 * t:256 * t + 256].rearrange("p (g d) -> p g d", g=SGG) for t in range(TT)]
            wide = lambda v, t: v[:, t, :].unsqueeze(2).broadcast_to([P, SGG, SGD])
            for t in range(TT):
                ins = dve.tensor_reduce(mu[:, t, :], vg[t], AX.X, ALU.add)
            link(ins)
            link(dve.tensor_scalar(V("mu"), V("mu"), 1.0 / SGD, None, ALU.mult))
            for t in range(TT):
                ins = dve.tensor_tensor(vg[t], vg[t], wide(mu, t), ALU.subtract)
            link(ins)
            for t in range(TT):
                ins = dve.tensor_tensor(sq[t], vg[t], vg[t], ALU.mult)
            link(ins)
            for t in range(TT):
                ins = dve.tensor_reduce(ssc[:, t, :], sq[t], AX.X, ALU.add)
            ins.then_inc(S("ln_squares"), 1)
            for h in range(SBH):
                dve.wait_ge(S("after_a"), h + 1)
                s = sa_flat[:, 384 * h:384 * h + 384]
                ins = dve.tensor_tensor(s, s, bank[(3, 4, 5, 6, 7, 0)[h]][:, 0:384], ALU.subtract)
            ins.then_inc(S("expo_ready"), 1)
            dve.wait_ge(S("mbc_done"), 1)
            big = C("bigpast").unsqueeze(1).broadcast_to([P, 2, P])
            for k in range(2):
                mb = bank[3 + 4 * k][:].rearrange("p (h b t) -> p h b t", h=2, b=2)
                dve.tensor_tensor(mw[k][:, :, 0, :], mb[:, :, 0, :], big, ALU.add)
                dve.tensor_copy(mw[k][:, :, 1, :], mb[:, :, 1, :])
                ins = dve.tensor_tensor(mw[k][:, :, 2, :], mb[:, :, 1, :], big, ALU.add)
            ins.then_inc(S("mw_ready"), 1)
            dve.wait_ge(S("cols_done"), 1)
            dve.tensor_copy(V("ccol"), bank[2][:, 0:16]).then_inc(S("ccol_ready"), 1)
            dve.wait_ge(S("ln_rstd"), 1)
            for t in range(TT):
                ins = dve.tensor_tensor(vg[t], vg[t], wide(rsc, t), ALU.mult)
            link(ins)
            for t in range(TT):
                ins = dve.tensor_tensor(z[:, t, Z_VC:Z_GATES], z[:, t, Z_VC:Z_GATES], Q("ln_g"), ALU.mult)
            link(ins)
            for t in range(TT):
                ins = dve.tensor_tensor(z[:, t, Z_VC:Z_GATES], z[:, t, Z_VC:Z_GATES], Q("ln_b"), ALU.add)
            ins.then_inc(S("ln_ready"), 1)
            for h in range(MLH):
                dve.wait_ge(S("scores_b"), h + 1)
                dve.wait_ge(S("decay_ready"), h + 1)
                m = mwh[h]
                dve.scalar_tensor_tensor(m, bank[(4, 5, 6, 7)[h]][:, 0:384].rearrange("p (b t) -> p b t", b=3),
                                         MLD ** -0.5, m, ALU.mult, ALU.mult).then_inc(S("s_ready"), 1)
            dve.wait_ge(S("weights_a"), 1)
            dve.tensor_tensor(sa[:, :, 0, :], sa[:, :, 0, :], strict, ALU.mult)
            dve.tensor_tensor(sa[:, :, 2, :], sa[:, :, 2, :], strict, ALU.mult).then_inc(S("a_ready"), 1)
            dve.wait_ge(S("mixed_done"), 1)
            mx = [bank[3][:, 256 * t:256 * t + 256].rearrange("p (g d) -> p g d", g=SGG) for t in range(TT)]
            yc = [xn[:, t, SBW + MLW:D] for t in range(TT)]
            for t in range(TT):
                ins = dve.tensor_tensor(yc[t].rearrange("p (g d) -> p g d", g=SGG), mx[t],
                                        Q("sgu_b").unsqueeze(2).broadcast_to([P, SGG, SGD]), ALU.add)
            link(ins)
            for t in range(TT):
                ins = dve.tensor_tensor(yc[t], yc[t], z[:, t, Z_UC:Z_VC], ALU.mult)
            ins.then_inc(S("yc_ready"), 1)
            dve.wait_ge(S("out_b"), 1)
            dve.wait_ge(S("ccol_ready"), 1)
            den = V("den")
            for t in range(TT):
                ins = dve.scalar_tensor_tensor(den[:, 4 * t:4 * t + 4], bank[4 + t][:, MLW:MLW + MLH], -1.0,
                                               V("ccol")[:, 8 + 4 * t:12 + 4 * t], ALU.mult, ALU.max)
            link(ins)
            for t in range(TT):
                d = den[:, 4 * t:4 * t + 4]
                ins = dve.tensor_tensor(d, bank[4 + t][:, MLW:MLW + MLH], d, ALU.max)
            link(ins)
            link(dve.reciprocal(den, den))
            hb = [xn[:, t, SBW:SBW + MLW].rearrange("p (h d) -> p h d", h=MLH) for t in range(TT)]
            for t in range(TT):
                ins = dve.tensor_tensor(hb[t], bank[4 + t][:, 0:MLW].rearrange("p (h d) -> p h d", h=MLH),
                                        den[:, 4 * t:4 * t + 4].unsqueeze(2).broadcast_to([P, MLH, MLD]), ALU.mult)
            ins.then_inc(S("hb_ready"), 1)
            dve.wait_ge(S("hb_squares"), 1)
            dve.tensor_reduce(V("ssb"), tmp.rearrange("p (g d) -> p g d", d=MLD), AX.X, ALU.add)\
               .then_inc(S("hb_sums"), 1)
            dve.wait_ge(S("hb_ready"), 1)
            for t in range(TT):
                ins = dve.tensor_tensor(xn[:, t, SBW:SBW + MLW], xn[:, t, SBW:SBW + MLW], z[:, t, Z_OB:Z_UC], ALU.mult)
            link(ins)
            dve.wait_ge(S("hb_rstd"), 1)
            for t in range(TT):
                ins = dve.tensor_tensor(hb[t], hb[t],
                                        V("rsb")[:, 4 * t:4 * t + 4].unsqueeze(2).broadcast_to([P, MLH, MLD]), ALU.mult)
            ins.then_inc(S("xn0_ready"), 1)
            turn_dve(1)
            add_chunks(U_WOUT, C_WOUT)
            norm_dve(1)
            for b in range(4, 8):
                dve.memset(bank[b][:], 0.0)
            turn_dve(2)
            dve.wait_ge(S("router_done"), 1)
            lg = V("lg").rearrange("p (a n) -> p a n", a=TT)
            two = lambda v: v.rearrange("p (a n) -> p a n", a=TT)
            over = lambda v, n: v.unsqueeze(2).broadcast_to([P, TT, n])
            same = lambda v, n: v.unsqueeze(1).broadcast_to([P, TT, n])
            NR = NG + NE
            link(dve.tensor_tensor(lg, bank[0][:, 0:2 * NR].rearrange("p (a n) -> p a n", a=TT),
                                   same(Q("router_b"), NR), ALU.add))
            gmax, eqg, ohg, idx = V("gmax"), two(V("eqg")), two(V("ohg")), V("idx")

            def one_hot(oh, scores, top, iota, n, cand):
                link(dve.tensor_reduce(top, scores, AX.X, ALU.max))
                link(dve.tensor_tensor(cand, scores, over(top, n), ALU.is_ge))
                link(dve.scalar_tensor_tensor(cand, cand, -64.0, same(iota, n), ALU.mult, ALU.add))
                link(dve.tensor_reduce(idx, cand, AX.X, ALU.min))
                link(dve.tensor_tensor(oh, cand, over(idx, n), ALU.is_equal))

            one_hot(ohg, lg[:, :, 0:NG], gmax, C("iota4"), NG, eqg)
            eg = two(V("eg"))
            dve.tensor_tensor(eg, lg[:, :, 0:NG], over(gmax, NG), ALU.subtract).then_inc(S("gdiff_ready"), 1)
            link(dve.tensor_scalar(V("pen"), V("ohg"), BIG, -BIG, ALU.mult, ALU.add))
            em, em4 = two(V("em")), V("em").rearrange("p (a g e) -> p a g e", a=TT, g=NG)
            pen = V("pen").rearrange("p (a g) -> p a g", a=TT)
            for t in range(TT):
                ins = dve.tensor_tensor(em4[:, t], lg[:, t, NG:NR].rearrange("p (g e) -> p g e", g=NG),
                                        ohg[:, t, :].unsqueeze(2).broadcast_to([P, NG, EPG]), ALU.mult)
            link(ins)
            for t in range(TT):
                ins = dve.tensor_tensor(em4[:, t], em4[:, t],
                                        pen[:, t, :].unsqueeze(2).broadcast_to([P, NG, EPG]), ALU.add)
            link(ins)
            oh1, oh2, cand = two(V("oh1")), two(V("oh2")), two(V("cand"))
            v1, v2, dv = V("v1"), V("v2"), V("dv")
            one_hot(oh1, em, v1, C("iota32"), NE, cand)
            link(dve.scalar_tensor_tensor(V("em"), V("oh1"), -2.0 * BIG, V("em"), ALU.mult, ALU.add))
            one_hot(oh2, em, v2, C("iota32"), NE, cand)
            dve.tensor_tensor(dv, v2, v1, ALU.subtract).then_inc(S("vdiff_ready"), 1)
            dve.tensor_tensor(V("sel"), V("oh1"), V("oh2"), ALU.add).then_inc(S("sel_ready"), 1)
            dve.wait_ge(S("xtok_high"), 1)
            dve.tensor_tensor(xtok_lo, xn[:], xtok_hi.bitcast(F32), ALU.subtract).then_inc(S("xtok_ready"), 1)
            dve.wait_ge(S("rank_done"), 1)
            link(dve.scalar_tensor_tensor(V("key"), bank[0][:, 128:192], 1.0, V("sel"), ALU.add, ALU.mult))
            dve.tensor_scalar(V("key"), V("key"), -1.0, None, ALU.add).then_inc(S("key_ready"), 1)
            dve.wait_ge(S("key_ready"), 1)
            link(dve.tensor_scalar(V("over"), V("key"), float(SLOTS), None, ALU.is_ge))
            dve.tensor_reduce(V("spill"), V("over"), AX.X, ALU.add).then_inc(S("spill_ready"), 1)
            dve.wait_ge(S("gexp_ready"), 1)
            gw, p1, p2 = V("gw"), V("p1"), V("p2")
            link(dve.tensor_reduce(gw, eg, AX.X, ALU.add))
            dve.wait_ge(S("vexp_ready"), 1)
            link(dve.scalar_tensor_tensor(p1, dv, 1.0, gw, ALU.add, ALU.mult))
            link(dve.reciprocal(p1, p1))
            link(dve.tensor_tensor(p2, p1, dv, ALU.mult))
            dve.tensor_tensor(oh1, oh1, over(p1, NE), ALU.mult)
            link(dve.tensor_tensor(oh2, oh2, over(p2, NE), ALU.mult))
            dve.tensor_tensor(oh1, oh1, oh2, ALU.add).then_inc(S("wt_ready"), 1)
            dve.wait_ge(S("wt_ready"), 1)
            dve.tensor_tensor(V("over"), V("over"), V("oh1"), ALU.mult).then_inc(S("over_ready"), 1)
            dve.wait_ge(S("spill_summed"), 1)
            dve.tensor_copy(spill_count[:], bank[0][0:1, 256:257]).then_inc(S("spill_known"), 1)

            def pick_pair(p, p0):
                b = p0 % 2
                if p0 >= 2:
                    dve.wait_ge(S("pickw_ready"), p - 1)
                two = slice(2 * p, 2 * p + 2) if isinstance(p, int) else bass.ds(2 * p, 2)
                key = V("key").rearrange("p (a e) -> p a e", a=TT)[:, :, two].unsqueeze(3)
                iota = C("iota64").unsqueeze(1)
                for t in range(TT):
                    ins = dve.tensor_tensor(pick[:, b, t], iota.broadcast_to([P, 2, SLOTS]),
                                            key[:, t].broadcast_to([P, 2, SLOTS]), ALU.is_equal)
                ins.then_inc(S("pick_ready"), 1)

            def gather_low(k0, wait):
                dve.wait_ge(S("gather_high"), wait)
                for k in range(4):
                    o = lambda x: x[:, k0 + k, :].rearrange("p (c s) -> p c s", s=SLOTS)[:, 0:3:2, :]
                    ins = dve.scalar_tensor_tensor(o(xglo), bank[1][:, P * k:P * k + P]
                                                   .rearrange("p (c s) -> p c s", s=SLOTS),
                                                   Q("g2")[:, k0 + k:k0 + k + 1], o(xghi).bitcast(F32), ALU.mult,
                                                   ALU.subtract)
                ins.then_inc(S("gather_ready"), 1)

            def turned_low(p, b):
                dve.wait_ge(S("turned_high"), p + 1)
                dve.tensor_tensor(slo[:, b, :], bank[1][:, 0:T], shi[:, b, :].bitcast(F32), ALU.subtract)
                for f in range(2):
                    o = lambda x: x[:, f, :].rearrange("p (c s) -> p c s", s=SLOTS)[:, 0:3:2, :]
                    ins = dve.tensor_tensor(o(htlo), bank[1][:, T + P * f:T + P * f + P]
                                            .rearrange("p (c s) -> p c s", s=SLOTS), o(hthi).bitcast(F32),
                                            ALU.subtract)
                ins.then_inc(S("turned_ready"), 1)

            def y_low(p):
                dve.wait_ge(S("y_high"), p + 1)
                for c in range(2):
                    y = slice(512 * c, 512 * c + 512)
                    ins = dve.tensor_tensor(ylo[:, y], bank[2 + c][:], yhi[:, y].bitcast(F32), ALU.subtract)
                ins.then_inc(S("y_pair"), 1)

            def hidden(p):
                dve.wait_ge(S("pair_silu"), p + 1)
                dve.tensor_tensor(hv, sgl, bank[0][:, 256:512], ALU.mult).then_inc(S("hidden_ready"), 1)

            def pair_dve(p, p0, off):
                n = U_MOE + 6 * p0 - 2
                ahead = (lambda k: split_to(n + k)) if off is None else (lambda k: split((n + k, off)))
                ahead(2)
                turned_low(p - 1, (p0 - 1) % 2)
                if p0 < PAIRS - 1:
                    pick_pair(p + 1, p0 + 1)
                ahead(3)
                ahead(4)
                ahead(5)
                hidden(p)
                if p0 < PAIRS - 1:
                    gather_low(0, 2 * p + 3)
                ahead(6)
                if p0 < PAIRS - 1:
                    gather_low(4, 2 * p + 4)
                ahead(7)
                y_low(p - 1)

            dve.wait_ge(S("key_ready"), 1)
            pick_pair(0, 0)
            pick_pair(1, 1)
            dve.wait_ge(S("zeros_ready"), 1)
            gather_low(0, 1)
            gather_low(4, 2)
            split_to(U_MOE + 5)
            hidden(0)
            gather_low(0, 3)
            gather_low(4, 4)
            pair_dve(1, 1, None)
            with dve.Fori(0, (PAIRS - 4) // 2) as j:
                for b in range(2):
                    pair_dve(2 * j + (2 + b), 2 + b, 4 * j)
            done[0] = U_MOE + 6 * (PAIRS - 2)
            pair_dve(PAIRS - 2, PAIRS - 2, None)
            pair_dve(PAIRS - 1, PAIRS - 1, None)
            turned_low(PAIRS - 1, (PAIRS - 1) % 2)
            y_low(PAIRS - 1)
            dve.wait_ge(S("scattered"), 1)
            overflow_dve(dve)
            add_down(U_MOE + 3 * NE)
            norm_dve(2)
            turn_dve(3)
            dve.wait_ge(S("p_high"), 1)
            dve.tensor_tensor(plo, p_t, phi.bitcast(F32), ALU.subtract).then_inc(S("p_split"), 1)
            split_to(U_PLEP + 2)
            for c in range(2):
                dve.wait_ge(*((S("proj_half"), 1) if c == 0 else (S("unit_used"), U_PLEP + 1)))
                dve.wait_ge(S("act_freed"), sum(BY_ACT[:C_PLEG + c + 1]))
                for t in range(TT):
                    ins = dve.tensor_tensor(gpr[:, t, :], gsb[:, t, 512 * c:512 * c + 512],
                                            bank[2 * ((C_PLEP + c) % 2) + t][:], ALU.mult)
                ins.then_inc(S("dve_freed"), 1)
                dve.wait_ge(S("dve_freed"), sum(BY_DVE[:C_PLEP + c + 1]))
                for t in range(TT):
                    r = xres[:, t, 512 * c:512 * c + 512]
                    ins = dve.tensor_tensor(r, gpr[:, t, :], r, ALU.add)
                if c == 0:
                    link(ins)
            ins.then_inc(S("residual_ready"), 1)
            dve.wait_ge(S("residual_ready"), R_PLE)
            split_to(U_SCIN + 1)
            dve.wait_ge(S("rstd_ready"), 4)
            dve.wait_ge(S("final1_loaded"), 16)
            for t in range(TT):
                ins = dve.scalar_tensor_tensor(xres[:, t, :], xres[:, t, :], rstd[:, t:t + 1], final_g,
                                               ALU.mult, ALU.mult)
            ins.then_inc(S("residual_ready"), 1)
            dve.wait_ge(S("residual_ready"), R_FINAL1)
            norm_dve(4)
            link(dve.memset(cvp[:, :, 0:2], 0.0))
            turn_dve(4)
            for i in range(6):
                split_to(U_SCIN + 2 * i + 3)
                g = G_SC + i
                dve.wait_ge(S("unit_used"), U_SCIN + 2 * i + 2)
                if i < 4:
                    dve.wait_ge(S("c_ready"), i + 1)
                    dve.tensor_tensor(cvp[:, 2 * i:2 * i + 2, 2:2 + T],
                                      csb[:, i % 2, :].rearrange("p (j t) -> p j t", j=2),
                                      bank[2 * (g % 2) + 1][:].rearrange("p (j t) -> p j t", j=2), ALU.mult)\
                       .then_inc(S("g_free"), 1)
                    dve.wait_ge(S("g_free"), g + 1)
                    dve.wait_ge(S("sc_begun"), i + 1)
                    for k in range(1, -1, -1):
                        for f in range(2 * i, 2 * i + 2):
                            ins = dve.scalar_tensor_tensor(scy[:, f, :], cvp[:, f, k:k + T], sc_conv[:, k, f:f + 1],
                                                           scy[:, f, :], ALU.mult, ALU.add)
                        link(ins)
                else:
                    f = 4 * (i - 4)
                    for k in range(2):
                        y = scy[:, f + 2 * k:f + 2 * k + 2, :]
                        dve.tensor_tensor(y, y, bank[2 * (g % 2) + k][:].rearrange("p (j t) -> p j t", j=2), ALU.mult)\
                           .then_inc(S("sc_product") if k == 0 else S("g_free"), 1)
            for f in range(4):
                dve.wait_ge(S("sc_high"), f + 1)
                dve.tensor_tensor(xlo[:, 2 * f:2 * f + 2, :], scy[:, 2 * f:2 * f + 2, :],
                                  xhi[:, 2 * f:2 * f + 2, :].bitcast(F32), ALU.subtract).then_inc(S("sc_ready"), 1)
            add_chunks(U_SCOUT, C_SCOUT)

            def ffn_dve(layer, e, off, e0):
                g0, d0, u0 = (G_FFN0, 0, U_FFN0) if layer == 0 else (G_FFN1, FE, U_FFN1)
                b, gb = e0 % 2, (g0 + e0) % 2
                n = u0 + 3 * e0 - 1

                def ahead(k):
                    if off is None:
                        split_to(n + k)
                    elif n + k < UNITS:
                        split((n + k, off))
                ahead(3)
                dve.wait_ge(S("ffn_begun"), layer * FE + 1 + e)
                for k in range(1, -1, -1):
                    for f in range(4):
                        src = bank[2 * gb + f // 2][:, (f % 2) * T:(f % 2 + 1) * T]
                        a = facc[:, b, f, 2 - k:T]
                        ins = dve.scalar_tensor_tensor(a, src[:, 0:T - 2 + k], cwn[:, b, 4 * k + f:4 * k + f + 1], a,
                                                       ALU.mult, ALU.add)
                    if k == 1:
                        link(ins)
                ins.then_inc(S("g_free"), 1)
                ahead(4)
                dve.wait_ge(S("g_free"), g0 + 1 + e)
                dve.wait_ge(S("silu_ready"), layer * FE + 1 + e)
                dve.tensor_tensor(facc[:, b, 2:4, :], facc[:, b, 0:2, :], facc[:, b, 2:4, :], ALU.mult)\
                   .then_inc(S("hv_ready"), 1)
                ahead(5)
                dve.wait_ge(S("hhi_ready"), d0 + 1 + e)
                dve.tensor_tensor(hlo[:, b, :, :], facc[:, b, 2:4, :], hhi[:, b, :, :].bitcast(F32), ALU.subtract)\
                   .then_inc(S("h_ready"), 1)

            def ffn(layer):
                ffn_dve(layer, 0, None, 0)
                ffn_dve(layer, 1, None, 1)
                u0 = U_FFN0 if layer == 0 else U_FFN1
                with dve.Fori(0, (FE - 3) // 2) as j:
                    chain.enter(j, 2)
                    for b in range(2):
                        ffn_dve(layer, 2 * j + (2 + b), 2 * j, 2 + b)
                    chain.leave(2, (FE - 3) // 2)
                done[0] = u0 + 3 * (FE - 1) + 2
                ffn_dve(layer, FE - 1, None, FE - 1)

            norm_dve(5)
            turn_dve(5)
            ffn(0)
            add_down(U_FFN0 + 3 * FE)
            norm_dve(6)
            turn_dve(6)
            cos = C("cos").rearrange("p (a n) -> p a n", a=TT)
            sin = C("sin").rearrange("p (a n) -> p a n", a=TT)
            rot = rp.rearrange("p k (h n) -> p k h n", h=8)
            for c in range(4):
                split_to(U_QKV + 2 * c + 3)
                dve.wait_ge(S("unit_used"), CHUNK_END[C_QKV + c])
                for t in range(TT):
                    src = bank[2 * ((C_QKV + c) % 2) + t][:].rearrange("p (h n) -> p h n", h=8)
                    dst = qkv[:, t, 512 * c:512 * c + 512].rearrange("p (h n) -> p h n", h=8)
                    cb = cos[:, t, :].unsqueeze(1).broadcast_to([P, 8, HALF])
                    sb_ = sin[:, t, :].unsqueeze(1).broadcast_to([P, 8, HALF])
                    x1, x2 = src[:, :, 0:HALF], src[:, :, HALF:HD]
                    dve.tensor_tensor(rot[:, 0], x1, cb, ALU.mult)
                    dve.tensor_tensor(rot[:, 1], x2, sb_, ALU.mult)
                    dve.tensor_tensor(rot[:, 2], x2, cb, ALU.mult)
                    link(dve.tensor_tensor(rot[:, 3], x1, sb_, ALU.mult))
                    dve.tensor_tensor(dst[:, :, 0:HALF], rot[:, 0], rot[:, 1], ALU.subtract)
                    ins = dve.tensor_tensor(dst[:, :, HALF:HD], rot[:, 2], rot[:, 3], ALU.add)
                    if t == 0:
                        link(ins)
                ins.then_inc(S("dve_freed"), 1)
                dve.wait_ge(S("dve_freed"), sum(BY_DVE[:C_QKV + c + 1]))
            split_to(U_WO + 2)
            for b in range(1, 8, 2):
                dve.wait_ge(S("qk_turned"), b + 1)
                dve.tensor_copy(qkt_flat[:, 512 * b:512 * b + 512], bank[b][:]).then_inc(S("qkt_dve"), 1)

            def attend_norm(h):
                b = h % 2
                dve.wait_ge(S("exp_done"), h + 1)
                link(dve.reciprocal(V("rl")[:, 2 * b:2 * b + 2], V("l")[:, 2 * b:2 * b + 2]))
                dve.tensor_scalar(ap_[:, b, 0:128], ap_[:, b, 0:128], V("rl")[:, 2 * b:2 * b + 1], None, ALU.mult)
                dve.tensor_scalar(ap_[:, b, 128:384], ap_[:, b, 128:384], V("rl")[:, 2 * b + 1:2 * b + 2], None,
                                  ALU.mult).then_inc(S("p_ready"), 1)

            for h in range(NH):
                b = h % 2
                dve.wait_ge(S("scores_done"), h + 1)
                dve.tensor_tensor(bank[b][:, 0:128], bank[b][:, 0:128], C("causal"), ALU.add)
                link(dve.tensor_tensor(bank[b][:, 256:384], bank[b][:, 256:384], C("causal"), ALU.add))
                dve.tensor_reduce(V("m")[:, 2 * b:2 * b + 1], bank[b][:, 0:128], AX.X, ALU.max)
                link(dve.tensor_reduce(V("m")[:, 2 * b + 1:2 * b + 2], bank[b][:, 128:384], AX.X, ALU.max))
                dve.tensor_scalar(V("nm")[:, 2 * b:2 * b + 2], V("m")[:, 2 * b:2 * b + 2], -(HD ** -0.5), None,
                                  ALU.mult).then_inc(S("negmax_ready"), 1)
                if h >= 1:
                    attend_norm(h - 1)
            attend_norm(NH - 1)
            for b in range(4):
                dve.wait_ge(S("o_high"), b + 1)
                dve.tensor_tensor(xlo[:, 2 * b:2 * b + 2, :], bank[4 + b][:].rearrange("p (j t) -> p j t", j=2),
                                  xhi[:, 2 * b:2 * b + 2, :].bitcast(F32), ALU.subtract).then_inc(S("o_ready"), 1)
            add_chunks(U_WO, C_WO)
            norm_dve(7)
            turn_dve(7)
            ffn(1)
            add_down(UNITS)
            dve.wait_ge(S("residual_ready"), R_FFN1)
            dve.wait_ge(S("rstd_ready"), 9)
            dve.wait_ge(S("final2_loaded"), 16)
            for t in range(TT):
                ins = dve.scalar_tensor_tensor(xn[:, t, :], xres[:, t, :], rstd[:, t:t + 1], final_g,
                                               ALU.mult, ALU.mult)
            ins.then_inc(S("y_ready"), 1)

        @block.tensor
        def _(pe):
            def wait_unit(n):
                unit0, off = n if isinstance(n, tuple) else (n, 0)
                pe.wait_ge(S("low_done"), (off if isinstance(off, int) else off * RING) + unit0 + 1)
                return unit0 % RING

            def mm3(o, ah, al, bh, bl, start, stop=False):
                pe.matmul(o, ah, bh, start=start, stop=False, skip_group_check=True)
                pe.matmul(o, ah, bl, start=False, stop=False, skip_group_check=True)
                return pe.matmul(o, al, bh, start=False, stop=stop, skip_group_check=True)

            def turn(q):
                pe.wait_ge(S("xn0_ready"), q + 1)
                pe.wait_ge(S("xn1_ready"), q + 1)
                for k in range(KD):
                    for t in range(TT):
                        ins = pe.transpose(bank[k // 2][:, (k % 2) * T + t * P:(k % 2) * T + t * P + P],
                                           xn[:, t, P * k:P * k + P], ident)
                    if k % 2:
                        ins.then_inc(S("turned"), 1)
                pe.wait_ge(S("xt_ready"), 4 * (q + 1))

            def dense(g, u0, width=512):
                if g >= 2:
                    if sum(BY_ACT[:g - 1]):
                        pe.wait_ge(S("act_freed"), sum(BY_ACT[:g - 1]))
                    pe.wait_ge(S("dve_freed"), sum(BY_DVE[:g - 1]))
                for u in range(2):
                    s = wait_unit(u0 + u)
                    for k in range(4):
                        kk = 4 * u + k
                        for t in range(TT):
                            w = slice(512 * k, 512 * k + 512)
                            ins = mm3(bank[2 * (g % 2) + t][:], xhi[:, kk, P * t:P * t + P], xlo[:, kk, P * t:P * t + P],
                                      whi[:, s, w], wlo[:, s, w], start=kk == 0, stop=kk == 7)
                    ins.then_inc(S("unit_used"), 1)

            pe.wait_ge(S("table_loaded"), 16)
            pe.wait_ge(S("params_loaded"), 16)
            turn(0)
            for c in range(6):
                dense(C_WIN + c, U_WIN + 2 * c)
            pe.wait_ge(S("act_freed"), 5)
            pe.wait_ge(S("dve_freed"), 5)
            s = wait_unit(12)
            for k in range(KD):
                for t in range(TT):
                    w = slice(TAIL * k, TAIL * k + TAIL)
                    ins = mm3(bank[t][:, 0:TAIL], xhi[:, k, P * t:P * t + P], xlo[:, k, P * t:P * t + P],
                              whi[:, s, w], wlo[:, s, w], start=k == 0, stop=k == 7)
            ins.then_inc(S("unit_used"), 1)
            pe.wait_ge(S("act_freed"), 7)
            pe.wait_ge(S("dve_freed"), 7)
            for j in range(6):
                for t in range(TT):
                    at = j * T + t * P
                    ins = pe.transpose(bank[4 + at // 512][:, at % 512:at % 512 + P], z[:, t, P * j:P * j + P], ident)
                if j % 2:
                    ins.then_inc(S("turned_a"), 1)
            for j in range(8):
                for t in range(TT):
                    ins = pe.transpose(bank[(7, 0, 1, 2)[j // 2]][0:MLD, (j % 2) * T + t * P:(j % 2) * T + t * P + P],
                                       z[:, t, Z_QB + MLD * j:Z_QB + MLD * j + MLD], ident)
                if j % 2:
                    ins.then_inc(S("turned_b"), 1)
            pe.wait_ge(S("qka_act"), 2)
            pe.wait_ge(S("qka_dve"), 1)
            for h in range(SBH):
                p0 = 64 * (h % 2)
                q_, k_ = qka[p0:p0 + 64, h // 2, :], qka[p0:p0 + 64, 3 + h // 2, :]
                if h == 4:
                    pe.wait_ge(S("cvb_act"), 2)
                b = bank[(3, 4, 5, 6, 7, 0)[h]]
                pe.matmul(b[:, 0:256], k_[:, 0:P], q_, start=True, stop=True, skip_group_check=True)
                pe.matmul(b[:, 256:384], k_[:, P:T], q_[:, P:T], start=True, stop=True, skip_group_check=True)\
                  .then_inc(S("scores_a"), 1)
            pe.wait_ge(S("logf_ready"), 1)
            pe.wait_ge(S("cvb_dve"), 2)
            lf = V("lf").rearrange("p (a n) -> p a n", a=TT)
            gt = V("gt").rearrange("p (a n) -> p a n", a=TT)
            upto, ones, later = C("upto"), C("ones"), C("later")
            r = bank[1][0:MLH, :]
            pe.matmul(r[:, 0:P], lf[:, 0, :], upto, start=True, stop=True, skip_group_check=True)
            pe.matmul(r[:, P:T], lf[:, 0, :], ones, start=True, stop=False, skip_group_check=True)
            pe.matmul(r[:, P:T], lf[:, 1, :], upto, start=False, stop=True, skip_group_check=True)
            pe.transpose(r[:, T:T + P], gt[:, 0, 0:4], ident)
            pe.transpose(r[:, T + P:2 * T], gt[:, 1, 0:4], ident).then_inc(S("brow_done"), 1)
            pe.wait_ge(S("l_ready"), 1)
            for h in range(SBH):
                b = bank[(3, 4, 5, 6, 7, 0)[h]]
                l = t1_flat[:, 384 * h:384 * h + 384]
                pe.matmul(b[:, 0:384], later, l, start=True, stop=False, skip_group_check=True)
                pe.matmul(b[:, 128:256], ones, l[:, 256:384], start=False, stop=True, skip_group_check=True)\
                  .then_inc(S("after_a"), 1)
            pe.wait_ge(S("mrow_ready"), 1)
            pe.wait_ge(S("enrow_ready"), 1)
            for t in range(TT):
                pe.transpose(bank[2][:, 4 * t:4 * t + 4], rows[1][:, P * t:P * t + P], ident[0:4, 0:4])
                ins = pe.transpose(bank[2][:, 8 + 4 * t:12 + 4 * t], rows[4][:, P * t:P * t + P], ident[0:4, 0:4])
            ins.then_inc(S("cols_done"), 1)
            pe.wait_ge(S("expo_ready"), 1)
            for h in range(MLH):
                ins = pe.matmul(bank[3 + 4 * (h // 2)][:, (h % 2) * T:(h % 2 + 1) * T],
                                ident[0:4, h:h + 1].broadcast_to([4, P]), rows[2], start=True, stop=True,
                                skip_group_check=True)
            ins.then_inc(S("mbc_done"), 1)
            pe.wait_ge(S("qkb_ready"), 1)
            pe.wait_ge(S("mw_ready"), 1)
            for h in range(MLH):
                b = bank[(4, 5, 6, 7)[h]]
                q_, k_ = qkb[:, h, :], qkb[:, 4 + h, :]
                pe.matmul(b[:, 0:256], k_[:, 0:P], q_, start=True, stop=True, skip_group_check=True)
                pe.matmul(b[:, 256:384], k_[:, P:T], q_[:, P:T], start=True, stop=True, skip_group_check=True)\
                  .then_inc(S("scores_b"), 1)
            pe.wait_ge(S("ln_ready"), 1)
            pe.wait_ge(S("sgu_masked"), 1)
            for t in range(TT):
                for g in range(SGG):
                    ins = pe.matmul(bank[3][:, 256 * t + 64 * g:256 * t + 64 * g + 64], sgu_w[:, g, :],
                                    z[:, t, Z_VC + 64 * g:Z_VC + 64 * g + 64], start=True, stop=True,
                                    skip_group_check=True)
            ins.then_inc(S("mixed_done"), 1)
            pe.wait_ge(S("a_ready"), 1)
            pe.wait_ge(S("ccol_ready"), 1)
            for h in range(SBH):
                v = [z[:, t, 2 * SBW + 64 * h:2 * SBW + 64 * h + 64] for t in range(TT)]
                o = [bank[1 + t][:, 64 * h:64 * h + 64] for t in range(TT)]
                pe.matmul(o[0], sa[:, h, 0, :], v[0], start=True, stop=True, skip_group_check=True)
                pe.matmul(o[1], sa[:, h, 1, :], v[0], start=True, stop=False, skip_group_check=True)
                ins = pe.matmul(o[1], sa[:, h, 2, :], v[1], start=False, stop=True, skip_group_check=True)
            ins.then_inc(S("out_a"), 1)
            pe.wait_ge(S("s_ready"), 4)
            for h in range(MLH):
                v = [z[:, t, Z_VB + MLD * h:Z_VB + MLD * h + MLD] for t in range(TT)]
                for vv, a, w in ((v, MLD * h, MLD), ([ones[:, 0:1]] * 2, MLW + h, 1)):
                    pe.matmul(bank[4][:, a:a + w], mwh[h][:, 0, :], vv[0], start=True, stop=True, skip_group_check=True)
                    pe.matmul(bank[5][:, a:a + w], mwh[h][:, 1, :], vv[0], start=True, stop=False, skip_group_check=True)
                    ins = pe.matmul(bank[5][:, a:a + w], mwh[h][:, 2, :], vv[1], start=False, stop=True,
                                    skip_group_check=True)
            ins.then_inc(S("out_b"), 1)
            turn(1)
            for c in range(2):
                dense(C_WOUT + c, U_WOUT + 2 * c)
            turn(2)
            pe.wait_ge(S("setup_low"), 1)
            NR = NG + NE
            for t in range(TT):
                for k in range(KD):
                    ins = mm3(bank[0][:, NR * t:NR * t + NR], xhi[:, k, P * t:P * t + P], xlo[:, k, P * t:P * t + P],
                              rhi[:, k, :], rlo[:, k, :], start=k == 0, stop=k == 7)
            ins.then_inc(S("router_done"), 1)
            pe.wait_ge(S("sel_ready"), 1)
            sel = V("sel").rearrange("p (a n) -> p a n", a=TT)
            strict = C("strict")
            pe.matmul(bank[0][:, 128:160], strict, sel[:, 0, :], start=True, stop=True, skip_group_check=True)
            pe.matmul(bank[0][:, 160:192], ones, sel[:, 0, :], start=True, stop=False, skip_group_check=True)
            pe.matmul(bank[0][:, 160:192], strict, sel[:, 1, :], start=False, stop=True, skip_group_check=True)\
              .then_inc(S("rank_done"), 1)
            pe.wait_ge(S("spill_ready"), 1)
            pe.matmul(bank[0][0:1, 256:257], V("spill"), ones[:, 0:1], start=True, stop=True, skip_group_check=True)\
              .then_inc(S("spill_summed"), 1)

            def gather(q0, p, k0):
                if k0 == 0:
                    pe.wait_ge(S("pick_ready"), p + 1)
                b = q0 % 2
                for k in range(4):
                    o = bank[1][:, P * k:P * k + P]
                    w = slice(P * (k0 + k), P * (k0 + k) + P)
                    for t in range(TT):
                        sl = pick[:, b, t].rearrange("p e s -> p (e s)")
                        pe.matmul(o, xtok_hi[:, t, w], sl, start=t == 0, stop=False, skip_group_check=True)
                        ins = pe.matmul(o, xtok_lo[:, t, w], sl, start=False, stop=t == 1, skip_group_check=True)
                ins.then_inc(S("gathered"), 1)

            def pair_gate_up(e, u):
                unit0, off = u
                w = slice(SLOTS * e, SLOTS * e + P)
                for i in range(2):
                    s = wait_unit((unit0 + i, off))
                    for k in range(4):
                        kk = 4 * i + k
                        c = slice(512 * k, 512 * k + 512)
                        ins = mm3(bank[0][:], xghi[:, kk, w], xglo[:, kk, w], whi[:, s, c], wlo[:, s, c],
                                  start=e == 0 and kk == 0)
                    ins.then_inc(S("unit_used"), 1)

            def pair_down(e, u):
                s = wait_unit(u)
                w = slice(SLOTS * e, SLOTS * e + P)
                for c in range(2):
                    for f in range(2):
                        v = slice(D * f + 512 * c, D * f + 512 * c + 512)
                        ins = mm3(bank[2 + c][:], hthi[:, f, w], htlo[:, f, w], whi[:, s, v], wlo[:, s, v],
                                  start=e == 0 and f == 0)
                ins.then_inc(S("unit_used"), 1)

            def scatter(p, p0, last=False):
                pe.wait_ge(S("y_pair"), p + 1)
                b = p0 % 2
                for t in range(TT):
                    for c in range(2):
                        y = slice(512 * c, 512 * c + 512)
                        a = slice(P * t, P * t + P)
                        ins = mm3(bank[4 + 2 * t + c][:], shi[:, b, a], slo[:, b, a], yhi[:, y], ylo[:, y],
                                  start=False)
                if last:
                    ins.then_inc(S("scattered"), 1)

            def turn_pair(p, p0):
                pe.wait_ge(S("hidden_ready"), p + 1)
                pe.wait_ge(S("pickw_ready"), p + 1)
                if p0 < PAIRS - 1:
                    pe.wait_ge(S("gather_ready"), 2 * p + 4)
                for t in range(TT):
                    pe.transpose(bank[1][:, P * t:P * t + P],
                                 pickw[:, p0 % 2, t].rearrange("p e s -> p (e s)"), ident)
                for f in range(2):
                    ins = pe.transpose(bank[1][:, T + P * f:T + P * f + P], hv[:, P * f:P * f + P], ident)
                ins.then_inc(S("turned_pair"), 1)

            def pair_step(p, p0, off):
                n = U_MOE + 6 * p0 - 2
                pair_gate_up(0, (n, off))
                if p0 >= 2:
                    scatter(p - 2, p0 - 2)
                pair_gate_up(1, (n + 2, off))
                pe.wait_ge(S("turned_ready"), p)
                if p0 < PAIRS - 1:
                    gather(p0 + 1, p + 1, 0)
                pair_down(0, (n + 4, off))
                if p0 < PAIRS - 1:
                    pe.wait_ge(S("gather_ready"), 2 * p + 3)
                    gather(p0 + 1, p + 1, 4)
                pair_down(1, (n + 5, off))
                turn_pair(p, p0)

            pe.wait_ge(S("xtok_ready"), 1)
            gather(0, 0, 0)
            pe.wait_ge(S("gather_ready"), 1)
            gather(0, 0, 4)
            pe.wait_ge(S("gather_ready"), 2)
            pe.wait_ge(S("spill_known"), 1)
            pair_gate_up(0, (U_MOE, 0))
            pair_gate_up(1, (U_MOE + 2, 0))
            gather(1, 1, 0)
            pe.wait_ge(S("gather_ready"), 3)
            gather(1, 1, 4)
            turn_pair(0, 0)
            pair_step(1, 1, 0)
            with pe.Fori(0, (PAIRS - 4) // 2) as j:
                for b in range(2):
                    pair_step(2 * j + (2 + b), 2 + b, 4 * j)
            pair_step(PAIRS - 2, PAIRS - 2, 0)
            pair_step(PAIRS - 1, PAIRS - 1, 0)
            scatter(PAIRS - 2, PAIRS - 2)
            pe.wait_ge(S("turned_ready"), PAIRS)
            pair_down(0, (U_MOE + 3 * NE - 2, 0))
            pair_down(1, (U_MOE + 3 * NE - 1, 0))
            scatter(PAIRS - 1, PAIRS - 1, last=True)
            overflow_pe(pe)

            def group(g0, u):
                unit0, off = u if isinstance(u, tuple) else (u, 0)
                for i in range(2):
                    s = wait_unit((unit0 + i, off))
                    for k in range(4):
                        kk = 4 * i + k
                        for f in range(4):
                            o = bank[2 * (g0 % 2) + f // 2][:, (f % 2) * T:(f % 2 + 1) * T]
                            w = slice(512 * k + P * f, 512 * k + P * f + P)
                            first = kk == 0 and f % 2 == 0
                            pe.matmul(o, whi[:, s, w], xhi[:, kk, :], start=first, stop=False, skip_group_check=True)
                            pe.matmul(o, whi[:, s, w], xlo[:, kk, :], start=False, stop=False, skip_group_check=True)
                            ins = pe.matmul(o, wlo[:, s, w], xhi[:, kk, :], start=False, stop=kk == 7,
                                            skip_group_check=True)
                    ins.then_inc(S("unit_used"), 1)

            def down(b, u, first):
                unit0, off = u if isinstance(u, tuple) else (u, 0)
                s = wait_unit(u)
                for t in range(TT):
                    for c in range(2):
                        for f in range(2):
                            w = slice(D * f + 512 * c, D * f + 512 * c + 512)
                            ins = mm3(bank[4 + 2 * t + c][:], hhi[:, b, f, P * t:P * t + P], hlo[:, b, f, P * t:P * t + P],
                                      whi[:, s, w], wlo[:, s, w], start=first and f == 0)
                ins.then_inc(S("unit_used"), 1)

            def expert_step(g0, d0, u0, e, e0, off):
                n = u0 + 2 + 3 * e0
                pe.wait_ge(S("g_free"), g0 + e)
                group(g0 + e0 + 1, (n, off))
                pe.wait_ge(S("h_ready"), d0 + 1 + e)
                down(e0 % 2, (n + 2, off), first=e0 == 0)

            def experts(g0, d0, u0, count):
                pe.wait_ge(S("g_free"), g0 - 1)
                group(g0, u0)
                expert_step(g0, d0, u0, 0, 0, 0)
                pairs = (count - 2) // 2
                with pe.Fori(0, pairs) as j:
                    for b in range(2):
                        expert_step(g0, d0, u0, 2 * j + (1 + b), 1 + b, 2 * j)
                for e in range(1 + 2 * pairs, count - 1):
                    expert_step(g0, d0, u0, e, e, 0)
                pe.wait_ge(S("h_ready"), d0 + count)
                down((count - 1) % 2, u0 + 3 * count - 1, first=False)

            turn(3)
            for c in range(2):
                dense(C_PLEG + c, U_PLEG + 2 * c)
            pe.wait_ge(S("p_split"), 1)
            s = wait_unit(U_PLEP)
            for c in range(2):
                g = C_PLEP + c
                pe.wait_ge(S("act_freed"), sum(BY_ACT[:g - 1]))
                for t in range(TT):
                    for k in range(2):
                        w = slice(D * k + 512 * c, D * k + 512 * c + 512)
                        ins = mm3(bank[2 * (g % 2) + t][:], phi[:, k, P * t:P * t + P], plo[:, k, P * t:P * t + P],
                                  whi[:, s, w], wlo[:, s, w], start=k == 0, stop=k == 1)
                ins.then_inc(S("proj_half") if c == 0 else S("unit_used"), 1)
            turn(4)
            for i in range(6):
                if i >= 2:
                    pe.wait_ge(S("g_free"), G_SC + i - 1)
                group(G_SC + i, U_SCIN + 2 * i)
            pe.wait_ge(S("sc_ready"), 4)
            for c in range(2):
                dense(C_SCOUT + c, U_SCOUT + 2 * c)
            turn(5)
            experts(G_FFN0, 0, U_FFN0, FE)
            turn(6)
            for c in range(6):
                dense(C_QKV + c, U_QKV + 2 * c)
            pe.wait_ge(S("dve_freed"), sum(BY_DVE[:C_QKV + 6]))
            pe.wait_ge(S("act_freed"), sum(BY_ACT[:C_QKV + 6]))
            for j in range(16):
                for t in range(TT):
                    ins = pe.transpose(bank[j // 2][:, (j % 2) * T + t * P:(j % 2) * T + t * P + P],
                                       qkv[:, t, P * j:P * j + P], ident)
                if j % 2:
                    ins.then_inc(S("qk_turned"), 1)
            pe.wait_ge(S("qkt_act"), 4)
            pe.wait_ge(S("qkt_dve"), 4)

            def scores(h):
                b, p0 = h % 2, 64 * (h % 2)
                q_, k_ = qkt[p0:p0 + 64, h // 2, :], qkt[p0:p0 + 64, 8 + h // 2, :]
                if h >= 2:
                    pe.wait_ge(S("exp_done"), h - 1)
                pe.matmul(bank[b][:, 0:128], q_[:, 0:P], k_[:, 0:P], start=True, stop=True, skip_group_check=True)
                pe.matmul(bank[b][:, 128:384], q_[:, P:T], k_, start=True, stop=True, skip_group_check=True)\
                  .then_inc(S("scores_done"), 1)

            def turn_p(h):
                b = h % 2
                pe.wait_ge(S("p_ready"), h + 1)
                if h >= 2:
                    pe.wait_ge(S("pt_ready"), h - 1)
                for k in range(3):
                    ins = pe.transpose(bank[2 + b][:, P * k:P * k + P], ap_[:, b, P * k:P * k + P], ident)
                ins.then_inc(S("p_turned"), 1)

            def values(h):
                b, j = h % 2, h // 2
                pe.wait_ge(S("pt_ready"), h + 1)
                v = [qkv[:, t, 2 * D + HD * h:2 * D + HD * h + HD] for t in range(TT)]
                o = bank[4 + j // 2][64 * (h % 2):64 * (h % 2) + 64, (j % 2) * T:(j % 2 + 1) * T]
                pe.matmul(o, v[0], apt[:, b, 0:256], start=True, stop=False, skip_group_check=True)
                pe.matmul(o[:, P:T], v[1], apt[:, b, 256:384], start=False, stop=True, skip_group_check=True)\
                  .then_inc(S("pv_done"), 1)

            scores(0)
            scores(1)
            for h in range(NH):
                turn_p(h)
                if h + 2 < NH:
                    scores(h + 2)
                values(h)
            pe.wait_ge(S("o_ready"), 4)
            for c in range(2):
                dense(C_WO + c, U_WO + 2 * c)
            turn(7)
            experts(G_FFN1, FE, U_FFN1, FE)


def constants():
    t = np.zeros((P, CONST_W), np.float32)

    def put(name, v):
        a, b = CONST[name]
        t[:, a:b] = np.asarray(v, np.float32).reshape(-1, b - a)

    i, j = np.arange(P)[:, None], np.arange(P)[None, :]
    put("ident", i == j)
    put("later", i > j)
    put("ones", np.ones((P, P)))
    put("upto", i <= j)
    put("strict", i < j)
    put("bigpast", np.where(i > j, BIG, 0.0))
    put("causal", np.where(j > i, -BIG, 0.0))
    inv = np.float32(10000.0) ** (-np.arange(HALF, dtype=np.float32) / np.float32(HALF))
    ang = np.arange(T, dtype=np.float32)[:, None] * inv.astype(np.float32)[None, :]
    for name, f in (("cos", np.cos), ("sin", np.sin)):
        put(name, f(ang).reshape(TT, P, HALF).transpose(1, 0, 2).reshape(P, -1))
    put("iota4", np.broadcast_to(np.arange(NG), (P, NG)))
    put("iota32", np.broadcast_to(np.arange(NE), (P, NE)))
    put("neghalf", np.full((P, 8), -0.5))
    put("iota64", np.broadcast_to(np.arange(SLOTS), (P, SLOTS)))
    return t


def rows_units(w, cols=512):
    k, n = w.shape
    per = UNIT // cols
    v = w.reshape(k // P // per, per, P, n // cols, cols)
    return v.transpose(3, 0, 2, 1, 4).reshape(-1, P, UNIT)


def expert_units(pairs, downs, together=1):
    e = pairs.shape[0]
    g = pairs.reshape(e, 2, 4, P, 512).transpose(0, 1, 3, 2, 4).reshape(e, 2, P, UNIT)
    d = downs.reshape(e, 2, P, D).transpose(0, 2, 1, 3).reshape(e, 1, P, UNIT)
    g, d = g.reshape(e // together, -1, P, UNIT), d.reshape(e // together, -1, P, UNIT)
    parts = [g[0]]
    for n in range(e // together - 1):
        parts += [g[n + 1], d[n]]
    parts.append(d[-1])
    return np.concatenate(parts)


def kernel(x, p, norm1_g, w_in, conv_w, conv_b, igate_b, fgate_b, mnorm_g, sb_out_g, sgu_ln_g, sgu_ln_b, sgu_w,
           sgu_b, sgu_out_g, w_out, norm2_g, router_gw, router_gb, router_ew, router_eb, w_gate, w_up, w_down,
           ple_norm_g, ple_gate_w, ple_proj_w, final_g, mix_norm_2, sc_w_in_2, sc_w_conv_2, sc_w_out_2, moba_w_qkv_2,
           moba_w_o_2, ffn_norm_2, ffn_w_up_2, ffn_w_conv_2, ffn_w_down_2, final_norm_2):
    import concourse.bacc as _bacc
    from concourse.bass_utils import run_bass_kernel_spmd as _run

    w = w_in[0]
    g0 = 3 * SBW + 4 * MLW
    w = np.concatenate([w[:, :g0], w[:, g0 + GATES:], w[:, g0:g0 + GATES]], axis=1)
    tail = w[:, 6 * 512:].reshape(KD, P, TAIL).transpose(1, 0, 2).reshape(P, KD * TAIL)
    tail = np.concatenate([tail, np.zeros((P, UNIT - KD * TAIL), w.dtype)], axis=1)[None]

    sc = sc_w_in_2[0]
    b_, c_, v_ = sc[:, :D], sc[:, D:2 * D], sc[:, 2 * D:]
    sc_cols = [np.concatenate([c_[:, 256 * i:256 * i + 256], v_[:, 256 * i:256 * i + 256]], axis=1) for i in range(4)]
    sc_cols = np.concatenate(sc_cols + [b_], axis=1)

    def ffn_units(layer):
        up = ffn_w_up_2[layer]
        pairs = np.concatenate([up[:, :FF].reshape(D, FE, 256), up[:, FF:].reshape(D, FE, 256)], axis=2)
        return expert_units(pairs.transpose(1, 0, 2), ffn_w_down_2[layer].reshape(FE, 256, D))

    stream = np.concatenate([
        rows_units(w[:, :6 * 512]), tail, rows_units(w_out[0]),
        expert_units(np.concatenate([w_gate[0], w_up[0]], axis=2), w_down[0], 2),
        rows_units(ple_gate_w[0]), ple_proj_w[0].reshape(2, P, D).transpose(1, 0, 2).reshape(1, P, UNIT),
        rows_units(sc_cols), rows_units(sc_w_out_2[0]), ffn_units(0),
        rows_units(moba_w_qkv_2[0]), rows_units(moba_w_o_2[0]), ffn_units(1)])

    prm = np.zeros((P, PARAM_W), np.float32)

    def put(name, v, rows=P):
        a, b = PARAM[name]
        prm[:rows, a:b] = v.reshape(-1, b - a)

    def cols(v):
        return v.reshape(-1, P).T

    put("g0", cols(norm1_g[0]))
    put("g1", cols(np.concatenate([sb_out_g[0], mnorm_g[0], sgu_out_g[0]])))
    put("g2", cols(norm2_g[0]))
    put("g3", cols(ple_norm_g[0]))
    put("g4", cols(mix_norm_2[0]))
    put("g5", cols(ffn_norm_2[0]))
    put("g6", cols(mix_norm_2[1]))
    put("g7", cols(ffn_norm_2[1]))
    put("gates_b", np.concatenate([igate_b[0], fgate_b[0]]))
    put("conv_w", conv_w[0].reshape(CONV_K, 8, MLD).transpose(2, 1, 0).reshape(MLD, -1), MLD)
    put("conv_b", conv_b[0].reshape(8, MLD).T, MLD)
    put("ln_g", sgu_ln_g[0])
    put("ln_b", sgu_ln_b[0])
    put("sgu_b", sgu_b[0].T)
    put("sgu_w", sgu_w[0].transpose(2, 0, 1).reshape(P, -1))
    put("router_b", np.concatenate([router_gb[0], router_eb[0]]))
    put("router_w", np.concatenate([router_gw[0], router_ew[0]], axis=1).reshape(KD, P, NG + NE)
        .transpose(1, 0, 2).reshape(P, -1))
    put("sc_conv", sc_w_conv_2[0].reshape(3, SCB, P).transpose(2, 0, 1).reshape(P, -1))
    fc = ffn_w_conv_2.reshape(2, 3, 2, FE, 2, P)
    put("ffn_conv", fc.transpose(5, 0, 3, 1, 2, 4).reshape(P, -1))
    p_in = p[0, 0].T.reshape(2, P, T).transpose(1, 0, 2)
    finals = np.stack([np.broadcast_to(final_g, (P, D)), np.broadcast_to(final_norm_2, (P, D))])
    x_in = x[0].reshape(TT, P, D).transpose(1, 0, 2)

    nc = _bacc.Bacc("TRN2", target_bir_lowering=False, num_devices=1)
    arrays = {"stream": stream, "table": constants(), "params": prm, "finals": finals, "p_in": p_in, "x_in": x_in}
    aps = []
    for name in arrays:
        arrays[name] = np.ascontiguousarray(arrays[name])
        aps.append(nc.dram_tensor(name, arrays[name].shape, F32, kind="ExternalInput").ap())
    out = nc.dram_tensor("out", (P, TT, D), F32, kind="ExternalOutput").ap()
    program(nc, *aps, out)
    r = _run(nc, [arrays], core_ids=[0])
    return np.ascontiguousarray(r.results[0]["out"].transpose(1, 0, 2)).reshape(1, T, D)
```

```python
from contextlib import ExitStack

import numpy as np

import concourse.bass as bass
from concourse import mybir

F32 = mybir.dt.float32
F32R = mybir.dt.float32r
ALU = mybir.AluOpType
ACT = mybir.ActivationFunctionType
AX = mybir.AxisListType

P = 128
D = 1024
T = 256
TT = T // P
KD = D // P
EPS = 1e-6
BIG = 1.0e30

SBW, SBH, SBD = 384, 6, 64
MLW, MLH, MLD = 384, 4, 96
SGW, SGG, SGD = 256, 4, 64
CONV_K = 4
NG, EPG, NE = 4, 8, 32
GATES = 8
N_IN = 3 * SBW + 4 * MLW + 2 * SGW + GATES
TAIL = N_IN - 6 * 512
Z_QB = 3 * SBW
Z_VB = Z_QB + 2 * MLW
Z_OB = Z_VB + MLW
Z_UC = Z_OB + MLW
Z_VC = Z_UC + SGW
Z_GATES = Z_VC + SGW
NH, HD = 16, 64
HALF = HD // 2
FF = 2816
FE = FF // 256
SCB = D // P

UNIT = 2048
U_WIN = 0
U_WOUT = U_WIN + 13
U_MOE = U_WOUT + 4
U_PLEG = U_MOE + 3 * NE
U_PLEP = U_PLEG + 4
U_SCIN = U_PLEP + 1
U_SCOUT = U_SCIN + 12
U_FFN0 = U_SCOUT + 4
U_QKV = U_FFN0 + 3 * FE
U_WO = U_QKV + 12
U_FFN1 = U_WO + 4
UNITS = U_FFN1 + 3 * FE
RING = 3

C_WIN, C_WOUT, C_PLEG, C_PLEP, C_SCOUT, C_QKV, C_WO, CHUNKS = 0, 7, 9, 11, 13, 15, 21, 23
BY_ACT = [1] * 7 + [0] * 2 + [1] * 2 + [0] * 2 + [0] * 2 + [0] * 4 + [1] * 2 + [0] * 2
BY_DVE = [1] * 7 + [1, 0] + [0] * 2 + [1] * 2 + [1, 0] + [1] * 4 + [0] * 2 + [1, 0]
CHUNK_END = [2, 4, 6, 8, 10, 12, 13] + [u + 2 * c + 2 for u, n in ((U_WOUT, 2), (U_PLEG, 2)) for c in range(n)] \
    + [U_PLEP + 1] * 2 + [u + 2 * c + 2 for u, n in ((U_SCOUT, 2), (U_QKV, 6), (U_WO, 2)) for c in range(n)]
G_SC, G_FFN0, G_FFN1 = 0, 6, 6 + FE

SLOTS = 64
PAIRS = NE // 2


def layout(parts):
    at, out = 0, {}
    for name, width in parts:
        out[name] = (at, at + width)
        at += width
    return out, at


CONST, CONST_W = layout([("ident", P), ("later", P), ("ones", P), ("upto", P), ("strict", P), ("bigpast", P),
                         ("causal", P), ("cos", TT * HALF), ("sin", TT * HALF), ("iota4", NG), ("iota32", NE),
                         ("neghalf", 8),
                         ("iota64", SLOTS)])
PARAM, PARAM_W = layout([("g0", KD), ("g1", KD), ("g2", KD), ("g3", KD), ("g4", KD), ("g5", KD), ("g6", KD),
                         ("g7", KD), ("gates_b", GATES), ("conv_w", 8 * CONV_K), ("conv_b", 8), ("ln_g", SGW),
                         ("ln_b", SGW), ("sgu_b", SGG), ("sgu_w", SGG * P), ("router_b", NG + NE),
                         ("router_w", KD * (NG + NE)), ("sc_conv", 3 * SCB), ("ffn_conv", 2 * FE * 12)])

A_S = TT * N_IN
A_T1 = A_S + SBH * 384
A_QKA = A_T1 + SBH * 384
ARENA = A_QKA + 8 * T
A_FINAL = 3072
A_PT = A_FINAL + D


def program(nc, stream, table, params, finals, p_in, x_in, out):
    ctx = ExitStack()
    with ctx:
        def sb(name, shape, dt=F32):
            return ctx.enter_context(nc.sbuf_tensor(name, shape, dt))

        sems = {}

        def S(name):
            if name not in sems:
                sems[name] = ctx.enter_context(nc.semaphore(name))
            return sems[name]

        raw = sb("raw", [P, RING, UNIT])
        whi = sb("whi", [P, RING, UNIT], F32R)
        wlo = sb("wlo", [P, RING, UNIT], F32R)
        cst = sb("cst", [P, CONST_W])
        par = sb("par", [P, PARAM_W])
        xres = sb("xres", [P, TT, D])
        xn = sb("xn", [P, TT, D])
        xhi = sb("xhi", [P, KD, T], F32R)
        xlo = sb("xlo", [P, KD, T], F32R)
        rounded = sb("rounded", [P, 7424], F32R)
        rhi = sb("rhi", [P, KD, NG + NE], F32R)
        rlo = sb("rlo", [P, KD, NG + NE], F32R)
        arena = sb("arena", [P, ARENA])
        sumsq = sb("sumsq", [P, TT])
        rstd = sb("rstd", [P, TT])
        mean = sb("mean", [P, TT])
        sm = sb("sm", [P, 832])
        rows2 = sb("rows2", [MLH, 2, T])
        spill_count = sb("spill_count", [1, 1], mybir.dt.int32)
        cwn = sb("cwn", [P, 2, 12])
        bank = [ctx.enter_context(nc.psum_tensor(f"bank{i}", [P, 512], F32)) for i in range(8)]

        def C(name):
            a, b = CONST[name]
            return cst[:, a:b]

        def Q(name):
            a, b = PARAM[name]
            return par[:, a:b]

        ident = C("ident")
        sgu_w = Q("sgu_w").rearrange("p (g t) -> p g t", g=SGG)
        router_w = Q("router_w").rearrange("p (k n) -> p k n", k=KD)
        conv_w = Q("conv_w").rearrange("p (j t) -> p j t", j=8)
        sc_conv = Q("sc_conv").rearrange("p (t j) -> p t j", t=3)
        ffn_conv = Q("ffn_conv").rearrange("p (l n) -> p l n", l=2)
        gate_b = Q("gates_b")
        small = {}
        at = 0
        for name, width in [("gt", 16), ("lf", 8), ("la", 8), ("ccol", 16), ("den", 8), ("ssb", 8), ("msb", 8),
                            ("rsb", 8), ("ssac", 4), ("msac", 4), ("rsac", 4), ("mu", 8), ("ssc", 8), ("msc", 8),
                            ("rsc", 8), ("lg", 72), ("gmax", 2), ("eqg", 8), ("ohg", 8), ("idx", 2), ("pen", 8),
                            ("eg", 8), ("gw", 2), ("em", 64), ("v1", 2), ("v2", 2), ("oh1", 64), ("oh2", 64),
                            ("cand", 64), ("dv", 2), ("p1", 2), ("p2", 2), ("m", 6), ("nm", 6), ("l", 6), ("rl", 6),
                            ("sel", 64), ("key", 64), ("over", 64), ("spill", 1)]:
            small[name] = (at, at + width)
            at += width
        assert at <= 832

        def V(name):
            a, b = small[name]
            return sm[:, a:b]

        z = arena[:, 0:TT * N_IN].rearrange("p (a n) -> p a n", a=TT)
        sa = arena[:, A_S:A_T1].rearrange("p (h b t) -> p h b t", h=SBH, b=3)
        t1 = arena[:, A_T1:A_QKA].rearrange("p (h b t) -> p h b t", h=SBH, b=3)
        sa_flat = arena[:, A_S:A_T1]
        t1_flat = arena[:, A_T1:A_QKA]
        qka = arena[:, A_QKA:A_QKA + 6 * T].rearrange("p (j t) -> p j t", j=6)
        qka_flat = arena[:, A_QKA:A_QKA + 6 * T]
        cvb = xn[0:MLD].rearrange("p a n -> p (a n)").rearrange("p (j t) -> p j t", j=8)
        qkb = arena[0:MLD, A_QKA:ARENA].rearrange("p (j t) -> p j t", j=8)
        mw = [z[:, a, Z_QB:Z_VB].rearrange("p (h b t) -> p h b t", h=2, b=3) for a in range(TT)]
        mwh = [mw[h // 2][:, h % 2] for h in range(MLH)]
        tmp = arena[:, 0:2 * SBW]
        vext = t1_flat[:, 0:TT * MLH * (MLD + 1)].rearrange("p (a h d) -> p a h d", a=TT, h=MLH)
        rows = [z[0:MLH, 1, T * r:T * r + T] for r in range(3)] + [rows2[:, r, :] for r in range(2)]
        hhi = rounded[:, 0:1024].rearrange("p (b f t) -> p b f t", b=2, f=2)
        hlo = rounded[:, 1024:2048].rearrange("p (b f t) -> p b f t", b=2, f=2)
        phi = rounded[:, 0:512].rearrange("p (k t) -> p k t", k=2)
        plo = rounded[:, 512:1024].rearrange("p (k t) -> p k t", k=2)
        xghi = rounded[:, 0:1536].rearrange("p (k n) -> p k n", k=KD)
        xglo = rounded[:, 1536:3072].rearrange("p (k n) -> p k n", k=KD)
        hthi = rounded[:, 3072:3456].rearrange("p (f n) -> p f n", f=2)
        htlo = rounded[:, 3456:3840].rearrange("p (f n) -> p f n", f=2)
        yhi, ylo = rounded[:, 3840:4864], rounded[:, 4864:5888]
        pick = rounded[:, 5888:6400].rearrange("p (b a e s) -> p b a e s", b=2, a=TT, e=2)
        shi = rounded[:, 6400:6912].rearrange("p (b t) -> p b t", b=2)
        slo = rounded[:, 6912:7424].rearrange("p (b t) -> p b t", b=2)
        ident_r, causal_r = rounded[:, 6400:6528], rounded[:, 6528:6656]
        xtok_hi = xhi[:].rearrange("p k t -> p (k t)").rearrange("p (a n) -> p a n", a=TT)
        xtok_lo = xlo[:].rearrange("p k t -> p (k t)").rearrange("p (a n) -> p a n", a=TT)
        pickw = arena[:, 0:512].rearrange("p (b a e s) -> p b a e s", b=2, a=TT, e=2)
        sgl = arena[:, 512:768]
        hv = arena[:, 768:1024]
        logits_t = arena[0:NG + NE, 512:768]
        xf = arena[:, 1024:1024 + KD * T].rearrange("p (k t) -> p k t", k=KD)
        wexp = arena[:, 3072:3072 + 3 * UNIT].rearrange("p (u n) -> p u n", u=3)
        osg = arena[:, 9216:9728]
        ohv = arena[:, 9728:10240]
        owt = arena[0:NE, 10240:10496]
        ows = arena[0:NE, 10496:10752]
        final_g = arena[:, A_FINAL:A_FINAL + D]
        p_t = arena[:, A_PT:A_PT + 2 * T].rearrange("p (k t) -> p k t", k=2)
        gsb = arena[:, 0:TT * D].rearrange("p (a n) -> p a n", a=TT)
        gpr = arena[:, TT * D:TT * D + 1024].rearrange("p (a n) -> p a n", a=TT)
        csb = arena[:, 0:1024].rearrange("p (b n) -> p b n", b=2)
        cvp = arena[:, 1024:1024 + SCB * (T + 2)].rearrange("p (j t) -> p j t", j=SCB)
        A_Y = 1024 + SCB * (T + 2)
        scy = arena[:, A_Y:A_Y + SCB * T].rearrange("p (j t) -> p j t", j=SCB)
        facc = arena[:, 0:2048].rearrange("p (b f t) -> p b f t", b=2, f=4)
        qkv = arena[:, 0:TT * 3 * D].rearrange("p (a n) -> p a n", a=TT)
        A_QT = TT * 3 * D
        qkt = arena[:, A_QT:A_QT + 16 * T].rearrange("p (j t) -> p j t", j=16)
        qkt_flat = arena[:, A_QT:A_QT + 16 * T]
        A_RP = A_QT + 16 * T
        rp = arena[:, A_RP:A_RP + 1024].rearrange("p (k n) -> p k n", k=4)
        ap_ = arena[:, A_RP + 640:A_RP + 640 + 3 * 384].rearrange("p (b n) -> p b n", b=3)
        apt = arena[:, A_RP + 1792:A_RP + 2560].rearrange("p (b n) -> p b n", b=2)

        block = ctx.enter_context(nc.Block())

        R_WOUT, R_MOE, R_PLE, R_FINAL1, R_SC, R_FFN0, R_ATT, R_FFN1 = range(1, 9)
        NORM_READS = [0, R_WOUT, R_MOE, R_PLE, R_FINAL1, R_SC, R_FFN0, R_ATT, R_FFN1]

        def group_end(u0, e, e0):
            return u0 + 2 if e0 == 0 else e * 3 + (u0 + 1)

        def down_end(u0, count, e, e0):
            return e * 3 + (u0 + 5)

        class Chain:

            def __init__(self, eng, sem):
                self.eng, self.sem, self.n, self.off = eng, sem, 0, 0

            def link(self, ins):
                self.n += 1
                ins.then_inc(self.sem, 1)
                self.eng.wait_ge(self.sem, self.off + self.n)

            def enter(self, j, per):
                self.off, self.start = j * per, self.n

            def leave(self, per, times):
                assert self.n - self.start == per
                self.off, self.n = 0, self.start + per * times

        def spilled(eng):
            eng.wait_ge(S("spill_known"), 1)
            return eng.value_load(spill_count[0:1, 0:1], min_val=0, max_val=2 * T)

        def each_expert(eng, body):
            for r in range(2):
                body(r, U_MOE + 2 * r, U_MOE + 8 + r)
            with eng.Fori(1, PAIRS - 1) as q:
                for r in range(2):
                    body(q * 2 + r, q * 6 + (U_MOE - 2 + 2 * r), q * 6 + (U_MOE + 8 + r))
            for r in range(2):
                body(NE - 2 + r, U_MOE + 3 * NE - 8 + 2 * r, U_MOE + 3 * NE - 2 + r)

        def overflow_act(act):
            with act.If(spilled(act) > 0):
                for k in range(KD):
                    act.wait_ge(S("of_turned"), k // 2 + 1)
                    ins = act.activation(xf[:, k, :], bank[k // 2][:, (k % 2) * T:(k % 2 + 1) * T], ACT.Copy,
                                         scale=Q("g2")[:, k:k + 1])
                ins.then_inc(S("of_tokens"), 1)

                def expert(n, gate_up, down):
                    for u, unit in enumerate((gate_up, gate_up + 1, down)):
                        act.dma_start(wexp[:, u, :], stream[unit]).then_inc(S(f"of_landed{u}"), 16)
                    act.wait_ge(S("of_gate_up"), n + 1)
                    act.activation(osg, bank[0][:], ACT.Silu).then_inc(S("of_silu"), 1)
                    act.wait_ge(S("of_down"), n + 1)

                each_expert(act, expert)

        def overflow_dve(dve):
            with dve.If(spilled(dve) > 0):
                dve.wait_ge(S("of_weights_turned"), 1)
                dve.tensor_copy(owt, bank[1][0:NE, 0:T]).then_inc(S("of_weights"), 1)
                dve.wait_ge(S("of_weights"), 1)

                def expert(n, gate_up, down):
                    one = ident[0:NE, n:n + 1] if isinstance(n, int) else ident[0:NE, bass.ds(n, 1)]
                    dve.tensor_tensor(ows, owt, one.broadcast_to([NE, T]), ALU.mult).then_inc(S("of_row"), 1)
                    dve.wait_ge(S("of_silu"), n + 1)
                    dve.tensor_tensor(ohv, osg, bank[1][:], ALU.mult).then_inc(S("of_product"), 1)
                    dve.wait_ge(S("of_product"), n + 1)
                    half = ohv.rearrange("p (f t) -> p f t", f=2)
                    dve.tensor_tensor(half, bank[2][:, 0:T].unsqueeze(1).broadcast_to([P, 2, T]), half, ALU.mult)\
                       .then_inc(S("of_hidden"), 1)
                    dve.wait_ge(S("of_down"), n + 1)

                each_expert(dve, expert)

        def overflow_pe(pe):
            with pe.If(spilled(pe) > 0):
                for k in range(KD):
                    for t in range(TT):
                        ins = pe.transpose(bank[k // 2][:, (k % 2) * T + t * P:(k % 2) * T + t * P + P],
                                           xn[:, t, P * k:P * k + P], ident)
                    if k % 2:
                        ins.then_inc(S("of_turned"), 1)
                pe.wait_ge(S("of_tokens"), 1)
                pe.wait_ge(S("over_ready"), 1)
                over = V("over").rearrange("p (a n) -> p a n", a=TT)
                for t in range(TT):
                    ins = pe.transpose(bank[1][0:NE, P * t:P * t + P], over[:, t, :], ident)
                ins.then_inc(S("of_weights_turned"), 1)
                pe.wait_ge(S("of_weights"), 1)

                def expert(n, gate_up, down):
                    pe.wait_ge(S("of_row"), n + 1)
                    pe.matmul(bank[2][:, 0:T], C("ones")[0:NE, :], ows, start=True, stop=True, skip_group_check=True)
                    for kk in range(KD):
                        if kk % 4 == 0:
                            pe.wait_ge(S(f"of_landed{kk // 4}"), n * 16 + 16)
                        for f in range(4):
                            w = 512 * (kk % 4) + P * f
                            ins = pe.matmul(bank[f // 2][:, (f % 2) * T:(f % 2 + 1) * T],
                                            wexp[:, kk // 4, w:w + P], xf[:, kk, :],
                                            start=kk == 0 and f % 2 == 0, stop=kk == 7, skip_group_check=True)
                    ins.then_inc(S("of_gate_up"), 1)
                    pe.wait_ge(S("of_hidden"), n + 1)
                    pe.wait_ge(S("of_landed2"), n * 16 + 16)
                    for t in range(TT):
                        for c in range(2):
                            for f in range(2):
                                w = D * f + 512 * c
                                ins = pe.matmul(bank[4 + 2 * t + c][:], ohv[:, T * f + P * t:T * f + P * t + P],
                                                wexp[:, 2, w:w + 512], start=False, stop=False, skip_group_check=True)
                    ins.then_inc(S("of_down"), 1)

                each_expert(pe, expert)

        @block.sync
        def _(sp):
            sp.dma_start(xres[:], x_in).then_inc(S("x_loaded"), 16)
            sp.dma_start(cst[:], table).then_inc(S("table_loaded"), 16)
            sp.dma_start(raw[:, 0, :], stream[0]).then_inc(S("landed0"), 16)
            sp.dma_start(par[:], params).then_inc(S("params_loaded"), 16)
            for n in range(1, RING):
                sp.dma_start(raw[:, n, :], stream[n]).then_inc(S(f"landed{n}"), 16)
            with sp.Fori(0, UNITS // RING - 1) as j:
                for s in range(RING):
                    sp.wait_ge(S("low_done"), RING * j + s + 1)
                    sp.dma_start(raw[:, s, :], stream[RING * j + (s + RING)]).then_inc(S(f"landed{s}"), 16)
            for t in range(TT):
                sp.wait_ge(S("y_ready"), t + 1)
                sp.dma_start(out[:, t, :], xn[:, t, :]).then_inc(S("stored"), 16)
            sp.wait_ge(S("stored"), TT * 16)

        @block.scalar
        def _(act):
            chain = Chain(act, S("act_chain"))
            done = [0]

            def split(n):
                unit0, off = n if isinstance(n, tuple) else (n, 0)
                s = unit0 % RING
                act.wait_ge(S(f"landed{s}"), off * 16 // RING + 16 * (unit0 // RING + 1) if isinstance(off, int)
                            else off * (16 // 1) + 16 * (unit0 // RING + 1))
                if unit0 >= RING:
                    act.wait_ge(S("unit_used"), (off if isinstance(off, int) else off * RING) + unit0 - RING + 1)
                act.activation(whi[:, s, :], raw[:, s, :], ACT.Copy).then_inc(S("high_done"), 1)

            def split_to(n):
                while done[0] <= min(n, UNITS - 1):
                    split(done[0])
                    done[0] += 1

            def norm_act(i):
                for t in range(TT):
                    if i == 0:
                        act.wait_ge(S("x_loaded"), 16)
                    else:
                        act.wait_ge(S("residual_ready") if t else S("tile0_ready"), NORM_READS[i])
                    act.activation(xn[:, t, :], xres[:, t, :], ACT.Square, accum_out=sumsq[:, t:t + 1])\
                       .then_inc(S(f"sumsq{t}_ready"), 1)

            def turn_act(q):
                for k in range(KD):
                    if k % 2 == 0:
                        act.wait_ge(S("turned"), 4 * q + k // 2 + 1)
                    ins = act.activation(xhi[:, k, :], bank[4 + k // 2][:, (k % 2) * T:(k % 2 + 1) * T], ACT.Copy,
                                         scale=Q(f"g{q}")[:, k:k + 1])
                    if k % 2:
                        ins.then_inc(S("xhi_ready"), 1)

            norm_act(0)
            split_to(0)
            act.wait_ge(S("table_loaded"), 16)
            act.wait_ge(S("params_loaded"), 16)
            turn_act(0)
            split_to(1)
            act.activation(rhi[:], router_w, ACT.Copy).then_inc(S("setup_high"), 1)
            def logits_act(h0, h1):
                for h in range(h0, h1):
                    act.wait_ge(S("scores_a"), h + 1)
                    ins = act.activation(sa_flat[:, 384 * h:384 * h + 384], bank[4 + h % 4][:, 0:384], ACT.Copy,
                                         scale=SBD ** -0.5)
                    ins.then_inc(S("logits_act"), 1)
                act.wait_ge(S("logits_act"), h1)
                chain.link(act.activation(t1_flat[:, 384 * h0:384 * h1], sa_flat[:, 384 * h0:384 * h1], ACT.Abs))

            def softplus_act(h0, h1):
                t = t1_flat[:, 384 * h0:384 * h1]
                chain.link(act.activation(t, t, ACT.Exp, scale=-1.0))
                act.activation(t, t, ACT.Ln, bias=1.0).then_inc(S("softplus_log"), 1)

            for c in range(7):
                split_to(min(U_WIN + 2 * c + 3, 12))
                act.wait_ge(S("unit_used"), CHUNK_END[C_WIN + c])
                w = min(512, N_IN - 512 * c)
                act.activation(z[:, 0, 512 * c:512 * c + w], bank[2 * (c % 2)][:, 0:w], ACT.Copy)\
                   .then_inc(S("act_freed"), 1)
                if c == 2:
                    for b in (0, 2):
                        act.wait_ge(S("turned_a"), b + 1)
                        act.activation(qka_flat[:, 512 * b:512 * b + 512], bank[4 + b][:], ACT.Copy)\
                           .then_inc(S("qka_act"), 1)
                elif c == 3:
                    logits_act(0, 4)
                elif c == 4:
                    for b in range(2):
                        act.wait_ge(S("turned_b"), b + 1)
                        act.activation(cvb[:, 2 * b:2 * b + 2, :],
                                       bank[4 + b][0:MLD, :].rearrange("p (j t) -> p j t", j=2), ACT.Copy)\
                           .then_inc(S("cvb_act"), 1)
                    softplus_act(0, 4)
                elif c == 5:
                    logits_act(4, 6)
                    act.wait_ge(S("cvb_dve"), 2)
                    act.wait_ge(S("cvb_act"), 2)
                    for j in range(8):
                        act.activation(qkb[:, j, :], cvb[:, j, :], ACT.Identity, scale=conv_w[0:MLD, j, 3:4],
                                       bias=Q("conv_b")[0:MLD, j:j + 1]).then_inc(S("conv_begun"), 1)
            softplus_act(4, 6)
            act.wait_ge(S("gates_ready"), 1)
            gt = V("gt").rearrange("p (a n) -> p a n", a=TT)
            la = V("la").rearrange("p (a n) -> p a n", a=TT)
            chain.link(act.activation(la, gt[:, :, 4:8], ACT.Abs))
            chain.link(act.activation(la, la, ACT.Exp, scale=-1.0))
            act.activation(la, la, ACT.Ln, bias=1.0).then_inc(S("gate_log"), 1)
            split_to(13)
            act.wait_ge(S("dve_freed"), sum(BY_DVE[:7]))
            chain.link(act.activation(z[:, :, Z_UC:Z_GATES], z[:, :, Z_UC:Z_GATES], ACT.Gelu_apprx_tanh))
            act.activation(z[:, :, Z_OB:Z_UC], z[:, :, Z_OB:Z_UC], ACT.Sigmoid).then_inc(S("gelu_ready"), 1)
            act.wait_ge(S("mrow_ready"), 1)
            act.activation(rows[4], rows[3], ACT.Exp, scale=-1.0).then_inc(S("enrow_ready"), 1)
            act.wait_ge(S("expo_ready"), 1)
            act.activation(sa_flat, sa_flat, ACT.Exp).then_inc(S("weights_a"), 1)
            split_to(14)
            act.wait_ge(S("conv_done"), 1)
            act.activation(qkb[:], qkb[:], ACT.Silu).then_inc(S("qkb_ready"), 1)
            split_to(15)
            act.wait_ge(S("ccol_ready"), 1)
            act.wait_ge(S("mw_ready"), 1)
            ccol = V("ccol")
            for h in range(MLH):
                act.activation(mwh[h][:, 0:2, :], mwh[h][:, 0:2, :], ACT.Exp, scale=-1.0, bias=ccol[:, h:h + 1])
                act.activation(mwh[h][:, 2, :], mwh[h][:, 2, :], ACT.Exp, scale=-1.0, bias=ccol[:, 4 + h:5 + h])\
                   .then_inc(S("decay_ready"), 1)
            act.wait_ge(S("out_a"), 1)
            ssac = V("ssac")
            for t in range(TT):
                chain.link(act.activation(xn[:, t, 0:SBW], bank[1 + t][:, 0:SBW], ACT.Copy))
            act.wait_ge(S("ln_squares"), 1)
            for t in range(TT):
                ins = act.activation(tmp[:, 0:SBW], xn[:, t, 0:SBW], ACT.Square, accum_out=ssac[:, t:t + 1])
                chain.link(ins)
            act.wait_ge(S("yc_ready"), 1)
            for t in range(TT):
                ins = act.activation(tmp[:, 0:SGW], xn[:, t, SBW + MLW:D], ACT.Square, accum_out=ssac[:, 2 + t:3 + t])
                if t == 0:
                    chain.link(ins)
            ins.then_inc(S("sumsq_ac"), 1)
            act.wait_ge(S("sumsq_ac"), 1)
            act.wait_ge(S("hb_ready"), 1)
            act.activation(tmp.rearrange("p (a n) -> p a n", a=TT), xn[:, :, SBW:SBW + MLW], ACT.Square)\
               .then_inc(S("hb_squares"), 1)
            act.wait_ge(S("rstd_ac"), 1)
            for t in range(TT):
                act.activation(xn[:, t, 0:SBW], xn[:, t, 0:SBW], ACT.Copy, scale=V("rsac")[:, t:t + 1])
                ins = act.activation(xn[:, t, SBW + MLW:D], xn[:, t, SBW + MLW:D], ACT.Copy,
                                     scale=V("rsac")[:, 2 + t:3 + t])
            ins.then_inc(S("xn1_ready"), 1)
            turn_act(1)
            for c in range(2):
                split_to(U_WOUT + 2 * c + 3)
            norm_act(1)
            turn_act(2)
            act.wait_ge(S("router_done"), 1)
            act.activation(xtok_hi, xn[:], ACT.Copy).then_inc(S("xtok_high"), 1)
            act.wait_ge(S("gdiff_ready"), 1)
            act.activation(V("eg"), V("eg"), ACT.Exp).then_inc(S("gexp_ready"), 1)
            act.wait_ge(S("vdiff_ready"), 1)
            act.activation(V("dv"), V("dv"), ACT.Exp).then_inc(S("vexp_ready"), 1)

            def gather_high(k0, wait, at=1):
                act.wait_ge(S("gathered"), wait)
                for k in range(4):
                    ins = act.activation(xghi[:, k0 + k, :].rearrange("p (c s) -> p c s", s=SLOTS)[:, 0:3:2, :],
                                         bank[at][:, P * k:P * k + P].rearrange("p (c s) -> p c s", s=SLOTS), ACT.Copy,
                                         scale=Q("g2")[:, k0 + k:k0 + k + 1])
                ins.then_inc(S("gather_high"), 1)

            def turned_high(p, b):
                act.wait_ge(S("turned_pair"), p + 1)
                act.activation(shi[:, b, :], bank[1][:, 0:T], ACT.Copy)
                for f in range(2):
                    ins = act.activation(hthi[:, f, :].rearrange("p (c s) -> p c s", s=SLOTS)[:, 0:3:2, :],
                                         bank[1][:, T + P * f:T + P * f + P].rearrange("p (c s) -> p c s", s=SLOTS),
                                         ACT.Copy)
                ins.then_inc(S("turned_high"), 1)

            def y_high(wait):
                act.wait_ge(S("unit_used"), wait)
                for c in range(2):
                    ins = act.activation(yhi[:, 512 * c:512 * c + 512], bank[2 + c][:], ACT.Copy)
                ins.then_inc(S("y_high"), 1)

            def silu_pair(wait):
                act.wait_ge(S("unit_used"), wait)
                act.activation(sgl, bank[0][:, 0:256], ACT.Silu).then_inc(S("pair_silu"), 1)

            def pair_act(p, p0, off):
                n = U_MOE + 6 * p0 - 2
                ahead = (lambda k: split_to(n + k)) if off is None else (lambda k: split((n + k, off)))
                used = lambda k: (0 if off is None else off * RING) + (n + k)
                ahead(2)
                turned_high(p - 1, (p0 - 1) % 2)
                ahead(3)
                ahead(4)
                ahead(5)
                silu_pair(used(4))
                if p0 < PAIRS - 1:
                    gather_high(0, 2 * p + 3)
                ahead(6)
                if p0 < PAIRS - 1:
                    gather_high(4, 2 * p + 4)
                ahead(7)
                y_high(used(6))

            act.wait_ge(S("zeros_ready"), 1)
            gather_high(0, 1)
            gather_high(4, 2, 2)
            split_to(U_MOE + 5)
            silu_pair(U_MOE + 4)
            gather_high(0, 3)
            gather_high(4, 4, 2)
            pair_act(1, 1, None)
            assert done[0] == U_MOE + 12
            with act.Fori(0, (PAIRS - 4) // 2) as j:
                for b in range(2):
                    pair_act(2 * j + (2 + b), 2 + b, 4 * j)
            done[0] = U_MOE + 6 * (PAIRS - 2)
            pair_act(PAIRS - 2, PAIRS - 2, None)
            pair_act(PAIRS - 1, PAIRS - 1, None)
            turned_high(PAIRS - 1, (PAIRS - 1) % 2)
            y_high(U_MOE + 3 * NE)
            overflow_act(act)

            def ffn_act(layer, e, off, e0):
                g0, d0, u0 = (G_FFN0, 0, U_FFN0) if layer == 0 else (G_FFN1, FE, U_FFN1)
                b, gb = e0 % 2, (g0 + e0) % 2
                n = u0 + 3 * e0 - 1

                def ahead(k):
                    if off is None:
                        split_to(n + k)
                    elif n + k < UNITS:
                        split((n + k, off))
                ahead(3)
                act.wait_ge(S("unit_used"), group_end(u0, e, e0))
                act.wait_ge(S("taps_ready"), layer * FE + 1 + e)
                if e0 >= 2:
                    act.wait_ge(S("h_ready"), d0 - 1 + e)
                for f in range(4):
                    ins = act.activation(facc[:, b, f, :], bank[2 * gb + f // 2][:, (f % 2) * T:(f % 2 + 1) * T],
                                         ACT.Copy, scale=cwn[:, b, 8 + f:9 + f])
                ins.then_inc(S("ffn_begun"), 1)
                ahead(4)
                act.wait_ge(S("g_free"), g0 + 1 + e)
                act.activation(facc[:, b, 0:2, :], facc[:, b, 0:2, :], ACT.Silu).then_inc(S("silu_ready"), 1)
                ahead(5)
                act.wait_ge(S("hv_ready"), layer * FE + 1 + e)
                if e0 >= 2:
                    act.wait_ge(S("unit_used"), down_end(u0, FE, e - 2, e0 - 2))
                act.activation(hhi[:, b, :, :], facc[:, b, 2:4, :], ACT.Copy).then_inc(S("hhi_ready"), 1)

            norm_act(2)
            act.dma_start(p_t, p_in).then_inc(S("p_loaded"), 16)
            act.dma_start(final_g, finals[0]).then_inc(S("final1_loaded"), 16)
            turn_act(3)
            act.wait_ge(S("p_loaded"), 16)
            act.activation(phi, p_t, ACT.Copy).then_inc(S("p_high"), 1)
            for c in range(2):
                split_to(U_PLEG + 2 * c + 3)
                act.wait_ge(S("unit_used"), CHUNK_END[C_PLEG + c])
                for t in range(TT):
                    ins = act.activation(gsb[:, t, 512 * c:512 * c + 512], bank[2 * ((C_PLEG + c) % 2) + t][:],
                                         ACT.Sigmoid)
                ins.then_inc(S("act_freed"), 1)
            split_to(U_PLEP + 2)
            norm_act(3)
            split_to(U_SCIN + 1)
            norm_act(4)
            turn_act(4)
            for i in range(6):
                split_to(U_SCIN + 2 * i + 3)
                if i < 4:
                    g = G_SC + i
                    act.wait_ge(S("unit_used"), U_SCIN + 2 * i + 2)
                    act.activation(csb[:, i % 2, :], bank[2 * (g % 2)][:], ACT.Copy).then_inc(S("c_ready"), 1)
                    act.wait_ge(S("g_free"), g + 1)
                    for f in range(2 * i, 2 * i + 2):
                        ins = act.activation(scy[:, f, :], cvp[:, f, 2:2 + T], ACT.Copy, scale=sc_conv[:, 2, f:f + 1])
                    ins.then_inc(S("sc_begun"), 1)
            for f in range(4):
                act.wait_ge(*((S("g_free"), G_SC + 5 + f // 2) if f % 2 else (S("sc_product"), f // 2 + 1)))
                act.activation(xhi[:, 2 * f:2 * f + 2, :], scy[:, 2 * f:2 * f + 2, :], ACT.Copy)\
                   .then_inc(S("sc_high"), 1)
            for c in range(2):
                split_to(U_SCOUT + 2 * c + 3)

            def ffn(layer):
                ffn_act(layer, 0, None, 0)
                ffn_act(layer, 1, None, 1)
                u0 = U_FFN0 if layer == 0 else U_FFN1
                assert done[0] == min(u0 + 8, UNITS)
                with act.Fori(0, (FE - 3) // 2) as j:
                    for b in range(2):
                        ffn_act(layer, 2 * j + (2 + b), 2 * j, 2 + b)
                done[0] = u0 + 3 * (FE - 1) + 2
                ffn_act(layer, FE - 1, None, FE - 1)

            norm_act(5)
            turn_act(5)
            ffn(0)
            norm_act(6)
            turn_act(6)
            act.activation(ident_r, ident, ACT.Copy)
            act.activation(causal_r, C("causal"), ACT.Copy).then_inc(S("mask_ready"), 1)
            for c in range(6):
                split_to(U_QKV + 2 * c + 3)
                if c >= 4:
                    for b in range(4 * (c - 4), 4 * (c - 4) + 4):
                        act.wait_ge(S("qk_turned"), b + 1)
                        act.activation(qkt_flat[:, 512 * b:512 * b + 512], bank[4 + b % 4][:], ACT.Copy)\
                           .then_inc(S("qkt_ready"), 1)
                    act.wait_ge(S("unit_used"), CHUNK_END[C_QKV + c])
                    for t in range(TT):
                        ins = act.activation(qkv[:, t, 512 * c:512 * c + 512], bank[2 * ((C_QKV + c) % 2) + t][:],
                                             ACT.Copy)
                    ins.then_inc(S("act_freed"), 1)

            def pt_copy(h):
                act.wait_ge(S("p_turned"), h + 1)
                if h >= 2:
                    act.wait_ge(S("pv_done"), h - 1)
                act.activation(apt[:, h % 2, :], bank[3][:, 0:384], ACT.Copy).then_inc(S("pt_ready"), 1)

            for h in range(NH):
                act.wait_ge(S("negmax_ready"), h + 1)
                if h >= 3:
                    act.wait_ge(S("p_turned"), h - 2)
                b = h % 3
                nm, l = V("nm"), V("l")
                act.activation(ap_[:, b, 0:128], bank[b][:, 0:128], ACT.Exp, scale=HD ** -0.5,
                               bias=nm[:, 2 * b:2 * b + 1], accum_out=l[:, 2 * b:2 * b + 1])
                act.activation(ap_[:, b, 128:384], bank[b][:, 128:384], ACT.Exp, scale=HD ** -0.5,
                               bias=nm[:, 2 * b + 1:2 * b + 2], accum_out=l[:, 2 * b + 1:2 * b + 2])\
                   .then_inc(S("exp_done"), 1)
                if h >= 1:
                    pt_copy(h - 1)
            pt_copy(NH - 1)
            for b in range(4):
                act.wait_ge(S("pv_done"), 4 * b + 4)
                act.activation(xhi[:, 2 * b:2 * b + 2, :], bank[4 + b][:].rearrange("p (j t) -> p j t", j=2),
                               ACT.Copy).then_inc(S("o_high"), 1)
            for c in range(2):
                split_to(U_WO + 2 * c + 3)
            norm_act(7)
            act.dma_start(final_g, finals[1]).then_inc(S("final2_loaded"), 16)
            turn_act(7)
            ffn(1)
            norm_act(8)

        @block.gpsimd
        def _(pool):
            chain = Chain(pool, S("pool_chain"))
            nh = C("neghalf")

            def rsqrt(dst, mid, src, count, width):
                chain.link(pool.tensor_scalar(mid, src, 1.0 / count, EPS, ALU.mult, ALU.add))
                return pool.tensor_tensor(dst, mid, nh[:, 0:width], ALU.pow)

            def norm_pool(i):
                for t in range(TT):
                    pool.wait_ge(S(f"sumsq{t}_ready"), i + 1)
                    rsqrt(rstd[:, t:t + 1], mean[:, t:t + 1], sumsq[:, t:t + 1], D, 1)\
                        .then_inc(S(f"rstd{t}_ready"), 1)
                pool.wait_ge(S("rstd1_ready"), i + 1)

            pool.wait_ge(S("table_loaded"), 16)
            norm_pool(0)
            pool.wait_ge(S("params_loaded"), 16)
            pool.memset(sgu_w[64:128, :, 0:64], 0.0).then_inc(S("sgu_masked"), 1)
            pool.wait_ge(S("sgu_masked"), 1)
            pool.wait_ge(S("act_freed"), 5)
            pool.wait_ge(S("dve_freed"), 5)
            pool.wait_ge(S("after_a"), SBH)
            for t in range(TT):
                pool.tensor_copy(vext[:, t, :, 0:MLD], z[:, t, Z_VB:Z_OB].rearrange("p (h d) -> p h d", h=MLH))
            pool.memset(vext[:, :, :, MLD:MLD + 1], 1.0).then_inc(S("values_ready"), 1)
            pool.wait_ge(S("ln_squares"), 1)
            rsqrt(V("rsc"), V("msc"), V("ssc"), SGD, 8).then_inc(S("ln_rstd"), 1)
            pool.wait_ge(S("sumsq_ac"), 1)
            chain.link(pool.tensor_scalar(V("msac")[:, 0:2], V("ssac")[:, 0:2], 1.0 / SBW, EPS, ALU.mult, ALU.add))
            chain.link(pool.tensor_scalar(V("msac")[:, 2:4], V("ssac")[:, 2:4], 1.0 / SGW, EPS, ALU.mult, ALU.add))
            pool.tensor_tensor(V("rsac"), V("msac"), nh[:, 0:4], ALU.pow).then_inc(S("rstd_ac"), 1)
            pool.wait_ge(S("hb_sums"), 1)
            rsqrt(V("rsb"), V("msb"), V("ssb"), MLD, 8).then_inc(S("hb_rstd"), 1)
            norm_pool(1)

            def weigh_pair(p, p0):
                b = p0 % 2
                if p0 >= 2:
                    pool.wait_ge(S("turned_pair"), p - 1)
                two = bass.ds(2 * p, 2) if p0 is not p else slice(2 * p, 2 * p + 2)
                wt = V("oh1").rearrange("p (a e) -> p a e", a=TT)[:, :, two].unsqueeze(3)
                pool.wait_ge(S("pick_ready"), p + 1)
                for t in range(TT):
                    ins = pool.tensor_tensor(pickw[:, b, t], pick[:, b, t].bitcast(F32),
                                             wt[:, t].broadcast_to([P, 2, SLOTS]), ALU.mult)
                ins.then_inc(S("pickw_ready"), 1)

            for zero in (xghi, xglo, hthi, htlo):
                ins = pool.memset(zero[:, :, SLOTS:2 * SLOTS].bitcast(F32), 0.0)
            ins.then_inc(S("zeros_ready"), 1)
            pool.wait_ge(S("zeros_ready"), 1)
            pool.wait_ge(S("xtok_high"), 1)
            pool.tensor_tensor(xtok_lo, xn[:], xtok_hi.bitcast(F32), ALU.subtract).then_inc(S("xtok_ready"), 1)
            pool.wait_ge(S("wt_ready"), 1)
            weigh_pair(0, 0)
            weigh_pair(1, 1)
            with pool.Fori(0, (PAIRS - 2) // 2) as j:
                for b in range(2):
                    weigh_pair(2 * j + (2 + b), 2 + b)
            norm_pool(2)
            norm_pool(3)
            norm_pool(4)

            def taps(layer, e, e0):
                g0 = G_FFN0 if layer == 0 else G_FFN1
                b = e0 % 2
                if e0 >= 2 or layer == 1:
                    pool.wait_ge(S("g_free"), g0 - 1 + e)
                src = ffn_conv[:, layer, 12 * e0:12 * e0 + 12] if isinstance(e, int) else \
                    par[:, bass.ds(e * 12 + (PARAM["ffn_conv"][0] + layer * FE * 12), 12)]
                pool.tensor_copy(cwn[:, b, :], src).then_inc(S("taps_ready"), 1)

            def ffn(layer):
                taps(layer, 0, 0)
                taps(layer, 1, 1)
                with pool.Fori(0, (FE - 3) // 2) as j:
                    for b in range(2):
                        taps(layer, 2 * j + (2 + b), 2 + b)
                taps(layer, FE - 1, FE - 1)

            norm_pool(5)
            ffn(0)
            norm_pool(6)
            norm_pool(7)
            ffn(1)
            norm_pool(8)

        @block.vector
        def _(dve):
            chain = Chain(dve, S("dve_chain"))
            link = chain.link
            done = [0]

            def split(n):
                unit0, off = n if isinstance(n, tuple) else (n, 0)
                s = unit0 % RING
                dve.wait_ge(S("high_done"), (off if isinstance(off, int) else off * RING) + unit0 + 1)
                dve.tensor_tensor(wlo[:, s, :], raw[:, s, :], whi[:, s, :].bitcast(F32), ALU.subtract)\
                   .then_inc(S("low_done"), 1)

            def split_to(n):
                while done[0] <= min(n, UNITS - 1):
                    split(done[0])
                    done[0] += 1

            def norm_dve(i):
                for t in range(TT):
                    dve.wait_ge(S(f"rstd{t}_ready"), i + 1)
                    dve.tensor_scalar(xn[:, t, :], xres[:, t, :], rstd[:, t:t + 1], None, ALU.mult)\
                       .then_inc(S(f"xn{t}_ready"), 1)

            def turn_dve(q):
                for k in range(KD):
                    if k % 2 == 0:
                        dve.wait_ge(S("xhi_ready"), 4 * q + k // 2 + 1)
                    ins = dve.scalar_tensor_tensor(xlo[:, k, :], bank[4 + k // 2][:, (k % 2) * T:(k % 2 + 1) * T],
                                                   Q(f"g{q}")[:, k:k + 1], xhi[:, k, :].bitcast(F32), ALU.mult,
                                                   ALU.subtract)
                    if k % 2:
                        ins.then_inc(S("xt_ready"), 1)

            def add_chunks(u0, c0):
                for c in range(2):
                    split_to(u0 + 2 * c + 3)
                    dve.wait_ge(S("unit_used"), CHUNK_END[c0 + c])
                    for t in range(TT):
                        r = xres[:, t, 512 * c:512 * c + 512]
                        ins = dve.tensor_tensor(r, bank[2 * ((c0 + c) % 2) + t][:], r, ALU.add)
                        if c == 1 and t == 0:
                            ins.then_inc(S("tile0_ready"), 1)
                    ins.then_inc(S("dve_freed") if c == 0 else S("residual_ready"), 1)

            def add_down(units):
                if units != U_MOE + 3 * NE:
                    dve.wait_ge(S("unit_used"), units)
                for t in range(TT):
                    for c in range(2):
                        r = xres[:, t, 512 * c:512 * c + 512]
                        ins = dve.tensor_tensor(r, bank[4 + 2 * t + c][:], r, ALU.add)
                    ins.then_inc(S("tile0_ready") if t == 0 else S("residual_ready"), 1)

            dve.wait_ge(S("x_loaded"), 16)
            norm_dve(0)
            split_to(0)
            dve.wait_ge(S("table_loaded"), 16)
            dve.wait_ge(S("params_loaded"), 16)
            turn_dve(0)
            split_to(1)
            dve.wait_ge(S("setup_high"), 1)
            dve.tensor_tensor(rlo[:], router_w, rhi[:].bitcast(F32), ALU.subtract).then_inc(S("setup_low"), 1)
            strict = C("strict").unsqueeze(1)

            def softplus_dve(h0, h1):
                dve.wait_ge(S("softplus_log"), 1 if h0 == 0 else 2)
                a, t = sa_flat[:, 384 * h0:384 * h1], t1_flat[:, 384 * h0:384 * h1]
                link(dve.scalar_tensor_tensor(t, a, 0.0, t, ALU.max, ALU.add))
                link(dve.tensor_tensor(a, a, t, ALU.subtract))
                for k in (2, 0):
                    u = t1[:, h0:h1, k, :]
                    ins = dve.tensor_tensor(u, u, strict.broadcast_to([P, h1 - h0, P]), ALU.mult)
                ins.then_inc(S("l_ready"), 1)

            def conv_tap(k):
                for j in range(8):
                    y = qkb[:, j, 3 - k:T]
                    ins = dve.scalar_tensor_tensor(y, cvb[:, j, 0:T - 3 + k], conv_w[0:MLD, j, k:k + 1], y,
                                                   ALU.mult, ALU.add)
                return ins

            for c in range(7):
                split_to(min(U_WIN + 2 * c + 3, 12))
                dve.wait_ge(S("unit_used"), CHUNK_END[C_WIN + c])
                w = min(512, N_IN - 512 * c)
                dve.tensor_copy(z[:, 1, 512 * c:512 * c + w], bank[2 * (c % 2) + 1][:, 0:w]).then_inc(S("dve_freed"), 1)
                if c == 2:
                    dve.wait_ge(S("turned_a"), 2)
                    dve.tensor_copy(qka_flat[:, 512:1024], bank[5][:]).then_inc(S("qka_dve"), 1)
                elif c == 4:
                    for b in range(2, 4):
                        dve.wait_ge(S("turned_b"), b + 1)
                        dve.tensor_copy(cvb[:, 2 * b:2 * b + 2, :],
                                        bank[4 + b][0:MLD, :].rearrange("p (j t) -> p j t", j=2))\
                           .then_inc(S("cvb_dve"), 1)
                elif c == 5:
                    softplus_dve(0, 4)
            dve.wait_ge(S("act_freed"), 7)
            dve.wait_ge(S("dve_freed"), 7)
            gt = V("gt").rearrange("p (a n) -> p a n", a=TT)
            dve.tensor_tensor(gt, z[:, :, Z_GATES:N_IN], gate_b.unsqueeze(1).broadcast_to([P, TT, GATES]), ALU.add)\
               .then_inc(S("gates_ready"), 1)
            softplus_dve(4, 6)
            dve.wait_ge(S("gates_ready"), 1)
            dve.wait_ge(S("gate_log"), 1)
            lf = V("lf").rearrange("p (a n) -> p a n", a=TT)
            dve.scalar_tensor_tensor(lf, gt[:, :, 4:8], 0.0, V("la").rearrange("p (a n) -> p a n", a=TT),
                                     ALU.min, ALU.subtract).then_inc(S("logf_ready"), 1)
            dve.wait_ge(S("cvb_act"), 2)
            dve.wait_ge(S("conv_begun"), 8)
            link(conv_tap(0))
            dve.wait_ge(S("brow_done"), 1)
            link(dve.tensor_copy(rows[0], bank[1][0:MLH, 0:T]))
            link(dve.tensor_tensor(rows[1], bank[1][0:MLH, T:2 * T], rows[0], ALU.subtract))
            link(dve.tensor_tensor_scan(rows[2], rows[1], rows[1], 0.0, ALU.max, ALU.max))
            dve.tensor_tensor(rows[3], rows[0], rows[2], ALU.add).then_inc(S("mrow_ready"), 1)
            for h in range(SBH):
                dve.wait_ge(S("after_a"), h + 1)
                s = sa_flat[:, 384 * h:384 * h + 384]
                ins = dve.tensor_tensor(s, s, bank[(3, 4, 5, 6, 7, 0)[h]][:, 0:384], ALU.subtract)
            ins.then_inc(S("expo_ready"), 1)
            dve.wait_ge(S("cols_done"), 1)
            dve.tensor_copy(V("ccol"), bank[2][:, 0:16]).then_inc(S("ccol_ready"), 1)
            link(conv_tap(1))
            dve.wait_ge(S("weights_a"), 1)
            six = strict.broadcast_to([P, SBH, P])
            dve.tensor_tensor(sa[:, :, 0, :], sa[:, :, 0, :], six, ALU.mult)
            dve.tensor_tensor(sa[:, :, 2, :], sa[:, :, 2, :], six, ALU.mult).then_inc(S("a_ready"), 1)
            conv_tap(2).then_inc(S("conv_done"), 1)
            dve.wait_ge(S("mbc_done"), 1)
            big = C("bigpast").unsqueeze(1).broadcast_to([P, 2, P])
            for k in range(2):
                mb = bank[3 + 4 * k][:].rearrange("p (h b t) -> p h b t", h=2, b=2)
                dve.tensor_tensor(mw[k][:, :, 0, :], mb[:, :, 0, :], big, ALU.add)
                dve.tensor_copy(mw[k][:, :, 1, :], mb[:, :, 1, :])
                ins = dve.tensor_tensor(mw[k][:, :, 2, :], mb[:, :, 1, :], big, ALU.add)
            ins.then_inc(S("mw_ready"), 1)
            dve.wait_ge(S("gelu_ready"), 1)
            vg = [z[:, t, Z_VC:Z_GATES].rearrange("p (g d) -> p g d", g=SGG) for t in range(TT)]
            mu = V("mu").rearrange("p (a g) -> p a g", a=TT)
            ssc = V("ssc").rearrange("p (a g) -> p a g", a=TT)
            rsc = V("rsc").rearrange("p (a g) -> p a g", a=TT)
            sq = [tmp[:, 256 * t:256 * t + 256].rearrange("p (g d) -> p g d", g=SGG) for t in range(TT)]
            wide = lambda v, t: v[:, t, :].unsqueeze(2).broadcast_to([P, SGG, SGD])
            for t in range(TT):
                ins = dve.tensor_reduce(mu[:, t, :], vg[t], AX.X, ALU.add)
            link(ins)
            link(dve.tensor_scalar(V("mu"), V("mu"), 1.0 / SGD, None, ALU.mult))
            for t in range(TT):
                ins = dve.tensor_tensor(vg[t], vg[t], wide(mu, t), ALU.subtract)
            link(ins)
            for t in range(TT):
                ins = dve.tensor_tensor(sq[t], vg[t], vg[t], ALU.mult)
            link(ins)
            for t in range(TT):
                ins = dve.tensor_reduce(ssc[:, t, :], sq[t], AX.X, ALU.add)
            ins.then_inc(S("ln_squares"), 1)
            split_to(13)
            dve.wait_ge(S("ln_rstd"), 1)
            for t in range(TT):
                ins = dve.tensor_tensor(vg[t], vg[t], wide(rsc, t), ALU.mult)
            link(ins)
            for t in range(TT):
                ins = dve.tensor_tensor(z[:, t, Z_VC:Z_GATES], z[:, t, Z_VC:Z_GATES], Q("ln_g"), ALU.mult)
            link(ins)
            for t in range(TT):
                ins = dve.tensor_tensor(z[:, t, Z_VC:Z_GATES], z[:, t, Z_VC:Z_GATES], Q("ln_b"), ALU.add)
            ins.then_inc(S("ln_ready"), 1)
            for h in range(MLH):
                dve.wait_ge(S("scores_b"), h + 1)
                dve.wait_ge(S("decay_ready"), h + 1)
                m = mwh[h]
                dve.scalar_tensor_tensor(m, bank[(4, 5, 6, 0)[h]][:, 0:384].rearrange("p (b t) -> p b t", b=3),
                                         MLD ** -0.5, m, ALU.mult, ALU.mult).then_inc(S("s_ready"), 1)
            dve.wait_ge(S("mixed_done"), 1)
            mx = [bank[3][:, 256 * t:256 * t + 256].rearrange("p (g d) -> p g d", g=SGG) for t in range(TT)]
            yc = [xn[:, t, SBW + MLW:D] for t in range(TT)]
            for t in range(TT):
                ins = dve.tensor_tensor(yc[t].rearrange("p (g d) -> p g d", g=SGG), mx[t],
                                        Q("sgu_b").unsqueeze(2).broadcast_to([P, SGG, SGD]), ALU.add)
            link(ins)
            for t in range(TT):
                ins = dve.tensor_tensor(yc[t], yc[t], z[:, t, Z_UC:Z_VC], ALU.mult)
            ins.then_inc(S("yc_ready"), 1)
            dve.wait_ge(S("out_b"), 1)
            dve.wait_ge(S("ccol_ready"), 1)
            den = V("den")
            for t in range(TT):
                o = bank[6 + t][:, 0:MLW + MLH].rearrange("p (h d) -> p h d", h=MLH)
                ins = dve.scalar_tensor_tensor(den[:, 4 * t:4 * t + 4].unsqueeze(2), o[:, :, MLD:], -1.0,
                                               V("ccol")[:, 8 + 4 * t:12 + 4 * t].unsqueeze(2), ALU.mult, ALU.max)
            link(ins)
            for t in range(TT):
                o = bank[6 + t][:, 0:MLW + MLH].rearrange("p (h d) -> p h d", h=MLH)
                d = den[:, 4 * t:4 * t + 4].unsqueeze(2)
                ins = dve.tensor_tensor(d, o[:, :, MLD:], d, ALU.max)
            link(ins)
            link(dve.reciprocal(den, den))
            hb = [xn[:, t, SBW:SBW + MLW].rearrange("p (h d) -> p h d", h=MLH) for t in range(TT)]
            for t in range(TT):
                o = bank[6 + t][:, 0:MLW + MLH].rearrange("p (h d) -> p h d", h=MLH)
                ins = dve.tensor_tensor(hb[t], o[:, :, 0:MLD],
                                        den[:, 4 * t:4 * t + 4].unsqueeze(2).broadcast_to([P, MLH, MLD]), ALU.mult)
            ins.then_inc(S("hb_ready"), 1)
            dve.wait_ge(S("hb_squares"), 1)
            dve.tensor_reduce(V("ssb"), tmp.rearrange("p (g d) -> p g d", d=MLD), AX.X, ALU.add)\
               .then_inc(S("hb_sums"), 1)
            dve.wait_ge(S("hb_ready"), 1)
            for t in range(TT):
                ins = dve.tensor_tensor(xn[:, t, SBW:SBW + MLW], xn[:, t, SBW:SBW + MLW], z[:, t, Z_OB:Z_UC], ALU.mult)
            link(ins)
            dve.wait_ge(S("hb_rstd"), 1)
            for t in range(TT):
                ins = dve.tensor_tensor(hb[t], hb[t],
                                        V("rsb")[:, 4 * t:4 * t + 4].unsqueeze(2).broadcast_to([P, MLH, MLD]), ALU.mult)
            ins.then_inc(S("xn0_ready"), 1)
            turn_dve(1)
            add_chunks(U_WOUT, C_WOUT)
            norm_dve(1)
            turn_dve(2)
            dve.wait_ge(S("router_done"), 1)
            dve.tensor_copy(logits_t, bank[0][0:NG + NE, 0:T]).then_inc(S("logits_ready"), 1)
            dve.wait_ge(S("logits_turned"), 1)
            lg = V("lg").rearrange("p (a n) -> p a n", a=TT)
            two = lambda v: v.rearrange("p (a n) -> p a n", a=TT)
            over = lambda v, n: v.unsqueeze(2).broadcast_to([P, TT, n])
            same = lambda v, n: v.unsqueeze(1).broadcast_to([P, TT, n])
            NR = NG + NE
            link(dve.tensor_tensor(lg, bank[1][:, 0:2 * NR].rearrange("p (a n) -> p a n", a=TT),
                                   same(Q("router_b"), NR), ALU.add))
            gmax, eqg, ohg, idx = V("gmax"), two(V("eqg")), two(V("ohg")), V("idx")

            def one_hot(oh, scores, top, iota, n, cand):
                link(dve.tensor_reduce(top, scores, AX.X, ALU.max))
                link(dve.tensor_tensor(cand, scores, over(top, n), ALU.is_ge))
                link(dve.scalar_tensor_tensor(cand, cand, -64.0, same(iota, n), ALU.mult, ALU.add))
                link(dve.tensor_reduce(idx, cand, AX.X, ALU.min))
                link(dve.tensor_tensor(oh, cand, over(idx, n), ALU.is_equal))

            one_hot(ohg, lg[:, :, 0:NG], gmax, C("iota4"), NG, eqg)
            eg = two(V("eg"))
            dve.tensor_tensor(eg, lg[:, :, 0:NG], over(gmax, NG), ALU.subtract).then_inc(S("gdiff_ready"), 1)
            link(dve.tensor_scalar(V("pen"), V("ohg"), BIG, -BIG, ALU.mult, ALU.add))
            em, em4 = two(V("em")), V("em").rearrange("p (a g e) -> p a g e", a=TT, g=NG)
            pen = V("pen").rearrange("p (a g) -> p a g", a=TT)
            for t in range(TT):
                ins = dve.tensor_tensor(em4[:, t], lg[:, t, NG:NR].rearrange("p (g e) -> p g e", g=NG),
                                        ohg[:, t, :].unsqueeze(2).broadcast_to([P, NG, EPG]), ALU.mult)
            link(ins)
            for t in range(TT):
                ins = dve.tensor_tensor(em4[:, t], em4[:, t],
                                        pen[:, t, :].unsqueeze(2).broadcast_to([P, NG, EPG]), ALU.add)
            link(ins)
            oh1, oh2, cand = two(V("oh1")), two(V("oh2")), two(V("cand"))
            v1, v2, dv = V("v1"), V("v2"), V("dv")
            one_hot(oh1, em, v1, C("iota32"), NE, cand)
            link(dve.scalar_tensor_tensor(V("em"), V("oh1"), -2.0 * BIG, V("em"), ALU.mult, ALU.add))
            one_hot(oh2, em, v2, C("iota32"), NE, cand)
            dve.tensor_tensor(dv, v2, v1, ALU.subtract).then_inc(S("vdiff_ready"), 1)
            dve.tensor_tensor(V("sel"), V("oh1"), V("oh2"), ALU.add).then_inc(S("sel_ready"), 1)
            dve.wait_ge(S("rank_done"), 1)
            link(dve.scalar_tensor_tensor(V("key"), bank[0][:, 128:192], 1.0, V("sel"), ALU.add, ALU.mult))
            dve.tensor_scalar(V("key"), V("key"), -1.0, None, ALU.add).then_inc(S("key_ready"), 1)
            def pick_pair(p, p0):
                b = p0 % 2
                if p0 >= 2:
                    dve.wait_ge(S("pickw_ready"), p - 1)
                two = slice(2 * p, 2 * p + 2) if isinstance(p, int) else bass.ds(2 * p, 2)
                key = V("key").rearrange("p (a e) -> p a e", a=TT)[:, :, two].unsqueeze(3)
                iota = C("iota64").unsqueeze(1)
                for t in range(TT):
                    ins = dve.tensor_tensor(pick[:, b, t], iota.broadcast_to([P, 2, SLOTS]),
                                            key[:, t].broadcast_to([P, 2, SLOTS]), ALU.is_equal)
                ins.then_inc(S("pick_ready"), 1)

            dve.wait_ge(S("key_ready"), 1)
            pick_pair(0, 0)
            pick_pair(1, 1)
            link(dve.tensor_scalar(V("over"), V("key"), float(SLOTS), None, ALU.is_ge))
            dve.tensor_reduce(V("spill"), V("over"), AX.X, ALU.add).then_inc(S("spill_ready"), 1)
            dve.wait_ge(S("gexp_ready"), 1)
            gw, p1, p2 = V("gw"), V("p1"), V("p2")
            link(dve.tensor_reduce(gw, eg, AX.X, ALU.add))
            dve.wait_ge(S("vexp_ready"), 1)
            link(dve.scalar_tensor_tensor(p1, dv, 1.0, gw, ALU.add, ALU.mult))
            link(dve.reciprocal(p1, p1))
            link(dve.tensor_tensor(p2, p1, dv, ALU.mult))
            dve.tensor_tensor(oh1, oh1, over(p1, NE), ALU.mult)
            link(dve.tensor_tensor(oh2, oh2, over(p2, NE), ALU.mult))
            dve.tensor_tensor(oh1, oh1, oh2, ALU.add).then_inc(S("wt_ready"), 1)
            dve.wait_ge(S("wt_ready"), 1)
            dve.tensor_tensor(V("over"), V("over"), V("oh1"), ALU.mult).then_inc(S("over_ready"), 1)
            for b in range(4, 8):
                dve.memset(bank[b][:], 0.0)
            dve.wait_ge(S("spill_summed"), 1)
            dve.tensor_copy(spill_count[:], bank[0][0:1, 256:257]).then_inc(S("spill_known"), 1)

            def gather_low(k0, wait, at=1):
                dve.wait_ge(S("gather_high"), wait)
                for k in range(4):
                    o = lambda x: x[:, k0 + k, :].rearrange("p (c s) -> p c s", s=SLOTS)[:, 0:3:2, :]
                    ins = dve.scalar_tensor_tensor(o(xglo), bank[at][:, P * k:P * k + P]
                                                   .rearrange("p (c s) -> p c s", s=SLOTS),
                                                   Q("g2")[:, k0 + k:k0 + k + 1], o(xghi).bitcast(F32), ALU.mult,
                                                   ALU.subtract)
                ins.then_inc(S("gather_ready"), 1)

            def turned_low(p, b):
                dve.wait_ge(S("turned_high"), p + 1)
                dve.tensor_tensor(slo[:, b, :], bank[1][:, 0:T], shi[:, b, :].bitcast(F32), ALU.subtract)
                for f in range(2):
                    o = lambda x: x[:, f, :].rearrange("p (c s) -> p c s", s=SLOTS)[:, 0:3:2, :]
                    ins = dve.tensor_tensor(o(htlo), bank[1][:, T + P * f:T + P * f + P]
                                            .rearrange("p (c s) -> p c s", s=SLOTS), o(hthi).bitcast(F32),
                                            ALU.subtract)
                ins.then_inc(S("turned_ready"), 1)

            def y_low(p):
                dve.wait_ge(S("y_high"), p + 1)
                for c in range(2):
                    y = slice(512 * c, 512 * c + 512)
                    ins = dve.tensor_tensor(ylo[:, y], bank[2 + c][:], yhi[:, y].bitcast(F32), ALU.subtract)
                ins.then_inc(S("y_pair"), 1)

            def hidden(p):
                dve.wait_ge(S("pair_silu"), p + 1)
                dve.tensor_tensor(hv, sgl, bank[0][:, 256:512], ALU.mult).then_inc(S("hidden_ready"), 1)

            def pair_dve(p, p0, off):
                n = U_MOE + 6 * p0 - 2
                ahead = (lambda k: split_to(n + k)) if off is None else (lambda k: split((n + k, off)))
                ahead(2)
                turned_low(p - 1, (p0 - 1) % 2)
                if p0 < PAIRS - 1:
                    pick_pair(p + 1, p0 + 1)
                ahead(3)
                ahead(4)
                ahead(5)
                hidden(p)
                if p0 < PAIRS - 1:
                    gather_low(0, 2 * p + 3)
                ahead(6)
                if p0 < PAIRS - 1:
                    gather_low(4, 2 * p + 4)
                ahead(7)
                y_low(p - 1)

            dve.wait_ge(S("zeros_ready"), 1)
            gather_low(0, 1)
            gather_low(4, 2, 2)
            split_to(U_MOE + 5)
            hidden(0)
            gather_low(0, 3)
            gather_low(4, 4, 2)
            pair_dve(1, 1, None)
            with dve.Fori(0, (PAIRS - 4) // 2) as j:
                for b in range(2):
                    pair_dve(2 * j + (2 + b), 2 + b, 4 * j)
            done[0] = U_MOE + 6 * (PAIRS - 2)
            pair_dve(PAIRS - 2, PAIRS - 2, None)
            pair_dve(PAIRS - 1, PAIRS - 1, None)
            turned_low(PAIRS - 1, (PAIRS - 1) % 2)
            y_low(PAIRS - 1)
            dve.wait_ge(S("scattered"), 1)
            overflow_dve(dve)
            add_down(U_MOE + 3 * NE)
            norm_dve(2)
            turn_dve(3)
            dve.wait_ge(S("p_high"), 1)
            dve.tensor_tensor(plo, p_t, phi.bitcast(F32), ALU.subtract).then_inc(S("p_split"), 1)
            split_to(U_PLEP + 1)
            for c in range(2):
                dve.wait_ge(*((S("proj_half"), 1) if c == 0 else (S("unit_used"), U_PLEP + 1)))
                dve.wait_ge(S("act_freed"), sum(BY_ACT[:C_PLEG + c + 1]))
                for t in range(TT):
                    ins = dve.tensor_tensor(gpr[:, t, :], gsb[:, t, 512 * c:512 * c + 512],
                                            bank[2 * ((C_PLEP + c) % 2) + t][:], ALU.mult)
                ins.then_inc(S("dve_freed"), 1)
                dve.wait_ge(S("dve_freed"), sum(BY_DVE[:C_PLEP + c + 1]))
                for t in range(TT):
                    r = xres[:, t, 512 * c:512 * c + 512]
                    ins = dve.tensor_tensor(r, gpr[:, t, :], r, ALU.add)
                    if c == 1 and t == 0:
                        ins.then_inc(S("tile0_ready"), 1)
                if c == 0:
                    link(ins)
            ins.then_inc(S("residual_ready"), 1)
            dve.wait_ge(S("residual_ready"), R_PLE)
            split_to(U_SCIN + 1)
            dve.wait_ge(S("final1_loaded"), 16)
            for t in range(TT):
                dve.wait_ge(S(f"rstd{t}_ready"), 4)
                ins = dve.scalar_tensor_tensor(xres[:, t, :], xres[:, t, :], rstd[:, t:t + 1], final_g,
                                               ALU.mult, ALU.mult)
                ins.then_inc(S("tile0_ready") if t == 0 else S("residual_ready"), 1)
            dve.wait_ge(S("residual_ready"), R_FINAL1)
            norm_dve(4)
            link(dve.memset(cvp[:, :, 0:2], 0.0))
            turn_dve(4)
            for i in range(6):
                split_to(U_SCIN + 2 * i + 3)
                g = G_SC + i
                dve.wait_ge(S("unit_used"), U_SCIN + 2 * i + 2)
                if i < 4:
                    dve.wait_ge(S("c_ready"), i + 1)
                    dve.tensor_tensor(cvp[:, 2 * i:2 * i + 2, 2:2 + T],
                                      csb[:, i % 2, :].rearrange("p (j t) -> p j t", j=2),
                                      bank[2 * (g % 2) + 1][:].rearrange("p (j t) -> p j t", j=2), ALU.mult)\
                       .then_inc(S("g_free"), 1)
                    dve.wait_ge(S("g_free"), g + 1)
                    dve.wait_ge(S("sc_begun"), i + 1)
                    for k in range(1, -1, -1):
                        for f in range(2 * i, 2 * i + 2):
                            ins = dve.scalar_tensor_tensor(scy[:, f, :], cvp[:, f, k:k + T], sc_conv[:, k, f:f + 1],
                                                           scy[:, f, :], ALU.mult, ALU.add)
                        link(ins)
                else:
                    f = 4 * (i - 4)
                    for k in range(2):
                        y = scy[:, f + 2 * k:f + 2 * k + 2, :]
                        dve.tensor_tensor(y, y, bank[2 * (g % 2) + k][:].rearrange("p (j t) -> p j t", j=2), ALU.mult)\
                           .then_inc(S("sc_product") if k == 0 else S("g_free"), 1)
            for f in range(4):
                dve.wait_ge(S("sc_high"), f + 1)
                dve.tensor_tensor(xlo[:, 2 * f:2 * f + 2, :], scy[:, 2 * f:2 * f + 2, :],
                                  xhi[:, 2 * f:2 * f + 2, :].bitcast(F32), ALU.subtract).then_inc(S("sc_ready"), 1)
            add_chunks(U_SCOUT, C_SCOUT)

            def ffn_dve(layer, e, off, e0):
                g0, d0, u0 = (G_FFN0, 0, U_FFN0) if layer == 0 else (G_FFN1, FE, U_FFN1)
                b, gb = e0 % 2, (g0 + e0) % 2
                n = u0 + 3 * e0 - 1

                def ahead(k):
                    if off is None:
                        split_to(n + k)
                    elif n + k < UNITS:
                        split((n + k, off))
                ahead(3)
                dve.wait_ge(S("ffn_begun"), layer * FE + 1 + e)
                for k in range(1, -1, -1):
                    for f in range(4):
                        src = bank[2 * gb + f // 2][:, (f % 2) * T:(f % 2 + 1) * T]
                        a = facc[:, b, f, 2 - k:T]
                        ins = dve.scalar_tensor_tensor(a, src[:, 0:T - 2 + k], cwn[:, b, 4 * k + f:4 * k + f + 1], a,
                                                       ALU.mult, ALU.add)
                    if k == 1:
                        link(ins)
                ins.then_inc(S("g_free"), 1)
                ahead(4)
                dve.wait_ge(S("g_free"), g0 + 1 + e)
                dve.wait_ge(S("silu_ready"), layer * FE + 1 + e)
                dve.tensor_tensor(facc[:, b, 2:4, :], facc[:, b, 0:2, :], facc[:, b, 2:4, :], ALU.mult)\
                   .then_inc(S("hv_ready"), 1)
                ahead(5)
                dve.wait_ge(S("hhi_ready"), d0 + 1 + e)
                dve.tensor_tensor(hlo[:, b, :, :], facc[:, b, 2:4, :], hhi[:, b, :, :].bitcast(F32), ALU.subtract)\
                   .then_inc(S("h_ready"), 1)

            def ffn(layer):
                ffn_dve(layer, 0, None, 0)
                ffn_dve(layer, 1, None, 1)
                u0 = U_FFN0 if layer == 0 else U_FFN1
                with dve.Fori(0, (FE - 3) // 2) as j:
                    chain.enter(j, 2)
                    for b in range(2):
                        ffn_dve(layer, 2 * j + (2 + b), 2 * j, 2 + b)
                    chain.leave(2, (FE - 3) // 2)
                done[0] = u0 + 3 * (FE - 1) + 2
                ffn_dve(layer, FE - 1, None, FE - 1)

            norm_dve(5)
            turn_dve(5)
            ffn(0)
            add_down(U_FFN0 + 3 * FE)
            norm_dve(6)
            turn_dve(6)
            cos = C("cos").rearrange("p (a n) -> p a n", a=TT)
            sin = C("sin").rearrange("p (a n) -> p a n", a=TT)
            rot = rp.rearrange("p k (h n) -> p k h n", h=8)
            for c in range(4):
                split_to(U_QKV + 2 * c + 3)
                dve.wait_ge(S("unit_used"), CHUNK_END[C_QKV + c])
                for t in range(TT):
                    src = bank[2 * ((C_QKV + c) % 2) + t][:].rearrange("p (h n) -> p h n", h=8)
                    dst = qkv[:, t, 512 * c:512 * c + 512].rearrange("p (h n) -> p h n", h=8)
                    cb = cos[:, t, :].unsqueeze(1).broadcast_to([P, 8, HALF])
                    sb_ = sin[:, t, :].unsqueeze(1).broadcast_to([P, 8, HALF])
                    x1, x2 = src[:, :, 0:HALF], src[:, :, HALF:HD]
                    dve.tensor_tensor(rot[:, 0], x1, cb, ALU.mult)
                    dve.tensor_tensor(rot[:, 1], x2, sb_, ALU.mult)
                    dve.tensor_tensor(rot[:, 2], x2, cb, ALU.mult)
                    link(dve.tensor_tensor(rot[:, 3], x1, sb_, ALU.mult))
                    dve.tensor_tensor(dst[:, :, 0:HALF], rot[:, 0], rot[:, 1], ALU.subtract)
                    ins = dve.tensor_tensor(dst[:, :, HALF:HD], rot[:, 2], rot[:, 3], ALU.add)
                    if t == 0:
                        link(ins)
                ins.then_inc(S("dve_freed"), 1)
                dve.wait_ge(S("dve_freed"), sum(BY_DVE[:C_QKV + c + 1]))
            split_to(U_WO)

            def attend_norm(h):
                b = h % 3
                dve.wait_ge(S("exp_done"), h + 1)
                link(dve.reciprocal(V("rl")[:, 2 * b:2 * b + 2], V("l")[:, 2 * b:2 * b + 2]))
                dve.tensor_scalar(ap_[:, b, 0:128], ap_[:, b, 0:128], V("rl")[:, 2 * b:2 * b + 1], None, ALU.mult)
                dve.tensor_scalar(ap_[:, b, 128:384], ap_[:, b, 128:384], V("rl")[:, 2 * b + 1:2 * b + 2], None,
                                  ALU.mult).then_inc(S("p_ready"), 1)

            for h in range(NH):
                b = h % 3
                dve.wait_ge(S("scores_done"), h + 1)
                dve.tensor_reduce(V("m")[:, 2 * b:2 * b + 1], bank[b][:, 0:128], AX.X, ALU.max)
                link(dve.tensor_reduce(V("m")[:, 2 * b + 1:2 * b + 2], bank[b][:, 128:384], AX.X, ALU.max))
                dve.tensor_scalar(V("nm")[:, 2 * b:2 * b + 2], V("m")[:, 2 * b:2 * b + 2], -(HD ** -0.5), None,
                                  ALU.mult).then_inc(S("negmax_ready"), 1)
                if h >= 1:
                    attend_norm(h - 1)
            attend_norm(NH - 1)
            split_to(U_WO + 1)
            for b in range(4):
                dve.wait_ge(S("o_high"), b + 1)
                dve.tensor_tensor(xlo[:, 2 * b:2 * b + 2, :], bank[4 + b][:].rearrange("p (j t) -> p j t", j=2),
                                  xhi[:, 2 * b:2 * b + 2, :].bitcast(F32), ALU.subtract).then_inc(S("o_ready"), 1)
            add_chunks(U_WO, C_WO)
            norm_dve(7)
            turn_dve(7)
            ffn(1)
            add_down(UNITS)
            dve.wait_ge(S("residual_ready"), R_FFN1)
            dve.wait_ge(S("final2_loaded"), 16)
            for t in range(TT):
                dve.wait_ge(S(f"rstd{t}_ready"), 9)
                dve.scalar_tensor_tensor(xn[:, t, :], xres[:, t, :], rstd[:, t:t + 1], final_g,
                                         ALU.mult, ALU.mult).then_inc(S("y_ready"), 1)

        @block.tensor
        def _(pe):
            def wait_unit(n):
                unit0, off = n if isinstance(n, tuple) else (n, 0)
                pe.wait_ge(S("low_done"), (off if isinstance(off, int) else off * RING) + unit0 + 1)
                return unit0 % RING

            def mm3(o, ah, al, bh, bl, start, stop=False):
                pe.matmul(o, ah, bh, start=start, stop=False, skip_group_check=True)
                pe.matmul(o, ah, bl, start=False, stop=False, skip_group_check=True)
                return pe.matmul(o, al, bh, start=False, stop=stop, skip_group_check=True)

            def turn(q):
                pe.wait_ge(S("xn0_ready"), q + 1)
                pe.wait_ge(S("xn1_ready"), q + 1)
                for k in range(KD):
                    for t in range(TT):
                        ins = pe.transpose(bank[4 + k // 2][:, (k % 2) * T + t * P:(k % 2) * T + t * P + P],
                                           xn[:, t, P * k:P * k + P], ident)
                    if k % 2:
                        ins.then_inc(S("turned"), 1)

            def wait_turned(q, k):
                if isinstance(q, str) and k % 2 == 0:
                    pe.wait_ge(S(q), k // 2 + 1)
                elif q is not None and k % 2 == 0:
                    pe.wait_ge(S("xt_ready"), 4 * q + k // 2 + 1)

            def dense(g, u0, q=None):
                if g >= 2:
                    if sum(BY_ACT[:g - 1]):
                        pe.wait_ge(S("act_freed"), sum(BY_ACT[:g - 1]))
                    pe.wait_ge(S("dve_freed"), sum(BY_DVE[:g - 1]))
                for u in range(2):
                    s = wait_unit(u0 + u)
                    for k in range(4):
                        kk = 4 * u + k
                        wait_turned(q, kk)
                        for t in range(TT):
                            w = slice(512 * k, 512 * k + 512)
                            ins = mm3(bank[2 * (g % 2) + t][:], xhi[:, kk, P * t:P * t + P], xlo[:, kk, P * t:P * t + P],
                                      whi[:, s, w], wlo[:, s, w], start=kk == 0, stop=kk == 7)
                    ins.then_inc(S("unit_used"), 1)

            pe.wait_ge(S("table_loaded"), 16)
            turn(0)
            def turn_queries():
                pe.wait_ge(S("act_freed"), 2)
                pe.wait_ge(S("dve_freed"), 2)
                for j in range(6):
                    for t in range(TT):
                        at = j * T + t * P
                        ins = pe.transpose(bank[4 + at // 512][:, at % 512:at % 512 + P], z[:, t, P * j:P * j + P],
                                           ident)
                    if j % 2:
                        ins.then_inc(S("turned_a"), 1)

            def scores_a(h0, h1):
                for h in range(h0, h1):
                    p0 = 64 * (h % 2)
                    q_, k_ = qka[p0:p0 + 64, h // 2, :], qka[p0:p0 + 64, 3 + h // 2, :]
                    b = bank[4 + h % 4]
                    pe.matmul(b[:, 0:256], k_[:, 0:P], q_, start=True, stop=True, skip_group_check=True)
                    pe.matmul(b[:, 256:384], k_[:, P:T], q_[:, P:T], start=True, stop=True, skip_group_check=True)\
                      .then_inc(S("scores_a"), 1)

            def turn_conv_inputs():
                pe.wait_ge(S("act_freed"), 4)
                pe.wait_ge(S("dve_freed"), 4)
                pe.wait_ge(S("logits_act"), 4)
                for j in range(8):
                    for t in range(TT):
                        ins = pe.transpose(bank[4 + j // 2][0:MLD, (j % 2) * T + t * P:(j % 2) * T + t * P + P],
                                           z[:, t, Z_QB + MLD * j:Z_QB + MLD * j + MLD], ident)
                    if j % 2:
                        ins.then_inc(S("turned_b"), 1)

            for c in range(6):
                dense(C_WIN + c, U_WIN + 2 * c, 0 if c == 0 else None)
                if c == 2:
                    turn_queries()
                elif c == 3:
                    pe.wait_ge(S("qka_act"), 2)
                    pe.wait_ge(S("qka_dve"), 1)
                    scores_a(0, 4)
                elif c == 4:
                    turn_conv_inputs()
                elif c == 5:
                    pe.wait_ge(S("cvb_act"), 2)
                    scores_a(4, 6)
            pe.wait_ge(S("act_freed"), 5)
            pe.wait_ge(S("dve_freed"), 5)
            s = wait_unit(12)
            for k in range(KD):
                for t in range(TT):
                    w = slice(TAIL * k, TAIL * k + TAIL)
                    ins = mm3(bank[t][:, 0:TAIL], xhi[:, k, P * t:P * t + P], xlo[:, k, P * t:P * t + P],
                              whi[:, s, w], wlo[:, s, w], start=k == 0, stop=k == 7)
            ins.then_inc(S("unit_used"), 1)
            lf = V("lf").rearrange("p (a n) -> p a n", a=TT)
            gt = V("gt").rearrange("p (a n) -> p a n", a=TT)
            upto, ones, later = C("upto"), C("ones"), C("later")

            def after(h0, h1):
                for h in range(h0, h1):
                    b = bank[(3, 4, 5, 6, 7, 0)[h]]
                    l = t1_flat[:, 384 * h:384 * h + 384]
                    pe.matmul(b[:, 0:384], later, l, start=True, stop=False, skip_group_check=True)
                    pe.matmul(b[:, 128:256], ones, l[:, 256:384], start=False, stop=True, skip_group_check=True)\
                      .then_inc(S("after_a"), 1)

            pe.wait_ge(S("dve_freed"), 6)
            pe.wait_ge(S("cvb_dve"), 2)
            pe.wait_ge(S("logits_act"), 6)
            pe.wait_ge(S("l_ready"), 1)
            after(0, 4)
            pe.wait_ge(S("act_freed"), 7)
            pe.wait_ge(S("dve_freed"), 7)
            pe.wait_ge(S("logf_ready"), 1)
            r = bank[1][0:MLH, :]
            pe.matmul(r[:, 0:P], lf[:, 0, :], upto, start=True, stop=True, skip_group_check=True)
            pe.matmul(r[:, P:T], lf[:, 0, :], ones, start=True, stop=False, skip_group_check=True)
            pe.matmul(r[:, P:T], lf[:, 1, :], upto, start=False, stop=True, skip_group_check=True)
            pe.transpose(r[:, T:T + P], gt[:, 0, 0:4], ident)
            pe.transpose(r[:, T + P:2 * T], gt[:, 1, 0:4], ident).then_inc(S("brow_done"), 1)
            pe.wait_ge(S("l_ready"), 2)
            after(4, 6)
            pe.wait_ge(S("mrow_ready"), 1)
            pe.wait_ge(S("enrow_ready"), 1)
            for t in range(TT):
                pe.transpose(bank[2][:, 4 * t:4 * t + 4], rows[1][:, P * t:P * t + P], ident[0:4, 0:4])
                ins = pe.transpose(bank[2][:, 8 + 4 * t:12 + 4 * t], rows[4][:, P * t:P * t + P], ident[0:4, 0:4])
            ins.then_inc(S("cols_done"), 1)
            pe.wait_ge(S("expo_ready"), 1)
            for h in range(MLH):
                ins = pe.matmul(bank[3 + 4 * (h // 2)][:, (h % 2) * T:(h % 2 + 1) * T],
                                ident[0:4, h:h + 1].broadcast_to([4, P]), rows[2], start=True, stop=True,
                                skip_group_check=True)
            ins.then_inc(S("mbc_done"), 1)
            pe.wait_ge(S("a_ready"), 1)
            pe.wait_ge(S("ccol_ready"), 1)
            for h in range(SBH):
                v = [z[:, t, 2 * SBW + 64 * h:2 * SBW + 64 * h + 64] for t in range(TT)]
                o = [bank[1 + t][:, 64 * h:64 * h + 64] for t in range(TT)]
                pe.matmul(o[0], sa[:, h, 0, :], v[0], start=True, stop=True, skip_group_check=True)
                pe.matmul(o[1], sa[:, h, 1, :], v[0], start=True, stop=False, skip_group_check=True)
                ins = pe.matmul(o[1], sa[:, h, 2, :], v[1], start=False, stop=True, skip_group_check=True)
            ins.then_inc(S("out_a"), 1)
            pe.wait_ge(S("qkb_ready"), 1)
            for h in range(MLH):
                b = bank[(4, 5, 6, 0)[h]]
                q_, k_ = qkb[:, h, :], qkb[:, 4 + h, :]
                pe.matmul(b[:, 0:256], k_[:, 0:P], q_, start=True, stop=True, skip_group_check=True)
                pe.matmul(b[:, 256:384], k_[:, P:T], q_[:, P:T], start=True, stop=True, skip_group_check=True)\
                  .then_inc(S("scores_b"), 1)
            pe.wait_ge(S("mw_ready"), 1)
            pe.wait_ge(S("ln_ready"), 1)
            pe.wait_ge(S("sgu_masked"), 1)
            for t in range(TT):
                for g in range(SGG):
                    ins = pe.matmul(bank[3][:, 256 * t + 64 * g:256 * t + 64 * g + 64], sgu_w[:, g, :],
                                    z[:, t, Z_VC + 64 * g:Z_VC + 64 * g + 64], start=True, stop=True,
                                    skip_group_check=True)
            ins.then_inc(S("mixed_done"), 1)
            pe.wait_ge(S("s_ready"), 4)
            pe.wait_ge(S("values_ready"), 1)
            for h in range(MLH):
                w = slice((MLD + 1) * h, (MLD + 1) * (h + 1))
                pe.matmul(bank[6][:, w], mwh[h][:, 0, :], vext[:, 0, h, :], start=True, stop=True,
                          skip_group_check=True)
                pe.matmul(bank[7][:, w], mwh[h][:, 1, :], vext[:, 0, h, :], start=True, stop=False,
                          skip_group_check=True)
                ins = pe.matmul(bank[7][:, w], mwh[h][:, 2, :], vext[:, 1, h, :], start=False, stop=True,
                                skip_group_check=True)
            ins.then_inc(S("out_b"), 1)
            turn(1)
            for c in range(2):
                dense(C_WOUT + c, U_WOUT + 2 * c, 1 if c == 0 else None)
            turn(2)
            pe.wait_ge(S("setup_low"), 1)
            NR = NG + NE
            for k in range(KD):
                wait_turned(2, k)
                ins = mm3(bank[0][0:NR, 0:T], rhi[:, k, :], rlo[:, k, :], xhi[:, k, :], xlo[:, k, :],
                          start=k == 0, stop=k == 7)
            ins.then_inc(S("router_done"), 1)
            pe.wait_ge(S("logits_ready"), 1)
            for t in range(TT):
                ins = pe.transpose(bank[1][:, NR * t:NR * t + NR], logits_t[:, P * t:P * t + P], ident[0:NR, 0:NR])
            ins.then_inc(S("logits_turned"), 1)
            pe.wait_ge(S("sel_ready"), 1)
            sel = V("sel").rearrange("p (a n) -> p a n", a=TT)
            strict = C("strict")
            pe.matmul(bank[0][:, 128:160], strict, sel[:, 0, :], start=True, stop=True, skip_group_check=True)
            pe.matmul(bank[0][:, 160:192], ones, sel[:, 0, :], start=True, stop=False, skip_group_check=True)
            pe.matmul(bank[0][:, 160:192], strict, sel[:, 1, :], start=False, stop=True, skip_group_check=True)\
              .then_inc(S("rank_done"), 1)
            def gather(q0, p, k0, at=1):
                if k0 == 0:
                    pe.wait_ge(S("pick_ready"), p + 1)
                b = q0 % 2
                for k in range(4):
                    o = bank[at][:, P * k:P * k + P]
                    w = slice(P * (k0 + k), P * (k0 + k) + P)
                    for t in range(TT):
                        sl = pick[:, b, t].rearrange("p e s -> p (e s)")
                        pe.matmul(o, xtok_hi[:, t, w], sl, start=t == 0, stop=False, skip_group_check=True)
                        ins = pe.matmul(o, xtok_lo[:, t, w], sl, start=False, stop=t == 1, skip_group_check=True)
                ins.then_inc(S("gathered"), 1)

            def pair_gate_up(e, u):
                unit0, off = u
                w = slice(SLOTS * e, SLOTS * e + P)
                for i in range(2):
                    s = wait_unit((unit0 + i, off))
                    for k in range(4):
                        kk = 4 * i + k
                        c = slice(512 * k, 512 * k + 512)
                        ins = mm3(bank[0][:], xghi[:, kk, w], xglo[:, kk, w], whi[:, s, c], wlo[:, s, c],
                                  start=e == 0 and kk == 0)
                    ins.then_inc(S("unit_used"), 1)

            def pair_down(e, u):
                s = wait_unit(u)
                w = slice(SLOTS * e, SLOTS * e + P)
                for c in range(2):
                    for f in range(2):
                        v = slice(D * f + 512 * c, D * f + 512 * c + 512)
                        ins = mm3(bank[2 + c][:], hthi[:, f, w], htlo[:, f, w], whi[:, s, v], wlo[:, s, v],
                                  start=e == 0 and f == 0)
                ins.then_inc(S("unit_used"), 1)

            def scatter(p, p0, last=False):
                pe.wait_ge(S("y_pair"), p + 1)
                b = p0 % 2
                for t in range(TT):
                    for c in range(2):
                        y = slice(512 * c, 512 * c + 512)
                        a = slice(P * t, P * t + P)
                        ins = mm3(bank[4 + 2 * t + c][:], shi[:, b, a], slo[:, b, a], yhi[:, y], ylo[:, y],
                                  start=False)
                if last:
                    ins.then_inc(S("scattered"), 1)

            def turn_pair(p, p0):
                pe.wait_ge(S("hidden_ready"), p + 1)
                pe.wait_ge(S("pickw_ready"), p + 1)
                if p0 < PAIRS - 1:
                    pe.wait_ge(S("gather_ready"), 2 * p + 4)
                for t in range(TT):
                    pe.transpose(bank[1][:, P * t:P * t + P],
                                 pickw[:, p0 % 2, t].rearrange("p e s -> p (e s)"), ident)
                for f in range(2):
                    ins = pe.transpose(bank[1][:, T + P * f:T + P * f + P], hv[:, P * f:P * f + P], ident)
                ins.then_inc(S("turned_pair"), 1)

            def pair_step(p, p0, off):
                n = U_MOE + 6 * p0 - 2
                pair_gate_up(0, (n, off))
                if p0 >= 2:
                    scatter(p - 2, p0 - 2)
                pair_gate_up(1, (n + 2, off))
                pe.wait_ge(S("turned_ready"), p)
                if p0 < PAIRS - 1:
                    gather(p0 + 1, p + 1, 0)
                pair_down(0, (n + 4, off))
                if p0 < PAIRS - 1:
                    pe.wait_ge(S("gather_ready"), 2 * p + 3)
                    gather(p0 + 1, p + 1, 4)
                pair_down(1, (n + 5, off))
                turn_pair(p, p0)

            pe.wait_ge(S("xtok_ready"), 1)
            gather(0, 0, 0)
            pe.wait_ge(S("spill_ready"), 1)
            pe.matmul(bank[0][0:1, 256:257], V("spill"), ones[:, 0:1], start=True, stop=True, skip_group_check=True)\
              .then_inc(S("spill_summed"), 1)
            gather(0, 0, 4, 2)
            pe.wait_ge(S("gather_ready"), 2)
            pe.wait_ge(S("spill_known"), 1)
            pair_gate_up(0, (U_MOE, 0))
            pair_gate_up(1, (U_MOE + 2, 0))
            gather(1, 1, 0)
            gather(1, 1, 4, 2)
            turn_pair(0, 0)
            pair_step(1, 1, 0)
            with pe.Fori(0, (PAIRS - 4) // 2) as j:
                for b in range(2):
                    pair_step(2 * j + (2 + b), 2 + b, 4 * j)
            pair_step(PAIRS - 2, PAIRS - 2, 0)
            pair_step(PAIRS - 1, PAIRS - 1, 0)
            scatter(PAIRS - 2, PAIRS - 2)
            pe.wait_ge(S("turned_ready"), PAIRS)
            pair_down(0, (U_MOE + 3 * NE - 2, 0))
            pair_down(1, (U_MOE + 3 * NE - 1, 0))
            scatter(PAIRS - 1, PAIRS - 1, last=True)
            overflow_pe(pe)

            def group(g0, u, q=None):
                unit0, off = u if isinstance(u, tuple) else (u, 0)
                for i in range(2):
                    s = wait_unit((unit0 + i, off))
                    for k in range(4):
                        kk = 4 * i + k
                        wait_turned(q, kk)
                        for f in range(4):
                            o = bank[2 * (g0 % 2) + f // 2][:, (f % 2) * T:(f % 2 + 1) * T]
                            w = slice(512 * k + P * f, 512 * k + P * f + P)
                            first = kk == 0 and f % 2 == 0
                            pe.matmul(o, whi[:, s, w], xhi[:, kk, :], start=first, stop=False, skip_group_check=True)
                            pe.matmul(o, whi[:, s, w], xlo[:, kk, :], start=False, stop=False, skip_group_check=True)
                            ins = pe.matmul(o, wlo[:, s, w], xhi[:, kk, :], start=False, stop=kk == 7,
                                            skip_group_check=True)
                    ins.then_inc(S("unit_used"), 1)

            def down(b, u, first):
                unit0, off = u if isinstance(u, tuple) else (u, 0)
                s = wait_unit(u)
                for t in range(TT):
                    for c in range(2):
                        for f in range(2):
                            w = slice(D * f + 512 * c, D * f + 512 * c + 512)
                            ins = mm3(bank[4 + 2 * t + c][:], hhi[:, b, f, P * t:P * t + P], hlo[:, b, f, P * t:P * t + P],
                                      whi[:, s, w], wlo[:, s, w], start=first and f == 0)
                ins.then_inc(S("unit_used"), 1)

            def expert_step(g0, d0, u0, e, e0, off):
                n = u0 + 2 + 3 * e0
                pe.wait_ge(S("g_free"), g0 + e)
                group(g0 + e0 + 1, (n, off))
                pe.wait_ge(S("h_ready"), d0 + 1 + e)
                down(e0 % 2, (n + 2, off), first=e0 == 0)

            def experts(g0, d0, u0, count, q):
                pe.wait_ge(S("g_free"), g0 - 1)
                group(g0, u0, q)
                expert_step(g0, d0, u0, 0, 0, 0)
                pairs = (count - 2) // 2
                with pe.Fori(0, pairs) as j:
                    for b in range(2):
                        expert_step(g0, d0, u0, 2 * j + (1 + b), 1 + b, 2 * j)
                for e in range(1 + 2 * pairs, count - 1):
                    expert_step(g0, d0, u0, e, e, 0)
                pe.wait_ge(S("h_ready"), d0 + count)
                down((count - 1) % 2, u0 + 3 * count - 1, first=False)

            turn(3)
            for c in range(2):
                dense(C_PLEG + c, U_PLEG + 2 * c, 3 if c == 0 else None)
            pe.wait_ge(S("p_split"), 1)
            s = wait_unit(U_PLEP)
            for c in range(2):
                g = C_PLEP + c
                pe.wait_ge(S("act_freed"), sum(BY_ACT[:g - 1]))
                for t in range(TT):
                    for k in range(2):
                        w = slice(D * k + 512 * c, D * k + 512 * c + 512)
                        ins = mm3(bank[2 * (g % 2) + t][:], phi[:, k, P * t:P * t + P], plo[:, k, P * t:P * t + P],
                                  whi[:, s, w], wlo[:, s, w], start=k == 0, stop=k == 1)
                ins.then_inc(S("proj_half") if c == 0 else S("unit_used"), 1)
            turn(4)
            for i in range(6):
                if i >= 2:
                    pe.wait_ge(S("g_free"), G_SC + i - 1)
                group(G_SC + i, U_SCIN + 2 * i, 4 if i == 0 else None)
            pe.wait_ge(S("g_free"), G_SC + 6)
            for c in range(2):
                dense(C_SCOUT + c, U_SCOUT + 2 * c, "sc_ready" if c == 0 else None)
            turn(5)
            experts(G_FFN0, 0, U_FFN0, FE, 5)
            turn(6)
            def turn_heads(half):
                pe.wait_ge(S("dve_freed"), sum(BY_DVE[:C_QKV + 2 * half + 2]))
                if half:
                    pe.wait_ge(S("qkt_ready"), 4)
                for j in range(8):
                    for t in range(TT):
                        w = D * half + P * j
                        ins = pe.transpose(bank[4 + j // 2][:, (j % 2) * T + t * P:(j % 2) * T + t * P + P],
                                           qkv[:, t, w:w + P], ident)
                    if j % 2:
                        ins.then_inc(S("qk_turned"), 1)

            for c in range(6):
                dense(C_QKV + c, U_QKV + 2 * c, 6 if c == 0 else None)
                if c in (3, 4):
                    turn_heads(c - 3)
            pe.wait_ge(S("act_freed"), sum(BY_ACT[:C_QKV + 6]))
            pe.wait_ge(S("qkt_ready"), 8)
            pe.wait_ge(S("mask_ready"), 1)

            def scores(h):
                b, p0 = h % 3, 64 * (h % 2)
                q_, k_ = qkt[p0:p0 + 64, h // 2, :], qkt[p0:p0 + 64, 8 + h // 2, :]
                if h >= 3:
                    pe.wait_ge(S("exp_done"), h - 2)
                pe.matmul(bank[b][:, 0:128], q_[:, 0:P], k_[:, 0:P], start=True, stop=False, skip_group_check=True)
                pe.matmul(bank[b][:, 0:128], ident_r, causal_r, start=False, stop=True, skip_group_check=True)
                pe.matmul(bank[b][:, 128:384], q_[:, P:T], k_, start=True, stop=False, skip_group_check=True)
                pe.matmul(bank[b][:, 256:384], ident_r, causal_r, start=False, stop=True, skip_group_check=True)\
                  .then_inc(S("scores_done"), 1)

            def turn_p(h):
                pe.wait_ge(S("p_ready"), h + 1)
                if h >= 1:
                    pe.wait_ge(S("pt_ready"), h)
                for k in range(3):
                    ins = pe.transpose(bank[3][:, P * k:P * k + P], ap_[:, h % 3, P * k:P * k + P], ident)
                ins.then_inc(S("p_turned"), 1)

            def values(h):
                b, j = h % 2, h // 2
                pe.wait_ge(S("pt_ready"), h + 1)
                v = [qkv[:, t, 2 * D + HD * h:2 * D + HD * h + HD] for t in range(TT)]
                o = bank[4 + j // 2][64 * (h % 2):64 * (h % 2) + 64, (j % 2) * T:(j % 2 + 1) * T]
                pe.matmul(o, v[0], apt[:, b, 0:256], start=True, stop=False, skip_group_check=True)
                pe.matmul(o[:, P:T], v[1], apt[:, b, 256:384], start=False, stop=True, skip_group_check=True)\
                  .then_inc(S("pv_done"), 1)

            for h in range(3):
                scores(h)
            for h in range(NH):
                turn_p(h)
                if h + 3 < NH:
                    scores(h + 3)
                values(h)
            for c in range(2):
                dense(C_WO + c, U_WO + 2 * c, "o_ready" if c == 0 else None)
            turn(7)
            experts(G_FFN1, FE, U_FFN1, FE, 7)


def constants():
    t = np.zeros((P, CONST_W), np.float32)

    def put(name, v):
        a, b = CONST[name]
        t[:, a:b] = np.asarray(v, np.float32).reshape(-1, b - a)

    i, j = np.arange(P)[:, None], np.arange(P)[None, :]
    put("ident", i == j)
    put("later", i > j)
    put("ones", np.ones((P, P)))
    put("upto", i <= j)
    put("strict", i < j)
    put("bigpast", np.where(i > j, BIG, 0.0))
    put("causal", np.where(j > i, -BIG, 0.0))
    inv = np.float32(10000.0) ** (-np.arange(HALF, dtype=np.float32) / np.float32(HALF))
    ang = np.arange(T, dtype=np.float32)[:, None] * inv.astype(np.float32)[None, :]
    for name, f in (("cos", np.cos), ("sin", np.sin)):
        put(name, f(ang).reshape(TT, P, HALF).transpose(1, 0, 2).reshape(P, -1))
    put("iota4", np.broadcast_to(np.arange(NG), (P, NG)))
    put("iota32", np.broadcast_to(np.arange(NE), (P, NE)))
    put("neghalf", np.full((P, 8), -0.5))
    put("iota64", np.broadcast_to(np.arange(SLOTS), (P, SLOTS)))
    return t


def rows_units(w, cols=512):
    k, n = w.shape
    per = UNIT // cols
    v = w.reshape(k // P // per, per, P, n // cols, cols)
    return v.transpose(3, 0, 2, 1, 4).reshape(-1, P, UNIT)


def expert_units(pairs, downs, together=1):
    e = pairs.shape[0]
    g = pairs.reshape(e, 2, 4, P, 512).transpose(0, 1, 3, 2, 4).reshape(e, 2, P, UNIT)
    d = downs.reshape(e, 2, P, D).transpose(0, 2, 1, 3).reshape(e, 1, P, UNIT)
    g, d = g.reshape(e // together, -1, P, UNIT), d.reshape(e // together, -1, P, UNIT)
    parts = [g[0]]
    for n in range(e // together - 1):
        parts += [g[n + 1], d[n]]
    parts.append(d[-1])
    return np.concatenate(parts)


def kernel(x, p, norm1_g, w_in, conv_w, conv_b, igate_b, fgate_b, mnorm_g, sb_out_g, sgu_ln_g, sgu_ln_b, sgu_w,
           sgu_b, sgu_out_g, w_out, norm2_g, router_gw, router_gb, router_ew, router_eb, w_gate, w_up, w_down,
           ple_norm_g, ple_gate_w, ple_proj_w, final_g, mix_norm_2, sc_w_in_2, sc_w_conv_2, sc_w_out_2, moba_w_qkv_2,
           moba_w_o_2, ffn_norm_2, ffn_w_up_2, ffn_w_conv_2, ffn_w_down_2, final_norm_2):
    import concourse.bacc as _bacc
    from concourse.bass_utils import run_bass_kernel_spmd as _run

    w = w_in[0]
    g0 = 3 * SBW + 4 * MLW
    w = np.concatenate([w[:, :g0], w[:, g0 + GATES:], w[:, g0:g0 + GATES]], axis=1)
    tail = w[:, 6 * 512:].reshape(KD, P, TAIL).transpose(1, 0, 2).reshape(P, KD * TAIL)
    tail = np.concatenate([tail, np.zeros((P, UNIT - KD * TAIL), w.dtype)], axis=1)[None]

    sc = sc_w_in_2[0]
    b_, c_, v_ = sc[:, :D], sc[:, D:2 * D], sc[:, 2 * D:]
    sc_cols = [np.concatenate([c_[:, 256 * i:256 * i + 256], v_[:, 256 * i:256 * i + 256]], axis=1) for i in range(4)]
    sc_cols = np.concatenate(sc_cols + [b_], axis=1)

    def ffn_units(layer):
        up = ffn_w_up_2[layer]
        pairs = np.concatenate([up[:, :FF].reshape(D, FE, 256), up[:, FF:].reshape(D, FE, 256)], axis=2)
        return expert_units(pairs.transpose(1, 0, 2), ffn_w_down_2[layer].reshape(FE, 256, D))

    stream = np.concatenate([
        rows_units(w[:, :6 * 512]), tail, rows_units(w_out[0]),
        expert_units(np.concatenate([w_gate[0], w_up[0]], axis=2), w_down[0], 2),
        rows_units(ple_gate_w[0]), ple_proj_w[0].reshape(2, P, D).transpose(1, 0, 2).reshape(1, P, UNIT),
        rows_units(sc_cols), rows_units(sc_w_out_2[0]), ffn_units(0),
        rows_units(moba_w_qkv_2[0]), rows_units(moba_w_o_2[0]), ffn_units(1)])

    prm = np.zeros((P, PARAM_W), np.float32)

    def put(name, v, rows=P):
        a, b = PARAM[name]
        prm[:rows, a:b] = v.reshape(-1, b - a)

    def cols(v):
        return v.reshape(-1, P).T

    put("g0", cols(norm1_g[0]))
    put("g1", cols(np.concatenate([sb_out_g[0], mnorm_g[0], sgu_out_g[0]])))
    put("g2", cols(norm2_g[0]))
    put("g3", cols(ple_norm_g[0]))
    put("g4", cols(mix_norm_2[0]))
    put("g5", cols(ffn_norm_2[0]))
    put("g6", cols(mix_norm_2[1]))
    put("g7", cols(ffn_norm_2[1]))
    put("gates_b", np.concatenate([igate_b[0], fgate_b[0]]))
    put("conv_w", conv_w[0].reshape(CONV_K, 8, MLD).transpose(2, 1, 0).reshape(MLD, -1), MLD)
    put("conv_b", conv_b[0].reshape(8, MLD).T, MLD)
    put("ln_g", sgu_ln_g[0])
    put("ln_b", sgu_ln_b[0])
    put("sgu_b", sgu_b[0].T)
    put("sgu_w", sgu_w[0].transpose(2, 0, 1).reshape(P, -1))
    put("router_b", np.concatenate([router_gb[0], router_eb[0]]))
    put("router_w", np.concatenate([router_gw[0], router_ew[0]], axis=1).reshape(KD, P, NG + NE)
        .transpose(1, 0, 2).reshape(P, -1))
    put("sc_conv", sc_w_conv_2[0].reshape(3, SCB, P).transpose(2, 0, 1).reshape(P, -1))
    fc = ffn_w_conv_2.reshape(2, 3, 2, FE, 2, P)
    put("ffn_conv", fc.transpose(5, 0, 3, 1, 2, 4).reshape(P, -1))
    p_in = p[0, 0].T.reshape(2, P, T).transpose(1, 0, 2)
    finals = np.stack([np.broadcast_to(final_g, (P, D)), np.broadcast_to(final_norm_2, (P, D))])
    x_in = x[0].reshape(TT, P, D).transpose(1, 0, 2)

    nc = _bacc.Bacc("TRN2", target_bir_lowering=False, num_devices=1)
    arrays = {"stream": stream, "table": constants(), "params": prm, "finals": finals, "p_in": p_in, "x_in": x_in}
    aps = []
    for name in arrays:
        arrays[name] = np.ascontiguousarray(arrays[name])
        aps.append(nc.dram_tensor(name, arrays[name].shape, F32, kind="ExternalInput").ap())
    out = nc.dram_tensor("out", (P, TT, D), F32, kind="ExternalOutput").ap()
    program(nc, *aps, out)
    r = _run(nc, [arrays], core_ids=[0])
    return np.ascontiguousarray(r.results[0]["out"].transpose(1, 0, 2)).reshape(1, T, D)
```
